# Optimizing a Trainium2 kernel written in Bass

```python
import math
import jax
import jax.numpy as jnp
from jax import lax
import numpy as np
import jax, jax.numpy as jnp

D_MODEL = 1024
BATCH = 1
SEQ = 256
DEPTH = 2

GRID_W = 64
CTX_LEN = 256
NORM_EPS = 1e-6

RW_HEAD_DIM = 64
RW_DIM = D_MODEL // 2
RW_HEADS = RW_DIM // RW_HEAD_DIM
RW_LORA_W = 32
RW_LORA_A = 32
RW_LORA_G = 96
RW_GN_EPS = 64e-5
RW_COLS = 3 * RW_DIM + 2 * RW_LORA_W + 2 * RW_LORA_A + RW_LORA_G
RW_SPLITS = (RW_DIM, 2 * RW_DIM, 3 * RW_DIM, 3 * RW_DIM + 2 * RW_LORA_W, 3 * RW_DIM + 2 * RW_LORA_W + 2 * RW_LORA_A)

MB_HEAD_DIM = 64
MB_DIM = D_MODEL // 2
MB_HEADS = MB_DIM // MB_HEAD_DIM
MB_GROUPS = 2
MB_STATE = 128
MB_CONV = 5
MB_CHUNK = 128
MB_XBC = MB_DIM + 2 * MB_GROUPS * MB_STATE
MB_COLS = MB_DIM + MB_XBC + 2 * MB_HEADS
MB_SPLITS = (MB_DIM, MB_DIM + MB_XBC)

MIX_IN = RW_COLS + MB_COLS
MIX_OUT = RW_DIM + MB_DIM

NA_HEAD_DIM = 64
NA_HEADS = D_MODEL // NA_HEAD_DIM
NA_KH = 8
NA_KW = 16
NA_QB = 16
NA_KB = 32

D_FF = 2816
N_EXPERTS = 8
TOP_K = 2


def _rms_norm(h, g):
    hf = h.astype(jnp.float32)
    hf = hf * lax.rsqrt(jnp.mean(hf * hf, axis=-1, keepdims=True) + NORM_EPS)
    return (hf * g.astype(jnp.float32)).astype(h.dtype)

def _modulate(h, shift, scale):
    return h * (1 + scale) + shift

def _heads(t, n_heads):
    return t.reshape(t.shape[:-1] + (n_heads, t.shape[-1] // n_heads))

def _swiglu(h, w1, w3, w2):
    return (jax.nn.silu(h @ w1) * (h @ w3)) @ w2

def _centred_shift(z, mu_prev, mu_next):
    z_prev = jnp.pad(z, ((0, 0), (1, 0), (0, 0)))[:, :-1]
    z_next = jnp.pad(z, ((0, 0), (0, 1), (0, 0)))[:, 1:]
    return z + mu_prev * (z_prev - z) + mu_next * (z_next - z)

def _centred_dwconv(x, w, b):
    k_w, ch = w.shape
    y = lax.conv_general_dilated(x, w[:, None, :].astype(x.dtype), window_strides=(1,),
                                 padding=[(k_w // 2, k_w // 2)],
                                 dimension_numbers=('NWC', 'WIO', 'NWC'), feature_group_count=ch)
    return y + b

def _rwkv7_scan(s0, r, w, k, v, a, b):
    def step(S, inp):
        r_t, w_t, k_t, v_t, a_t, b_t = inp
        sa = jnp.einsum('bhvk,bhk->bhv', S, a_t)
        S = S * w_t[:, :, None, :] + sa[..., None] * b_t[:, :, None, :] + v_t[..., None] * k_t[:, :, None, :]
        return S, jnp.einsum('bhvk,bhk->bhv', S, r_t)
    xs = tuple(jnp.moveaxis(t, 1, 0) for t in (r, w, k, v, a, b))
    s_fin, ys = lax.scan(step, s0, xs)
    return s_fin, jnp.moveaxis(ys, 0, 1)

def _segsum(x):
    n = x.shape[-1]
    cs = jnp.cumsum(x, axis=-1)
    return jnp.where(np.tril(np.ones((n, n), dtype=bool)), cs[..., :, None] - cs[..., None, :], -jnp.inf)

def _ssd_chunked(s0, X, A, Bm, Cm):
    b, t, nh, p = X.shape
    n = Bm.shape[-1]
    nc, cl = t // MB_CHUNK, MB_CHUNK
    X = X.reshape(b, nc, cl, nh, p)
    Bm = Bm.reshape(b, nc, cl, nh, n)
    Cm = Cm.reshape(b, nc, cl, nh, n)
    A = A.reshape(b, nc, cl, nh).transpose(0, 3, 1, 2)
    A_cs = jnp.cumsum(A, axis=-1)
    L = jnp.exp(_segsum(A))
    y_diag = jnp.einsum('bclhn,bcshn,bhcls,bcshp->bclhp', Cm, Bm, L, X)
    decay_states = jnp.exp(A_cs[..., -1:] - A_cs)
    states = jnp.einsum('bclhn,bhcl,bclhp->bchpn', Bm, decay_states, X)
    states = jnp.concatenate([s0[:, None], states], axis=1)
    chunk_decay = jnp.exp(_segsum(jnp.pad(A_cs[..., -1], ((0, 0), (0, 0), (1, 0)))))
    states = jnp.einsum('bhzc,bchpn->bzhpn', chunk_decay, states)
    y_off = jnp.einsum('bclhn,bchpn,bhcl->bclhp', Cm, states[:, :-1], jnp.exp(A_cs))
    return states[:, -1], (y_diag + y_off).reshape(b, t, nh, p)

def _prefix_scan(scan_fn, ctx_args, lat_args, s0, reverse):
    if reverse:
        ctx_args = tuple(jnp.flip(t, axis=1) for t in ctx_args)
        lat_args = tuple(jnp.flip(t, axis=1) for t in lat_args)
    s_ctx, y_ctx = scan_fn(s0, *ctx_args)
    _, y_lat = scan_fn(s_ctx, *lat_args)
    if reverse:
        y_ctx, y_lat = jnp.flip(y_ctx, axis=1), jnp.flip(y_lat, axis=1)
    return y_ctx, y_lat

def _rwkv_mamba_mixer(a_ctx, a_lat, w_in, w_out, rw_mu, rw_w0, rw_w_up, rw_a0, rw_a_up, rw_g_up,
                      rw_k_k, rw_k_a, rw_r_k, rw_gn_w, rw_gn_b, mb_conv_w, mb_conv_b,
                      mb_dt_bias, mb_a_log, mb_d, mb_norm_w):
    f32 = jnp.float32

    def prepare(h):
        b, t, _ = h.shape
        z = h @ w_in
        z_rw = _centred_shift(z[..., :RW_COLS], rw_mu[0], rw_mu[1])
        r, k, v, lw, la, lg = jnp.split(z_rw, RW_SPLITS, axis=-1)
        lw = lw.reshape(b, t, 2, RW_LORA_W)
        la = la.reshape(b, t, 2, RW_LORA_A)
        logw = (rw_w0 + jnp.einsum('btdl,dlc->btdc', jnp.tanh(lw), rw_w_up)).astype(f32)
        decay = jnp.exp(-jnp.exp(-jax.nn.softplus(-logw) - 0.5))
        iclr = jax.nn.sigmoid((rw_a0 + jnp.einsum('btdl,dlc->btdc', la, rw_a_up)).astype(f32))
        gate = jax.nn.sigmoid(lg) @ rw_g_up
        kk = _heads(k * rw_k_k, RW_HEADS).astype(f32)
        kk = kk / jnp.maximum(jnp.sqrt(jnp.sum(kk * kk, axis=-1, keepdims=True)), 1e-12)
        k_dir = _heads((k[:, :, None, :] * (1 + (iclr - 1) * rw_k_a)).astype(f32), RW_HEADS)
        rh = _heads(r.astype(f32), RW_HEADS)
        vh = _heads(v.astype(f32), RW_HEADS)
        dh = _heads(decay, RW_HEADS)
        ih = _heads(iclr, RW_HEADS)
        rw_args = [(rh, dh[:, :, d], k_dir[:, :, d], vh, -kk, kk * ih[:, :, d]) for d in range(2)]
        bonus_f = jnp.sum(rh * k_dir[:, :, 0] * rw_r_k[0].astype(f32), axis=-1, keepdims=True)
        bonus_b = jnp.sum(rh * k_dir[:, :, 1] * rw_r_k[1].astype(f32), axis=-1, keepdims=True)
        bonus = (bonus_f + bonus_b) * vh
        zg, xbc, dt_raw = jnp.split(z[..., RW_COLS:], MB_SPLITS, axis=-1)
        xbc = jax.nn.silu(_centred_dwconv(xbc, mb_conv_w, mb_conv_b))
        xm, bm, cm = jnp.split(xbc, (MB_DIM, MB_DIM + MB_GROUPS * MB_STATE), axis=-1)
        xm = _heads(xm.astype(f32), MB_HEADS)
        rep = MB_HEADS // MB_GROUPS
        bm = jnp.repeat(_heads(bm.astype(f32), MB_GROUPS), rep, axis=2)
        cm = jnp.repeat(_heads(cm.astype(f32), MB_GROUPS), rep, axis=2)
        dt = jax.nn.softplus(dt_raw.reshape(b, t, 2, MB_HEADS).astype(f32) + mb_dt_bias.astype(f32))
        a_neg = -jnp.exp(mb_a_log.astype(f32))
        mb_args = [(xm * dt[:, :, d, :, None], dt[:, :, d] * a_neg[d], bm, cm) for d in range(2)]
        return rw_args, mb_args, bonus, gate, xm, zg

    pc, pl = prepare(a_ctx), prepare(a_lat)
    bsz = a_lat.shape[0]
    s0_rw = jnp.zeros((bsz, RW_HEADS, RW_HEAD_DIM, RW_HEAD_DIM), f32)
    s0_mb = jnp.zeros((bsz, MB_HEADS, MB_HEAD_DIM, MB_STATE), f32)
    yrf_c, yrf_l = _prefix_scan(_rwkv7_scan, pc[0][0], pl[0][0], s0_rw, False)
    yrb_c, yrb_l = _prefix_scan(_rwkv7_scan, pc[0][1], pl[0][1], s0_rw, True)
    ymf_c, ymf_l = _prefix_scan(_ssd_chunked, pc[1][0], pl[1][0], s0_mb, False)
    ymb_c, ymb_l = _prefix_scan(_ssd_chunked, pc[1][1], pl[1][1], s0_mb, True)

    def finish(h, p, y_rw, y_mb):
        b, t, _ = h.shape
        _, _, bonus, gate, xm, zg = p
        mu = jnp.mean(y_rw, axis=-1, keepdims=True)
        var = jnp.mean(jnp.square(y_rw - mu), axis=-1, keepdims=True)
        y_rw = ((y_rw - mu) * lax.rsqrt(var + RW_GN_EPS)).reshape(b, t, RW_DIM) * rw_gn_w + rw_gn_b
        o_rw = (y_rw + bonus.reshape(b, t, RW_DIM)) * gate
        y_mb = (y_mb + mb_d.astype(f32)[:, None] * xm).reshape(b, t, MB_DIM) * jax.nn.silu(zg.astype(f32))
        y_mb = y_mb.reshape(b, t, MB_GROUPS, MB_DIM // MB_GROUPS)
        y_mb = (y_mb * lax.rsqrt(jnp.mean(y_mb * y_mb, axis=-1, keepdims=True) + NORM_EPS)).reshape(b, t, MB_DIM) * mb_norm_w
        return jnp.concatenate([o_rw, y_mb], axis=-1).astype(h.dtype) @ w_out

    return (finish(a_ctx, pc, yrf_c + yrb_c, ymf_c + ymb_c),
            finish(a_lat, pl, yrf_l + yrb_l, ymf_l + ymb_l))

def _neighbourhood_attention(a_ctx, a_lat, w_qkv, w_out, rpb, with_ctx_queries):
    b, t, d_model = a_lat.shape
    rows = t // GRID_W
    kh = min(NA_KH, rows)
    scale = NA_HEAD_DIM ** -0.5
    q, k, v = jnp.split(a_lat @ w_qkv, 3, axis=-1)
    qc, kc, vc = jnp.split(a_ctx @ w_qkv, 3, axis=-1)
    q_grid = (_heads(q, NA_HEADS) * scale).reshape(b, rows, GRID_W, NA_HEADS, NA_HEAD_DIM)
    k_grid = _heads(k, NA_HEADS).reshape(b, rows, GRID_W, NA_HEADS, NA_HEAD_DIM)
    v_grid = _heads(v, NA_HEADS).reshape(b, rows, GRID_W, NA_HEADS, NA_HEAD_DIM)
    qc, kc, vc = _heads(qc, NA_HEADS) * scale, _heads(kc, NA_HEADS), _heads(vc, NA_HEADS)

    n_cb = GRID_W // NA_QB
    q_cols = np.arange(GRID_W).reshape(n_cb, NA_QB)
    kb_start = np.clip(np.arange(n_cb) * NA_QB - NA_KW // 2, 0, GRID_W - NA_KB)
    key_cols = kb_start[:, None] + np.arange(NA_KB)
    win_start = np.clip(q_cols - NA_KW // 2, 0, GRID_W - NA_KW)
    kcol = key_cols[:, None, :]
    col_in = (kcol >= win_start[..., None]) & (kcol < win_start[..., None] + NA_KW)
    col_bias_idx = np.clip(kcol - q_cols[:, :, None] + NA_KW - 1, 0, 2 * NA_KW - 2)
    mask = np.broadcast_to(col_in[:, :, None, :], (n_cb, NA_QB, kh, NA_KB)).reshape(n_cb, NA_QB, kh * NA_KB)
    n_lat = kh * NA_KB

    def row_block(r):
        rs = jnp.clip(r - kh // 2, 0, rows - kh)
        k_rows = lax.dynamic_slice_in_dim(k_grid, rs, kh, axis=1)
        v_rows = lax.dynamic_slice_in_dim(v_grid, rs, kh, axis=1)
        k_blk = k_rows[:, :, key_cols].transpose(0, 2, 1, 3, 4, 5).reshape(b, n_cb, n_lat, NA_HEADS, NA_HEAD_DIM)
        v_blk = v_rows[:, :, key_cols].transpose(0, 2, 1, 3, 4, 5).reshape(b, n_cb, n_lat, NA_HEADS, NA_HEAD_DIM)
        q_blk = lax.dynamic_index_in_dim(q_grid, r, axis=1, keepdims=False).reshape(b, n_cb, NA_QB, NA_HEADS, NA_HEAD_DIM)
        row_idx = rs + jnp.arange(kh) - r + (NA_KH - 1)
        bias = rpb[:, row_idx][:, :, col_bias_idx]
        bias = bias.transpose(0, 2, 3, 1, 4).reshape(NA_HEADS, n_cb, NA_QB, n_lat).astype(jnp.float32)
        s_lat = jnp.einsum('bjqhd,bjkhd->bhjqk', q_blk, k_blk).astype(jnp.float32) + bias
        s_lat = jnp.where(mask, s_lat, -jnp.inf)
        s_ctx = jnp.einsum('bjqhd,bkhd->bhjqk', q_blk, kc).astype(jnp.float32)
        p = jax.nn.softmax(jnp.concatenate([s_lat, s_ctx], axis=-1), axis=-1).astype(v.dtype)
        o = (jnp.einsum('bhjqk,bjkhd->bjqhd', p[..., :n_lat], v_blk)
             + jnp.einsum('bhjqk,bkhd->bjqhd', p[..., n_lat:], vc))
        return o.reshape(b, GRID_W, d_model)

    o_rows = lax.map(row_block, jnp.arange(rows))
    o_lat = o_rows.transpose(1, 0, 2, 3).reshape(b, t, d_model) @ w_out
    o_ctx = None
    if with_ctx_queries:
        s = jnp.einsum('bqhd,bkhd->bhqk', qc, kc).astype(jnp.float32)
        p = jax.nn.softmax(s, axis=-1).astype(vc.dtype)
        o_ctx = jnp.einsum('bhqk,bkhd->bqhd', p, vc).reshape(a_ctx.shape) @ w_out
    return o_ctx, o_lat

def _moe_swiglu(h, router_w, router_b, w1, w3, w2):
    logits = (h @ router_w).astype(jnp.float32) + router_b.astype(jnp.float32)
    top_vals, top_idx = lax.top_k(logits, TOP_K)
    top_w = jax.nn.softmax(top_vals, axis=-1)
    gates = jnp.sum(jax.nn.one_hot(top_idx, N_EXPERTS, dtype=jnp.float32) * top_w[..., None], axis=-2).astype(h.dtype)
    out = jnp.zeros_like(h)
    for e in range(N_EXPERTS):
        out = out + gates[..., e:e + 1] * _swiglu(h, w1[e], w3[e], w2[e])
    return out

def first_inputs(seed: int = 0) -> dict:
    key = jax.random.key(seed)
    keys = iter(jax.random.split(key, 64))
    d = D_MODEL
    ne, no = (DEPTH + 1) // 2, DEPTH // 2

    def nrm(shape, scale):
        return scale * jax.random.normal(next(keys), shape, jnp.float32)

    def uni(shape, lo, hi):
        return jax.random.uniform(next(keys), shape, jnp.float32, lo, hi)

    dt0 = jnp.exp(uni((ne, 2, MB_HEADS), math.log(1e-3), math.log(1e-1)))
    return {
        'x': nrm((BATCH, SEQ, d), 1.0),
        'c': nrm((BATCH, d), 1.0),
        'ctx': nrm((BATCH, CTX_LEN, d), 1.0),
        'c_ctx': nrm((d,), 1.0),
        'w_ada': nrm((DEPTH, d, 6 * d), 0.5 * d ** -0.5),
        'b_ada': nrm((DEPTH, 6 * d), 0.02),
        'norm_mix': 1.0 + nrm((DEPTH, d), 0.05),
        'norm_ffn': 1.0 + nrm((DEPTH, d), 0.05),
        'norm_final': 1.0 + nrm((d,), 0.05),
        'mix_w_in': nrm((ne, d, MIX_IN), d ** -0.5),
        'mix_w_out': nrm((ne, MIX_OUT, d), MIX_OUT ** -0.5),
        'rw_mu': uni((ne, 2, RW_COLS), 0.0, 0.5),
        'rw_w0': uni((ne, 2, RW_DIM), -6.0, 1.0),
        'rw_w_up': nrm((ne, 2, RW_LORA_W, RW_DIM), 0.5 * RW_LORA_W ** -0.5),
        'rw_a0': nrm((ne, 2, RW_DIM), 0.5),
        'rw_a_up': nrm((ne, 2, RW_LORA_A, RW_DIM), 0.5 * RW_LORA_A ** -0.5),
        'rw_g_up': nrm((ne, RW_LORA_G, RW_DIM), RW_LORA_G ** -0.5),
        'rw_k_k': 0.85 + nrm((ne, RW_DIM), 0.05),
        'rw_k_a': 1.0 + nrm((ne, RW_DIM), 0.05),
        'rw_r_k': nrm((ne, 2, RW_HEADS, RW_HEAD_DIM), 0.1),
        'rw_gn_w': 1.0 + nrm((ne, RW_DIM), 0.05),
        'rw_gn_b': nrm((ne, RW_DIM), 0.02),
        'mb_conv_w': nrm((ne, MB_CONV, MB_XBC), MB_CONV ** -0.5),
        'mb_conv_b': nrm((ne, MB_XBC), 0.02),
        'mb_dt_bias': dt0 + jnp.log(-jnp.expm1(-dt0)),
        'mb_a_log': jnp.log(uni((ne, 2, MB_HEADS), 1.0, 16.0)),
        'mb_d': 1.0 + nrm((ne, MB_HEADS), 0.1),
        'mb_norm_w': 1.0 + nrm((ne, MB_DIM), 0.05),
        'ffn_w1': nrm((ne, d, D_FF), d ** -0.5),
        'ffn_w3': nrm((ne, d, D_FF), d ** -0.5),
        'ffn_w2': nrm((ne, D_FF, d), D_FF ** -0.5),
        'na_w_qkv': nrm((no, d, 3 * d), d ** -0.5),
        'na_w_out': nrm((no, d, d), d ** -0.5),
        'na_rpb': nrm((no, NA_HEADS, 2 * NA_KH - 1, 2 * NA_KW - 1), 0.1),
        'moe_router_w': nrm((no, d, N_EXPERTS), d ** -0.5),
        'moe_router_b': nrm((no, N_EXPERTS), 0.01),
        'moe_w1': nrm((no, N_EXPERTS, d, D_FF), d ** -0.5),
        'moe_w3': nrm((no, N_EXPERTS, d, D_FF), d ** -0.5),
        'moe_w2': nrm((no, N_EXPERTS, D_FF, d), D_FF ** -0.5),
    }

def first_block(x, c, ctx, c_ctx, w_ada, b_ada, norm_mix, norm_ffn, norm_final, mix_w_in, mix_w_out,
              rw_mu, rw_w0, rw_w_up, rw_a0, rw_a_up, rw_g_up, rw_k_k, rw_k_a, rw_r_k, rw_gn_w, rw_gn_b,
              mb_conv_w, mb_conv_b, mb_dt_bias, mb_a_log, mb_d, mb_norm_w, ffn_w1, ffn_w3, ffn_w2,
              na_w_qkv, na_w_out, na_rpb, moe_router_w, moe_router_b, moe_w1, moe_w3, moe_w2):
    h_ctx, h_lat = ctx, x
    c_lat_act, c_ctx_act = jax.nn.silu(c), jax.nn.silu(c_ctx)
    for i in range(DEPTH):
        j = i // 2
        update_ctx = i < DEPTH - 1
        m_lat = jnp.split((c_lat_act @ w_ada[i] + b_ada[i])[:, None, :], 6, axis=-1)
        m_ctx = jnp.split(c_ctx_act @ w_ada[i] + b_ada[i], 6, axis=-1)
        a_lat = _modulate(_rms_norm(h_lat, norm_mix[i]), m_lat[0], m_lat[1])
        a_ctx = _modulate(_rms_norm(h_ctx, norm_mix[i]), m_ctx[0], m_ctx[1])
        if i % 2 == 0:
            o_ctx, o_lat = _rwkv_mamba_mixer(a_ctx, a_lat, mix_w_in[j], mix_w_out[j], rw_mu[j], rw_w0[j],
                                             rw_w_up[j], rw_a0[j], rw_a_up[j], rw_g_up[j], rw_k_k[j],
                                             rw_k_a[j], rw_r_k[j], rw_gn_w[j], rw_gn_b[j], mb_conv_w[j],
                                             mb_conv_b[j], mb_dt_bias[j], mb_a_log[j], mb_d[j], mb_norm_w[j])
        else:
            o_ctx, o_lat = _neighbourhood_attention(a_ctx, a_lat, na_w_qkv[j], na_w_out[j], na_rpb[j], update_ctx)

        def channel_mixer(t):
            if i % 2 == 0:
                return _swiglu(t, ffn_w1[j], ffn_w3[j], ffn_w2[j])
            return _moe_swiglu(t, moe_router_w[j], moe_router_b[j], moe_w1[j], moe_w3[j], moe_w2[j])

        h_lat = h_lat + m_lat[2] * o_lat
        h_lat = h_lat + m_lat[5] * channel_mixer(_modulate(_rms_norm(h_lat, norm_ffn[i]), m_lat[3], m_lat[4]))
        if update_ctx:
            h_ctx = h_ctx + m_ctx[2] * o_ctx
            h_ctx = h_ctx + m_ctx[5] * channel_mixer(_modulate(_rms_norm(h_ctx, norm_ffn[i]), m_ctx[3], m_ctx[4]))
    return _rms_norm(h_lat, norm_final)


CHUNK = 64
D_CONV = D_MODEL // 4
CONV_WIDTH = 31
SB_HEAD_DIM = 64
D_SB = D_MODEL // 2
N_SB_HEADS = D_SB // SB_HEAD_DIM
RET_HEAD_DIM = 64
D_RET = D_MODEL // 4
N_RET_HEADS = D_RET // RET_HEAD_DIM
D_MIX = D_CONV + D_SB + D_RET
D_IN_PROJ = 2 * D_CONV + 3 * D_SB + 4 * D_RET
D_FF_2 = ((8 * D_MODEL // 3 + 127) // 128) * 128
Q_BLOCK = 128
ROPE_BASE = 10000.0
EPS = 1e-6


def rms_norm(x, g):
    xf = x.astype(jnp.float32)
    y = xf * lax.rsqrt(jnp.mean(xf * xf, axis=-1, keepdims=True) + EPS)
    return (y * g.astype(jnp.float32)).astype(x.dtype)

def layer_norm(x, g, b):
    xf = x.astype(jnp.float32)
    mu = jnp.mean(xf, axis=-1, keepdims=True)
    xc = xf - mu
    var = jnp.mean(xc * xc, axis=-1, keepdims=True)
    return (xc * lax.rsqrt(var + EPS) * g.astype(jnp.float32) + b.astype(jnp.float32)).astype(x.dtype)

def swiglu(h, w_in, w_out):
    gate, up = jnp.split(h @ w_in, 2, axis=-1)
    return (jax.nn.silu(gate) * up) @ w_out

def conv_module(u, conv_w, conv_b, ln_g, ln_b):
    a, b = jnp.split(u, 2, axis=-1)
    v = a * jax.nn.sigmoid(b)
    v = jnp.pad(v, ((0, 0), (CONV_WIDTH - 1, 0), (0, 0)))
    y = lax.conv_general_dilated(
        v, conv_w[:, None, :].astype(v.dtype), window_strides=(1,), padding="VALID",
        dimension_numbers=("NWC", "WIO", "NWC"), feature_group_count=D_CONV)
    y = y + conv_b
    return jax.nn.silu(layer_norm(y, ln_g, ln_b))

def stick_breaking(q, k, v):
    B, S, H, Dh = q.shape
    nb = S // Q_BLOCK
    qb = q.reshape(B, nb, Q_BLOCK, H, Dh).transpose(1, 0, 2, 3, 4)
    kpos = jnp.arange(S)
    scale = Dh ** -0.5

    def block(args):
        qi, i = args
        z = jnp.einsum("bqhd,bkhd->bhqk", qi, k,
                       preferred_element_type=jnp.float32) * scale
        qpos = i * Q_BLOCK + jnp.arange(Q_BLOCK)
        mask = kpos[None, :] < qpos[:, None]
        log_beta = jax.nn.log_sigmoid(z)
        log_not = jnp.where(mask, jax.nn.log_sigmoid(-z), 0.0)
        remain = lax.cumsum(log_not, axis=3, reverse=True) - log_not
        w = jnp.where(mask, jnp.exp(log_beta + remain), 0.0)
        return jnp.einsum("bhqk,bkhd->bqhd", w.astype(v.dtype), v)

    out = lax.map(block, (qb, jnp.arange(nb)))
    return out.transpose(1, 0, 2, 3, 4).reshape(B, S, H, Dh)

def rotary(x, pos):
    half = x.shape[-1] // 2
    inv = 1.0 / (ROPE_BASE ** (jnp.arange(half, dtype=jnp.float32) / half))
    ang = pos.astype(jnp.float32)[:, None] * inv[None, :]
    cos = jnp.cos(ang)[None, :, None, :]
    sin = jnp.sin(ang)[None, :, None, :]
    x1 = x[..., :half].astype(jnp.float32)
    x2 = x[..., half:].astype(jnp.float32)
    return jnp.concatenate([x1 * cos - x2 * sin, x1 * sin + x2 * cos], axis=-1).astype(x.dtype)

def retention(q, k, v):
    B, S, H, Dh = q.shape
    nc = S // CHUNK
    log_gamma = jnp.log1p(-jnp.exp2(-5.0 - jnp.arange(H, dtype=jnp.float32)))
    qc = (q * (Dh ** -0.5)).reshape(B, nc, CHUNK, H, Dh)
    kc = k.reshape(B, nc, CHUNK, H, Dh)
    vc = v.reshape(B, nc, CHUNK, H, Dh)
    idx = jnp.arange(CHUNK, dtype=jnp.float32)
    d_intra = jnp.exp(log_gamma[:, None, None] * jnp.abs(idx[:, None] - idx[None, :]))
    scores = jnp.einsum("bnihd,bnjhd->bnhij", qc, kc,
                        preferred_element_type=jnp.float32) * d_intra
    y_intra = jnp.einsum("bnhij,bnjhe->bnihe", scores, vc.astype(jnp.float32))
    k_decay = jnp.exp(log_gamma[None, :] * (CHUNK - 1 - idx)[:, None])
    kv = jnp.einsum("bnjhd,jh,bnjhe->bnhde", kc.astype(jnp.float32), k_decay,
                    vc.astype(jnp.float32))
    chunk_decay = jnp.exp(log_gamma * CHUNK)[None, :, None, None]

    def step(state, kv_n):
        return chunk_decay * state + kv_n, state

    _, s_prev = lax.scan(step, jnp.zeros((B, H, Dh, Dh), jnp.float32),
                         kv.transpose(1, 0, 2, 3, 4))
    s_prev = s_prev.transpose(1, 0, 2, 3, 4)
    q_decay = jnp.exp(log_gamma[None, :] * (idx + 1.0)[:, None])
    y_cross = jnp.einsum("bnihd,ih,bnhde->bnihe", qc.astype(jnp.float32), q_decay, s_prev)
    return (y_intra + y_cross).reshape(B, S, H, Dh)

def head_norm(y, g):
    B, S, H, Dh = y.shape
    mu = jnp.mean(y, axis=-1, keepdims=True)
    yc = y - mu
    var = jnp.mean(yc * yc, axis=-1, keepdims=True)
    return (yc * lax.rsqrt(var + EPS)).reshape(B, S, H * Dh) * g.astype(jnp.float32)

def hybrid_mixer(h, w_in, conv_w, conv_b, conv_ln_g, conv_ln_b, ret_norm_g, w_out, pos):
    B, S, _ = h.shape
    o1 = 2 * D_CONV
    o2 = o1 + D_SB
    o3 = o2 + D_SB
    o4 = o3 + D_SB
    o5 = o4 + D_RET
    o6 = o5 + D_RET
    o7 = o6 + D_RET
    u_conv, q_sb, k_sb, v_sb, q_r, k_r, v_r, g_r = jnp.split(
        h @ w_in, [o1, o2, o3, o4, o5, o6, o7], axis=-1)
    y_conv = conv_module(u_conv, conv_w, conv_b, conv_ln_g, conv_ln_b)
    sb = lambda t: t.reshape(B, S, N_SB_HEADS, SB_HEAD_DIM)
    y_sb = stick_breaking(sb(q_sb), sb(k_sb), sb(v_sb)).reshape(B, S, D_SB)
    rt = lambda t: t.reshape(B, S, N_RET_HEADS, RET_HEAD_DIM)
    y_r = retention(rotary(rt(q_r), pos), rotary(rt(k_r), pos), rt(v_r))
    y_r = jax.nn.silu(g_r.astype(jnp.float32)) * head_norm(y_r, ret_norm_g)
    y = jnp.concatenate([y_conv, y_sb, y_r.astype(h.dtype)], axis=-1)
    return y @ w_out

def second_inputs(seed: int = 0) -> dict:
    key = jax.random.key(seed)
    ks = jax.random.split(key, 20)
    f32 = jnp.float32
    nrm = lambda k, shape, scale: jax.random.normal(k, shape, f32) * scale
    gain = lambda k, shape: 1.0 + 0.02 * jax.random.normal(k, shape, f32)
    return {
        "x": jax.random.normal(ks[0], (BATCH, SEQ, D_MODEL), f32),
        "ffn1_norm": gain(ks[1], (DEPTH, D_MODEL)),
        "ffn1_w_in": nrm(ks[2], (DEPTH, D_MODEL, 2 * D_FF_2), D_MODEL ** -0.5),
        "ffn1_w_out": nrm(ks[3], (DEPTH, D_FF_2, D_MODEL), D_FF_2 ** -0.5),
        "mix_norm": gain(ks[4], (DEPTH, D_MODEL)),
        "mix_w_in": nrm(ks[5], (DEPTH, D_MODEL, D_IN_PROJ), D_MODEL ** -0.5),
        "conv_w": nrm(ks[6], (DEPTH, CONV_WIDTH, D_CONV), CONV_WIDTH ** -0.5),
        "conv_b": nrm(ks[7], (DEPTH, D_CONV), 0.02),
        "conv_ln_g": gain(ks[8], (DEPTH, D_CONV)),
        "conv_ln_b": nrm(ks[9], (DEPTH, D_CONV), 0.02),
        "ret_norm_g": gain(ks[10], (DEPTH, D_RET)),
        "mix_w_out": nrm(ks[11], (DEPTH, D_MIX, D_MODEL), D_MIX ** -0.5),
        "ffn2_norm": gain(ks[12], (DEPTH, D_MODEL)),
        "ffn2_w_in": nrm(ks[13], (DEPTH, D_MODEL, 2 * D_FF_2), D_MODEL ** -0.5),
        "ffn2_w_out": nrm(ks[14], (DEPTH, D_FF_2, D_MODEL), D_FF_2 ** -0.5),
        "final_norm": gain(ks[15], (D_MODEL,)),
    }

def second_block(x, ffn1_norm, ffn1_w_in, ffn1_w_out, mix_norm, mix_w_in, conv_w, conv_b,
              conv_ln_g, conv_ln_b, ret_norm_g, mix_w_out, ffn2_norm, ffn2_w_in, ffn2_w_out,
              final_norm):
    S = x.shape[1]
    pos = jnp.arange(S)
    for l in range(DEPTH):
        x = x + 0.5 * swiglu(rms_norm(x, ffn1_norm[l]), ffn1_w_in[l], ffn1_w_out[l])
        x = x + hybrid_mixer(rms_norm(x, mix_norm[l]), mix_w_in[l], conv_w[l], conv_b[l],
                             conv_ln_g[l], conv_ln_b[l], ret_norm_g[l], mix_w_out[l], pos)
        x = x + 0.5 * swiglu(rms_norm(x, ffn2_norm[l]), ffn2_w_in[l], ffn2_w_out[l])
    return rms_norm(x, final_norm)


def setup_inputs(seed=0):
    out = dict(first_inputs(seed))
    for name, value in second_inputs(seed + 1).items():
        if name != "x":
            out[name + "_2"] = value
    return out


def reference(
    x, c, ctx, c_ctx, w_ada, b_ada, norm_mix, norm_ffn, norm_final, mix_w_in, mix_w_out, rw_mu,
    rw_w0, rw_w_up, rw_a0, rw_a_up, rw_g_up, rw_k_k, rw_k_a, rw_r_k, rw_gn_w, rw_gn_b,
    mb_conv_w, mb_conv_b, mb_dt_bias, mb_a_log, mb_d, mb_norm_w, ffn_w1, ffn_w3, ffn_w2,
    na_w_qkv, na_w_out, na_rpb, moe_router_w, moe_router_b, moe_w1, moe_w3, moe_w2, ffn1_norm_2,
    ffn1_w_in_2, ffn1_w_out_2, mix_norm_2, mix_w_in_2, conv_w_2, conv_b_2, conv_ln_g_2,
    conv_ln_b_2, ret_norm_g_2, mix_w_out_2, ffn2_norm_2, ffn2_w_in_2, ffn2_w_out_2,
    final_norm_2,
):
    x = first_block(
        x, c, ctx, c_ctx, w_ada, b_ada, norm_mix, norm_ffn, norm_final, mix_w_in, mix_w_out,
        rw_mu, rw_w0, rw_w_up, rw_a0, rw_a_up, rw_g_up, rw_k_k, rw_k_a, rw_r_k, rw_gn_w,
        rw_gn_b, mb_conv_w, mb_conv_b, mb_dt_bias, mb_a_log, mb_d, mb_norm_w, ffn_w1, ffn_w3,
        ffn_w2, na_w_qkv, na_w_out, na_rpb, moe_router_w, moe_router_b, moe_w1, moe_w3, moe_w2,
    )
    return second_block(
        x, ffn1_norm_2, ffn1_w_in_2, ffn1_w_out_2, mix_norm_2, mix_w_in_2, conv_w_2, conv_b_2,
        conv_ln_g_2, conv_ln_b_2, ret_norm_g_2, mix_w_out_2, ffn2_norm_2, ffn2_w_in_2,
        ffn2_w_out_2, final_norm_2,
    )


_drawn_inputs = setup_inputs


def setup_inputs(seed=0):
    import zlib

    import numpy as np

    out = dict(_drawn_inputs(seed))
    spreads = {}
    factors = {'rw_w_up': 3.576,
     'rw_gn_w': 3.758,
     'rw_gn_b': 3.299,
     'mb_conv_b': 3.106,
     'mb_d': 3.45,
     'na_rpb': 5.68,
     'moe_router_b': 3.271,
     'ffn1_norm_2': 4.341,
     'conv_b_2': 3.772,
     'conv_ln_g_2': 33.862,
     'conv_ln_b_2': 35.234,
     'ret_norm_g_2': 38.741,
     'ffn2_norm_2': 5.532,
     'final_norm_2': 8.339}
    for name, (base, spread) in spreads.items():
        noise = np.random.default_rng([zlib.crc32(name.encode()), seed]).standard_normal(out[name].shape)
        drawn = base * np.exp(spread * noise) if base else spread * noise
        out[name] = jnp.asarray(drawn.astype(out[name].dtype))
    for name, factor in factors.items():
        out[name] = (out[name] * factor).astype(out[name].dtype)
    return out
```

```python
from contextlib import ExitStack

import numpy as np
import concourse.bass as bass
from concourse import mybir

F32 = mybir.dt.float32
F32R = mybir.dt.float32r
ACT = mybir.ActivationFunctionType
ALU = mybir.AluOpType
AX = mybir.AxisListType

P = 128
D = 1024
KT = D // P
SEG = 256
CTX, LAT = 0, 1
T2 = 2 * SEG
DFF = 2816
FT = DFF // P
NE = 8
RING = 3
LEAD = 2
EPS = 1e-6
E05 = float(np.exp(np.float32(-0.5)))
RC = 64
NRC = SEG // RC
RLEV = 5
MC = 128
NMC = T2 // MC
CONV2 = 31
BIG = 1e30

PARAMS = [("b_ada", 96), ("n_mix", 16), ("n_ffn", 16), ("n_fin", 8), ("mu_p", 14), ("mu_n", 14),
          ("w0", 8), ("a0", 8), ("kk", 4), ("ka", 4), ("rk", 8), ("gnw", 4), ("gnb", 4),
          ("cw", 40), ("cb", 8), ("mbd", 4), ("mbn", 4), ("dtb", 1), ("alog", 1),
          ("n1", 16), ("nm", 16), ("n2", 16), ("c2w", 124), ("c2b", 4), ("c2g", 4), ("c2bb", 4),
          ("rtg", 4), ("nf2", 8), ("rb", 8), ("rw", 64), ("cvec", 16)]
COL = {}
_c = 0
for _n, _w in PARAMS:
    COL[_n] = (_c, _c + _w)
    _c += _w
NPAR = _c

CONSTS = [("ident", 128), ("ones", 128), ("bones", 128), ("i64", 64),
          ("mx", 256), ("mn", 128), ("lv", 2 * (RLEV + 1) * 2 * 64), ("scan64", 1024),
          ("scan128", 512), ("mssd", 256)]
CCOL = {}
_c = 0
for _n, _w in CONSTS:
    CCOL[_n] = (_c, _c + _w)
    _c += _w
NCON = _c
CONSTS_B = [("iota", 16), ("tri", 128), ("smask", 128), ("rot", 128), ("cos", 256), ("sin", 256),
            ("dret", 4 * 384)]
BCOL = {}
_c = 0
for _n, _w in CONSTS_B:
    BCOL[_n] = (_c, _c + _w)
    _c += _w
NCONB = _c

STREAM = [("ada", 96), ("w_in", 27), ("w_out", 8), ("ffn_ctx", 3 * FT), ("ffn_lat", 3 * FT), ("qkv", 24),
          ("na_out", 8), ("moe", 3 * FT * NE)]
for _l in range(2):
    STREAM += [(f"f1_{_l}", 3 * FT), (f"in_{_l}", 24), (f"out_{_l}", 8), (f"f2_{_l}", 3 * FT)]
BASE = {}
_c = 0
for _n, _w in STREAM:
    BASE[_n] = _c
    _c += _w
NTILES = _c + LEAD


def build(nc, io):
    with ExitStack() as es:
        cursor = [nc.sbuf_base + (-nc.sbuf_base) % 64]

        def sb(name, shape, dt=F32, at=None):
            size = int(np.prod(shape[1:])) * 4
            off = cursor[0] if at is None else at
            if at is None:
                cursor[0] += (size + 31) // 32 * 32
            assert off + size <= nc.sbuf_usable_end, (name, off + size)
            return nc.alloc_sbuf_tensor_at(name, list(shape), dt, offset=off)

        raw = sb("w_raw", [P, RING, 1024])
        whi = sb("w_hi", [P, RING, 1024], F32R)
        wlo = sb("w_lo", [P, RING, 1024], F32R)
        hT = sb("hT", [P, KT, T2])
        g_hi = sb("g_hi", [P, 2, SEG], F32R)
        g_lo = sb("g_lo", [P, 2, SEG], F32R)
        g_f = sb("g_f", [P, 2, SEG])
        sil = sb("sil", [P, 2, SEG])
        rs = sb("rs", [P, T2])
        mod = sb("mod", [P, 96, 2])
        gsm = sb("gsm", [P, 4, KT, 2])
        par = sb("par", [P, NPAR])
        cv = sb("cv", [P, 16])
        cv_hi = sb("cv_hi", [P, 8, 2], F32R)
        cv_lo = sb("cv_lo", [P, 8, 2], F32R)
        ident = sb("ident", [P, 128])
        ones = sb("ones", [P, 128])
        bones = sb("bones", [P, 128])
        area = cursor[0]
        a_hi = sb("a_hi", [P, KT, T2], F32R)
        a_lo = sb("a_lo", [P, KT, T2], F32R)
        arena = cursor[0]
        END = nc.sbuf_usable_end // 64 * 64

        def lay(start, items):
            out = []
            for name, shape in items:
                out.append(sb(name, shape, at=start))
                start += (int(np.prod(shape[1:])) * 4 + 31) // 32 * 32
            return out + [start]

        zrw, con, zx, zg, zdt, m0 = lay(arena, [
            ("zrw", [P, 14, 2, 260]), ("con", [P, NCON - 384]), ("zx", [P, 8, 2, 260]),
            ("zg", [P, 4, T2]), ("zdt", [P, T2])])
        zx_at = m0 - (4 * T2 + T2 + 8 * 520) * 4
        ps = es.enter_context(nc.psum_tensor("ps", [P, 8, 512], F32))

        def pc(name, i=0, n=None):
            a, b = COL[name]
            return par[:, a + i:(a + i + n) if n else b]

        def cc(name):
            a, b = CCOL[name]
            return con[:, a - 384:b - 384]

        class Signal:

            def __init__(self, name):
                self.sem = es.enter_context(nc.semaphore(name))
                self.taken = {}
                self.made = 0
                self.one = (self.sem, 1)
                self.dma = (self.sem, 16)

            def next(self, who, n=1):
                self.taken[who] = self.taken.get(who, 0) + n
                return self.sem, self.taken[who]

        names = {}

        def S(name):
            if name not in names:
                names[name] = Signal(name)
            return names[name]

        raw_loaded = [S(f"raw_loaded{i}") for i in range(RING)]
        hi_ready, lo_ready, tile_used = S("hi_ready"), S("lo_ready"), S("tile_used")
        act_evac, dve_evac = S("act_evac"), S("dve_evac")

        block = es.enter_context(nc.Block())

        def repeat(eng, n, unroll, body, first=0):
            full = (n - first) // unroll
            if full >= 2:
                with eng.Fori(0, full) as i:
                    for j in range(unroll):
                        body(i * unroll + (first + j), j)
            else:
                full = 0
            for t in range(first + full * unroll, n):
                body(t, (t - first) % unroll)

        def one(t):
            return slice(t, t + 1) if isinstance(t, int) else bass.ds(t, 1)

        def sp_stream(sp):
            w = io["wstream"]
            for n in range(RING):
                sp.dma_start(raw[:, n, :], w[n]).then_inc(raw_loaded[n].sem, 16)

            def tile(n, j):
                sp.wait_ge(lo_ready.sem, n - (RING - 1))
                sp.dma_start(raw[:, j % RING, :], w[one(n)].rearrange("o p c -> p (o c)")
                             ).then_inc(raw_loaded[j % RING].sem, 16)
            repeat(sp, NTILES, RING, tile, first=RING)

        def act_split(act, n, i3, slot):
            act.wait_ge(raw_loaded[slot].sem, i3 * 16 + 16)
            act.wait_ge(tile_used.sem, n + 1)
            nc.scalar.activation(whi[:, slot, :], raw[:, slot, :], ACT.Copy).then_inc(hi_ready.sem, 1)

        def dve_split(dve, n, slot):
            dve.wait_ge(hi_ready.sem, n + 1)
            nc.vector.tensor_tensor(wlo[:, slot, :], raw[:, slot, :], whi[:, slot, :].bitcast(F32),
                                    ALU.subtract).then_inc(lo_ready.sem, 1)

        def run_tiles(eng, who, base, count, before=None, after=None, t0=0):
            full = count // RING
            if full < 2:
                full = 0

            def step(t, i, j):
                n = t + (base + LEAD)
                c = base + t0 + j + LEAD
                slot = c % RING
                if i is None:
                    i3 = n // RING
                else:
                    i3 = i + c // RING
                if before:
                    before(t)
                if who == "act":
                    act_split(eng, n, i3, slot)
                else:
                    dve_split(eng, n, slot)
                if after:
                    after(t, (base + t0 + j) % RING)
            if full:
                with eng.Fori(0, full) as i:
                    for j in range(RING):
                        step(i * RING + (t0 + j), i, j)
            for r in range(full * RING, count):
                step(t0 + r, None, r % RING)

        def pe_triple(out, lhs, rhs, start, stop, skip=True):
            nc.tensor.matmul(out, lhs[0], rhs[0], start=start, stop=False, skip_group_check=skip)
            nc.tensor.matmul(out, lhs[0], rhs[1], start=False, stop=False, skip_group_check=skip)
            return nc.tensor.matmul(out, lhs[1], rhs[0], start=False, stop=stop, skip_group_check=skip)

        evacs = {"act": 0, "dve": 0}

        def pe_gemm(pe, base, count, evac, by, outs):
            sig = act_evac if evac == "act" else dve_evac
            e0 = evacs[evac]
            evacs[evac] += count

            def tile(t, j):
                slot = (base + j) % RING
                pe.wait_ge(lo_ready.sem, t + (base + 1))
                pe.wait_ge(sig.sem, t + (e0 + 1))
                last = None
                groups = outs(5 + slot)
                for gi, (out, wfirst, operand) in enumerate(groups):
                    for k in range(KT):
                        w = (whi[:, slot, k * P:(k + 1) * P], wlo[:, slot, k * P:(k + 1) * P])
                        o = operand(k)
                        last = pe_triple(out, w if wfirst else o, o if wfirst else w, k == 0, k == KT - 1)
                last.then_inc(tile_used.sem, 1)
            repeat(pe, count, RING, tile)

        def used(base, t):
            return t + (base + RING + 1)

        def span(segs):
            return (slice(0, T2) if len(segs) == 2 else slice(segs[0] * SEG, segs[0] * SEG + SEG))

        def a_cols(segs):
            c = span(segs)
            return lambda k: (a_hi[:, k, c], a_lo[:, k, c])

        def pe_ffn(pe, base, seg, F):
            a = a_cols([seg])

            def h_tile(t, j, bank):
                slot = (base + j) % RING
                pe.wait_ge(lo_ready.sem, t + (base + 1))
                for k in range(KT):
                    w = (whi[:, slot, k * P:(k + 1) * P], wlo[:, slot, k * P:(k + 1) * P])
                    last = pe_triple(ps[:, bank, 0:SEG], w, a(k), k == 0, k == KT - 1)
                last.then_inc(tile_used.sem, 1)

            def out_tile(t, j, par_, f, first, lastf):
                slot = (base + j) % RING
                pe.wait_ge(lo_ready.sem, t + (base + 1))
                pe.wait_ge(S("g_ready").sem, f + (g0 + 1))
                for m in range(KT):
                    w = (whi[:, slot, m * P:(m + 1) * P], wlo[:, slot, m * P:(m + 1) * P])
                    g = (g_hi[:, par_, :], g_lo[:, par_, :])
                    last = pe_triple(ps[:, m // 2, (m % 2) * SEG:(m % 2 + 1) * SEG], w, g,
                                     first and m % 2 == 0, lastf)
                last.then_inc(tile_used.sem, 1)

            g0 = gcount["pe"]
            gcount["pe"] += F
            h_tile(0, 0, 4)
            h_tile(1, 1, 6)
            h_tile(2, 2, 5)
            h_tile(3, 0, 7)
            out_tile(4, 1, 0, 0, True, False)

            with pe.Fori(0, (F - 2) // 2) as i:
                for u in range(2):
                    t = i * 6 + (5 + 3 * u)
                    h_tile(t, 2, 4 + u)
                    h_tile(t + 1, 0, 6 + u)
                    out_tile(t + 2, 1, 1 - u, i * 2 + (1 + u), False, False)
            out_tile(3 * F - 1, 2, (F - 1) % 2, F - 1, False, True)

        gcount = {"pe": 0, "act": 0, "dve": 0}

        def act_ffn(act, base, F):
            g0 = gcount["act"]
            gcount["act"] += F

            def split(t, i, j):
                c = base + j + LEAD
                n = t + (base + LEAD)
                i3 = n // RING if i is None else i * 2 + c // RING
                act_split(act, n, i3, c % RING)

            def silu(f, th1, par_):
                act.wait_ge(tile_used.sem, used(base, th1))
                if not (isinstance(f, int) and f + g0 < 2):
                    act.wait_ge(S("g_ready").sem, f + (g0 - 1))
                nc.scalar.activation(sil[:, par_, :], ps[:, 4 + par_, 0:SEG], ACT.Silu
                                     ).then_inc(S("silu_ready").sem, 1)
            split(0, None, 0)
            split(1, None, 1)
            silu(0, 0, 0)
            split(2, None, 2)
            split(3, None, 3)
            split(4, None, 4)
            with act.Fori(0, (F - 2) // 2) as i:
                for u in range(2):
                    silu(i * 2 + (1 + u), i * 6 + (2 + 3 * u), 1 - u)
                    for v in range(3):
                        j = 5 + 3 * u + v
                        split(i * 6 + j, i, j)
            silu(F - 1, 3 * (F - 1) - 1, (F - 1) % 2)
            split(3 * F - 1, None, 3 * F - 1)

        def dve_ffn(dve, base, F, gate=None):
            g0 = gcount["dve"]
            gcount["dve"] += F

            def hidden(f, th3, tout, par_, e=None):
                dve.wait_ge(S("silu_ready").sem, f + (g0 + 1))
                dve.wait_ge(tile_used.sem, used(base, th3))
                nc.vector.tensor_tensor(g_f[:, par_, :], sil[:, par_, :], ps[:, 6 + par_, 0:SEG],
                                        ALU.mult).then_inc(S("g_f").sem, 1)
                cnt = 1
                if gate is not None:
                    dve.wait_ge(S("g_f").sem, f * 2 + (gf0 + 1))
                    nc.vector.tensor_tensor(g_f[:, par_, :], g_f[:, par_, :],
                                            gate[:, one(e), :].rearrange("p o t -> p (o t)"),
                                            ALU.mult).then_inc(S("g_f").sem, 1)
                    cnt = 2
                dve.wait_ge(S("g_f").sem, f * cnt + (gf0 + cnt))
                if tout is not None:
                    dve.wait_ge(tile_used.sem, used(base, tout))
                nc.vector.tensor_copy(g_hi[:, par_, :], g_f[:, par_, :]).then_inc(S("g_hi").sem, 1)
                dve.wait_ge(S("g_hi").sem, f + (g0 + 1))
                nc.vector.tensor_tensor(g_lo[:, par_, :], g_f[:, par_, :], g_hi[:, par_, :].bitcast(F32),
                                        ALU.subtract).then_inc(S("g_ready").sem, 1)

            def split(t, j):
                dve_split(dve, t + (base + LEAD), (base + j + LEAD) % RING)
            gf0 = gfc[0]
            gfc[0] += F * (2 if gate is not None else 1)
            split(0, 0)
            split(1, 1)
            hidden(0, 1, None, 0, 0)
            for t in (2, 3, 4):
                split(t, t)

            def pair(i, f0, e0, e1, first):
                for u in range(2):
                    f = i * 2 + (f0 + u)
                    t = i * 6 + (3 * (f0 + u) + 2)
                    hidden(f, t - 2, None if (first and u == 0) else t - 4, 1 - u, (e0, e1)[u])
                    for v in range(3):
                        split(t + v, 2 + v)
            if gate is None:
                pair(0, 1, 0, 0, True)
                with dve.Fori(0, (F - 4) // 2) as i:
                    pair(i, 3, 0, 0, False)
            else:
                pair(0, 1, 0, 0, True)
                with dve.Fori(0, 9) as i:
                    pair(i, 3, 0, 0, False)
                with dve.Fori(0, NE - 1) as e:
                    pair(e * 11, 21, e, e + 1, False)
                    with dve.Fori(0, 10) as i:
                        pair(e * 11 + i, 23, e + 1, e + 1, False)
            hidden(F - 1, 3 * (F - 1), 3 * (F - 3) + 4, (F - 1) % 2, NE - 1)
            split(3 * F - 1, 3 * F - 1)

        gfc = [0]

        class Chain:
            def __init__(self, eng, name):
                self.eng, self.sig, self.n = eng, S(name), 0

            def __call__(self, ins, also=None):
                self.n += 1
                ins.then_inc(self.sig.sem, 1)
                self.eng.wait_ge(self.sig.sem, self.n)

        def bc(ap, shape):
            return ap.broadcast_to(list(shape))

        def seg_cols(seg):
            return slice(seg * SEG, seg * SEG + SEG)

        def act_norm(act, seg, work, to_a=True):
            act.wait_ge(*S("h_ready").next("act"))
            nc.scalar.activation(work[:], hT[:, :, seg_cols(seg)], ACT.Square).then_inc(*S("sq_ready").one)
            act.wait_ge(*S("ms_ready").next("act"))
            nc.scalar.activation(rs[:, 0:SEG], rs[:, 0:SEG], ACT.Sqrt).then_inc(*S("rt_ready").one)
            if to_a:
                act.wait_ge(*S("a_ready").next("act"))
                nc.scalar.activation(a_hi[:, :, seg_cols(seg)], work[:], ACT.Copy).then_inc(*S("ahi_ready").one)

        def pe_norm(pe):
            pe.wait_ge(*S("sq_ready").next("pe"))
            for k in range(KT):
                last = nc.tensor.matmul(ps[:, 4, 0:SEG], ones[:], normw[:, k, :],
                                        start=(k == 0), stop=(k == KT - 1))
            last.then_inc(*S("ss_ready").one)

        def dve_norm(dve, link, seg, work, gain, shift, final=None):
            dve.wait_ge(*S("ss_ready").next("dve"))
            nc.vector.tensor_scalar(rs[:, 0:SEG], ps[:, 4, 0:SEG], 1.0 / D, EPS, ALU.mult, ALU.add
                                    ).then_inc(*S("ms_ready").one)
            dve.wait_ge(*S("rt_ready").next("dve"))
            link(nc.vector.reciprocal(rs[:, 0:SEG], rs[:, 0:SEG]))
            link(nc.vector.tensor_tensor(work[:], hT[:, :, seg_cols(seg)],
                                         bc(rs[:, 0:SEG].unsqueeze(1), [P, KT, SEG]), ALU.mult))
            for k in range(KT):
                dst = work[:, k, :] if final is None else hT[:, k, seg_cols(seg)]
                if shift is None:
                    last = nc.vector.tensor_scalar(dst, work[:, k, :], gain(k), None, ALU.mult)
                else:
                    last = nc.vector.tensor_scalar(dst, work[:, k, :], gain(k), shift(k), ALU.mult, ALU.add)
                if k < KT - 1:
                    link(last)
            if final is None:
                last.then_inc(*S("a_ready").one)
                dve.wait_ge(*S("ahi_ready").next("dve"))
                dve.wait_ge(*S("a_ready").next("dve"))
                nc.vector.tensor_tensor(a_lo[:, :, seg_cols(seg)], work[:],
                                        a_hi[:, :, seg_cols(seg)].bitcast(F32), ALU.subtract
                                        ).then_inc(*S("alo_ready").one)
                dve.wait_ge(*S("alo_ready").next("dve"))
            else:
                last.then_inc(*S(final).one)

        normw = sb("normw", [P, KT, SEG], at=arena)

        def load_list(sp):
            sp.dma_start(par[:], io["params"]).then_inc(*S("par").dma)
            sp.dma_start(ident[:], io["consts"][:, 0:128]).then_inc(*S("par").dma)
            sp.dma_start(ones[:], io["consts"][:, 128:256]).then_inc(*S("par").dma)
            sp.dma_start(bones[:], io["consts"][:, 256:384]).then_inc(*S("par").dma)
            sp.dma_start(con[:], io["consts"][:, 384:NCON]).then_inc(*S("par").dma)
            sp.dma_start(hT[:, :, 0:SEG], io["ctxT"]).then_inc(*S("par").dma)
            sp.dma_start(hT[:, :, SEG:T2], io["xT"]).then_inc(*S("par").dma)

        NLOAD = 7 * 16

        NJ = 6 * D // 1024
        GROUPS = 2 * NJ
        modr = sb("modr", [P, GROUPS, 1024], at=area)

        def ada_tiles(eng, tile, group_end):
            with eng.Fori(0, GROUPS // 3) as i:
                for g in range(3):
                    for k in range(KT):
                        tile(i, g * KT + k)
                    group_end(i, g)

        def act_ada(act):
            act.wait_ge(S("par").sem, NLOAD)
            nc.scalar.activation(cv[:], pc("cvec"), ACT.Silu).then_inc(*S("cv").one)
            act.wait_ge(*S("cv").next("act"))
            nc.scalar.activation(cv_hi[:].rearrange("p k s -> p (k s)"), cv[:], ACT.Copy).then_inc(*S("cvh").one)
            act.sem_inc(S("row_sb").sem, 3)

            def group_end(i, g):
                act.wait_ge(tile_used.sem, i * 3 * KT + used(0, (g + 1) * KT - 1))
                nc.scalar.activation(modr[0:2, bass.ds(i * 3 + g, 1), :].rearrange("p o c -> p (o c)"),
                                     ps[0:2, 2 * g:2 * g + 2, :].rearrange("p b c -> p (b c)"),
                                     ACT.Copy).then_inc(S("row_sb").sem, 1)
            ada_tiles(act, lambda i, j: act_split(act, i * 3 * KT + (j + LEAD), i * KT + (j + LEAD) // RING,
                                                  (j + LEAD) % RING), group_end)

        def pe_ada(pe):
            pe.wait_ge(*S("cvl").next("pe"))

            def tile(i, j):
                k, g, slot = j % KT, j // KT, j % RING
                if k == 0:
                    pe.wait_ge(S("row_sb").sem, i * 3 + (g + 1))
                pe.wait_ge(lo_ready.sem, i * 3 * KT + (j + 1))
                for half in range(2):
                    c = slice(half * 512, half * 512 + 512)
                    last = pe_triple(ps[0:2, 2 * g + half, :], (cv_hi[:, k, :], cv_lo[:, k, :]),
                                     (whi[:, slot, c], wlo[:, slot, c]), k == 0, k == KT - 1)
                last.then_inc(tile_used.sem, 1)
            ada_tiles(pe, tile, lambda i, g: None)
            pe.wait_ge(S("row_sb").sem, GROUPS + 3)
            for g in range(GROUPS):
                for c in range(8):
                    j = g * 8 + c
                    last = nc.tensor.transpose(ps[:, 6, 2 * j:2 * j + 2], modr[0:2, g, c * P:(c + 1) * P],
                                               ident[0:2, 0:2])
            last.then_inc(*S("mod_ps").one)

        def dve_ada(dve, link):
            dve.wait_ge(S("par").sem, NLOAD)
            dve.wait_ge(*S("cvh").next("dve"))
            nc.vector.tensor_tensor(cv_lo[:].rearrange("p k s -> p (k s)"), cv[:],
                                    cv_hi[:].rearrange("p k s -> p (k s)").bitcast(F32),
                                    ALU.subtract).then_inc(*S("cvl").one)
            ada_tiles(dve, lambda i, j: dve_split(dve, i * 3 * KT + (j + LEAD), (j + LEAD) % RING),
                      lambda i, g: None)
            dve.wait_ge(*S("mod_ps").next("dve"))
            link(nc.vector.tensor_tensor(mod[:], ps[:, 6, 0:192].rearrange("p (j s) -> p j s", s=2),
                                         bc(pc("b_ada").unsqueeze(2), [P, 96, 2]), ALU.add))
            for L in range(2):
                for h in range(2):
                    sc = mod[:, L * 48 + (3 * h + 1) * 8:L * 48 + (3 * h + 2) * 8, :]
                    dst = gsm[:, 2 * L + h, :, :]
                    g = pc("n_mix" if h == 0 else "n_ffn", 8 * L, 8)
                    link(nc.vector.tensor_scalar(dst, sc, 1.0, None, ALU.add))
                    link(nc.vector.tensor_tensor(dst, dst, bc(g.unsqueeze(2), [P, KT, 2]), ALU.mult))

        def m_col(L, j, k, s):
            return mod[:, L * 48 + j * 8 + k, s:s + 1]

        def gain_of(L, h, s):
            return lambda k: gsm[:, 2 * L + h, k, s:s + 1]

        def shift_of(L, h, s):
            return lambda k: m_col(L, 3 * h, k, s)

        def dve_resid(dve, link, base, count, segs, coef):
            def evac(t, slot):
                dve.wait_ge(tile_used.sem, used(base, t))
                for i, s in enumerate(segs):
                    dst = hT[:, t, seg_cols(s)]
                    c0 = s * SEG if len(segs) == 2 else 0
                    ins = nc.vector.scalar_tensor_tensor(dst, ps[:, 5 + slot, c0:c0 + SEG], coef(t, s), dst,
                                                         ALU.mult, ALU.add)
                    if i == len(segs) - 1:
                        ins.then_inc(dve_evac.sem, 1)
                    else:
                        link(ins)
            for t in range(count):
                dve_split(dve, base + t + LEAD, (base + t + LEAD) % RING)
                evac(t, (base + t) % RING)
            dve.wait_ge(dve_evac.sem, RING + evd["n"] + count)
            evd["n"] += count

        evd = {"n": 0}

        def dve_ffn_out(dve, link, base, F, seg, coef):
            dve.wait_ge(tile_used.sem, used(base, 3 * F - 1))
            for m in range(KT):
                dst = hT[:, m, seg_cols(seg)]
                src = ps[:, m // 2, (m % 2) * SEG:(m % 2 + 1) * SEG]
                c = coef(m)
                link(nc.vector.scalar_tensor_tensor(dst, src, c, dst, ALU.mult, ALU.add))


        ob = END - 16 * 1024 - 64
        o0 = sb("o0", [P, KT, T2], at=ob)
        xc, hin, _ = lay(area, [("xc", [P, 8, T2]), ("hin", [P, 2, NMC, 512])])
        xtm, btm, xdt, _ = lay(zx_at, [("xtm", [P, NMC, 512]), ("btm", [P, NMC, 2, P]), ("xdt", [P, 2, 512])])
        wm, cm_, e1, dd, gm, tmv, du, dw, dl_, _m = lay(m0, [
            ("wm", [P, 2, 512]), ("cm_", [P, 2, 512]), ("e1", [P, 512]), ("dd", [P, 512]),
            ("gm", [P, 2, P]), ("tmv", [P, 3, NMC, 40]), ("du", [P, T2]), ("dw", [P, T2]), ("dl_", [P, T2])])
        assert _m <= ob, (_m, ob)
        DT = 40

        def act_win(act):
            def evac_to(dst, pads):
                def evac(t, slot, first):
                    act.wait_ge(tile_used.sem, used(BASE["w_in"], t))
                    src = ps[:, 5 + slot, :]
                    if pads:
                        d = dst[:, one(t - first), :, 2:258].rearrange("p o s t -> p (o s) t")
                        src = src.rearrange("p (s t) -> p s t", s=2)
                    else:
                        d = dst[:, one(t - first), :].rearrange("p o t -> p (o t)")
                    nc.scalar.activation(d, src, ACT.Copy).then_inc(act_evac.sem, 1)
                return evac
            for n, dst, pads, first in ((8, zx, True, 0), (4, zg, False, 8), (1, zdt.rearrange("p (o t) -> p o t", o=1), False, 12),
                                        (14, zrw, True, 13)):
                ev = evac_to(dst, pads)
                run_tiles(act, "act", BASE["w_in"], n, t0=first,
                          after=lambda t, slot, ev=ev, first=first: ev(t, slot, first))

        def dve_win(dve, link):
            for z in (zx, zrw):
                for sl in (slice(0, 2), slice(258, 260)):
                    link(nc.vector.memset(z[:, :, :, sl], 0.0))
            run_tiles(dve, "dve", BASE["w_in"], 27)
            dve.wait_ge(act_evac.sem, RING + 27)

        def dve_conv(dve, link):
            for i in range(8):
                for tap in range(5):
                    x = zx[:, i, :, tap:tap + SEG]
                    dst = xc[:, i, :].rearrange("p (s t) -> p s t", s=2)
                    w = pc("cw", i * 5 + tap, 1)
                    if tap == 0:
                        link(nc.vector.tensor_scalar(dst, x, w, None, ALU.mult))
                    elif tap < 4:
                        link(nc.vector.scalar_tensor_tensor(dst, x, w, dst, ALU.mult, ALU.add))
                    else:
                        nc.vector.scalar_tensor_tensor(dst, x, w, dst, ALU.mult, ALU.add
                                                       ).then_inc(*S("conv_ready").one)

        def act_conv(act):
            for i in range(8):
                act.wait_ge(*S("conv_ready").next("act"))
                nc.scalar.activation(xc[:, i, :], xc[:, i, :], ACT.Silu, bias=pc("cb", i, 1)
                                     ).then_inc(*S("xc_ready").one)

        def dve_dt(dve, link):
            z, u, w, l = zdt[0:DT, :], du[0:DT, :], dw[0:DT, :], dl_[0:DT, :]
            link(nc.vector.tensor_scalar(z, z, pc("dtb", 0, 1)[0:DT], None, ALU.add))
            link(nc.vector.scalar_tensor_tensor(w, z, -1.0, z, ALU.mult, ALU.max))
            dve.wait_ge(*S("aneg").next("dve"))
            dve.sem_inc(S("dt_abs").sem, 1)
            dve.wait_ge(*S("dt_u").next("dve"))
            nc.vector.tensor_scalar(w, u, 1.0, None, ALU.add).then_inc(*S("dt_w").one)
            dve.wait_ge(*S("dt_l").next("dve"))
            link(nc.vector.scalar_tensor_tensor(u, w, -1.0, u, ALU.add, ALU.subtract))
            link(nc.vector.reciprocal(w, w))
            link(nc.vector.tensor_tensor(u, u, w, ALU.mult))
            link(nc.vector.tensor_tensor(l, l, u, ALU.subtract))
            link(nc.vector.scalar_tensor_tensor(z, z, 0.0, l, ALU.max, ALU.add))
            link(nc.vector.tensor_scalar(u, z, pc("alog", 0, 1)[0:DT], -1.0, ALU.mult, ALU.mult))
            link(nc.vector.tensor_tensor_scan(w, cc("scan128")[0:DT], u, 0.0, ALU.mult, ALU.add))
            ch = lambda a: a.rearrange("p (c l) -> p c l", l=MC)
            tot = ch(w)[:, :, MC - 1:MC]
            link(nc.vector.tensor_tensor(ch(l), bc(tot, [DT, NMC, MC]), ch(w), ALU.subtract))
            b = slice(32, DT)
            link(nc.vector.tensor_tensor(du[b], dw[b], du[b], ALU.subtract))
            link(nc.vector.tensor_tensor(ch(dw[b]), bc(ch(dw[b])[:, :, MC - 1:MC], [8, NMC, MC]),
                                         ch(du[b]), ALU.subtract))
            link(nc.vector.tensor_copy(dl_[b], du[b]))
            dg = e1[0:DT, 0:NMC * DT].rearrange("p (c j) -> p c j", c=NMC)
            link(nc.vector.tensor_copy(dg, bc(ident[0:DT, 0:DT].unsqueeze(1), [DT, NMC, DT])))
            f = slice(0, 32)
            link(nc.vector.tensor_tensor(dg[f], dg[f], bc(ch(dw[f])[:, :, MC - 1:MC], [32, NMC, DT]), ALU.mult))
            nc.vector.tensor_tensor(dg[b], dg[b], bc(ch(dw[b])[:, :, 0:1], [8, NMC, DT]), ALU.mult
                                    ).then_inc(*S("dt_rows").one)
            dve.wait_ge(*S("dt_rows").next("dve"))

        def act_dt(act):
            act.wait_ge(S("par").sem, NLOAD)
            al = pc("alog", 0, 1)[0:DT]
            nc.scalar.activation(al, al, ACT.Exp).then_inc(*S("aneg").one)
            act.wait_ge(*S("dt_abs").next("act"))
            nc.scalar.activation(du[0:DT], dw[0:DT], ACT.Exp, scale=-1.0).then_inc(*S("dt_u").one)
            act.wait_ge(*S("dt_w").next("act"))
            nc.scalar.activation(dl_[0:DT], dw[0:DT], ACT.Ln).then_inc(*S("dt_l").one)
            act.wait_ge(*S("dt_rows").next("act"))
            nc.scalar.activation(dl_[0:DT], dl_[0:DT], ACT.Exp).then_inc(*S("dec_rows").one)
            act.wait_ge(*S("tot_ps").next("act"))
            nc.scalar.activation(dd[:, 0:NMC * DT], ps[:, 4, 0:NMC * DT], ACT.Exp).then_inc(*S("etot").one)

        def pe_dt(pe):
            pe.wait_ge(*S("dt_rows").next("pe"))
            nc.tensor.matmul(ps[:, 4, 0:NMC * DT], ones[0:DT, :], e1[0:DT, 0:NMC * DT],
                             start=True, stop=True).then_inc(*S("tot_ps").one)
            pe.wait_ge(*S("dec_rows").next("pe"))
            for q, rows in enumerate((zdt, dw, dl_)):
                for c in range(NMC):
                    last = nc.tensor.transpose(ps[:, 5 + q, c * DT:(c + 1) * DT], rows[0:DT, c * MC:(c + 1) * MC],
                                               ident[0:DT, 0:DT])
            last.then_inc(*S("tm_ps").one)
            pe.wait_ge(*S("xc_ready").next("pe", 8))
            for c in range(NMC):
                for i in range(4):
                    last = nc.tensor.transpose(ps[:, c, i * P:(i + 1) * P], xc[:, i, c * MC:(c + 1) * MC], ident[:])
            last.then_inc(*S("xtm_ps").one)
            pe.wait_ge(*S("xtm_sb").next("pe"))
            for c in range(NMC):
                for g in range(2):
                    last = nc.tensor.transpose(ps[:, c // 2, ((c % 2) * 2 + g) * P:((c % 2) * 2 + g + 1) * P],
                                               xc[:, 4 + g, c * MC:(c + 1) * MC], ident[:])
            last.then_inc(*S("btm_ps").one)

        def dve_tm(dve, link):
            dve.wait_ge(*S("tm_ps").next("dve"))
            for q in range(3):
                link(nc.vector.tensor_copy(tmv[:, q, :, :].rearrange("p c j -> p (c j)"),
                                           ps[:, 5 + q, 0:NMC * DT]))
            dve.wait_ge(*S("xtm_ps").next("dve"))
            for c in range(NMC):
                last = nc.vector.tensor_copy(xtm[:, c, :], ps[:, c, :])
            last.then_inc(*S("xtm_sb").one)
            dve.wait_ge(*S("btm_ps").next("dve"))
            dve.wait_ge(*S("xtm_sb").next("dve"))
            for b_ in range(2):
                link(nc.vector.tensor_copy(btm[:, 2 * b_:2 * b_ + 2, :, :].rearrange("p c g n -> p (c g n)"),
                                           ps[:, b_, :]))

        def heads8(ap):
            return ap.rearrange("p (h e) -> p h e", h=8)

        def dve_states(dve, link):
            dve.wait_ge(*S("etot").next("dve"))
            link(nc.vector.memset(hin[:, 0, 0, :], 0.0))
            link(nc.vector.memset(hin[:, 1, 1, :], 0.0))
            et = dd[:, 0:NMC * DT].rearrange("p (c j) -> p c j", c=NMC)
            order = ((0, 1, 2, 3), (1, 0, 3, 2))
            for step in range(NMC - 1):
                for d in range(2):
                    c, nxt = order[d][step], order[d][step + 1]
                    if not (step == 0 and d == 0):
                        dve.wait_ge(*S("st_ps").next("dve"))
                        add_state(dve, link, *pend[0])
                    x = heads8(xdt[:, 0, :])
                    link(nc.vector.tensor_tensor(x, heads8(xtm[:, c, :]),
                                                 bc(tmv[:, 0, c, 32 * d:32 * d + 8].unsqueeze(2), [P, 8, 64]), ALU.mult))
                    nc.vector.tensor_tensor(x, x, bc(tmv[:, 2, c, 32 * d:32 * d + 8].unsqueeze(2), [P, 8, 64]),
                                            ALU.mult).then_inc(*S("xdd").one)
                    pend[0] = (d, c, nxt, et)
            dve.wait_ge(*S("st_ps").next("dve"))
            add_state(dve, link, *pend[0])

        pend = [None]

        def add_state(dve, link, d, c, nxt, et):
            dst = heads8(hin[:, d, nxt, :])
            link(nc.vector.tensor_tensor(dst, heads8(hin[:, d, c, :]),
                                         bc(et[:, c, 32 * d:32 * d + 8].unsqueeze(2), [P, 8, 64]), ALU.mult))
            link(nc.vector.tensor_tensor(hin[:, d, nxt, :], hin[:, d, nxt, :], ps[:, 0, :], ALU.add))

        def pe_states(pe):
            order = ((0, 1, 2, 3), (1, 0, 3, 2))
            for step in range(NMC - 1):
                for d in range(2):
                    c = order[d][step]
                    pe.wait_ge(*S("xdd").next("pe"))
                    for g in range(2):
                        last = nc.tensor.matmul(ps[:, 0, g * 256:(g + 1) * 256], btm[:, c, g, :],
                                                xdt[:, 0, g * 256:(g + 1) * 256], start=True, stop=True)
                    last.then_inc(*S("st_ps").one)

        def dve_ssd(dve, link):
            for c in range(NMC):
                cs = slice(c * MC, (c + 1) * MC)
                if c:
                    dve.wait_ge(*S("y_pe").next("dve"))
                for d in range(2):
                    ins = nc.vector.tensor_tensor(heads8(xdt[:, d, :]), heads8(xtm[:, c, :]),
                                                  bc(tmv[:, 0, c, 32 * d:32 * d + 8].unsqueeze(2), [P, 8, 64]),
                                                  ALU.mult)
                    link(ins)
                for g in range(2):
                    dve.wait_ge(*S("g_ps").next("dve"))
                    if g:
                        dve.wait_ge(*S("y_pe").next("dve"))
                    link(nc.vector.tensor_tensor(gm[:], bc(ps[:, 1, 0:P].unsqueeze(1), [P, 2, P]),
                                                 cc("mssd").rearrange("p (d t) -> p d t", d=2), ALU.mult))
                    for d in range(2):
                        dve.wait_ge(*S("e1").next("dve"))
                        h0 = 32 * d + 4 * g
                        link(nc.vector.tensor_tensor(
                            cm_[:, d, :].rearrange("p (h t) -> p h t", h=4), e1[:].rearrange("p (h t) -> p h t", h=4),
                            bc(xc[:, 6 + g, cs].unsqueeze(1), [P, 4, MC]), ALU.mult))
                        link(nc.vector.tensor_tensor(
                            dd[:].rearrange("p (h t) -> p h t", h=4), ps[:, 2 + d, :].rearrange("p (h t) -> p h t", h=4),
                            bc(tmv[:, 1, c, h0:h0 + 4].unsqueeze(2), [P, 4, MC]), ALU.subtract))
                        nc.vector.tensor_scalar(dd[:], dd[:], 0.0, None, ALU.min).then_inc(*S("dd").one)
                        dve.wait_ge(*S("e2").next("dve"))
                        nc.vector.tensor_tensor(
                            wm[:, d, :].rearrange("p (h t) -> p h t", h=4), e1[:].rearrange("p (h t) -> p h t", h=4),
                            bc(gm[:, d, :].unsqueeze(1), [P, 4, MC]), ALU.mult).then_inc(*S("wm").one)
                        dve.wait_ge(*S("wm").next("dve"))
            dve.wait_ge(*S("y_pe").next("dve"))

        def act_ssd(act):
            for c in range(NMC):
                for g in range(2):
                    for d in range(2):
                        act.wait_ge(*S("bc_ps").next("act"))
                        if not (c == 0 and g == 0 and d == 0):
                            act.wait_ge(*S("wm").next("act"))
                        nc.scalar.activation(e1[:], ps[:, 2 + d, :], ACT.Exp).then_inc(*S("e1").one)
                        act.wait_ge(*S("dd").next("act"))
                        nc.scalar.activation(e1[:], dd[:], ACT.Exp).then_inc(*S("e2").one)
                    act.wait_ge(*S("y_pe").next("act"))
                    if g == 1:
                        nc.scalar.activation(o0[:, 4:8, c * MC:(c + 1) * MC],
                                             ps[:, 4, :].rearrange("p (i t) -> p i t", i=4), ACT.Copy
                                             ).then_inc(*S("y_sb").one)
            act.wait_ge(*S("wm").next("act"))
            for i in range(4):
                last = nc.scalar.activation(zg[:, i, :], zg[:, i, :], ACT.Silu)
            last.then_inc(*S("zg_act").one)

        def pe_ssd(pe):
            for c in range(NMC):
                cs = slice(c * MC, (c + 1) * MC)
                for g in range(2):
                    nc.tensor.matmul(ps[:, 1, 0:P], xc[:, 4 + g, cs], xc[:, 6 + g, cs], start=True, stop=True
                                     ).then_inc(*S("g_ps").one)
                    for d in range(2):
                        for h in range(4):
                            j = 32 * d + 4 * g + h
                            last = nc.tensor.matmul(ps[:, 2 + d, h * MC:(h + 1) * MC],
                                                    ident[0:DT, j:j + 1].broadcast_to([DT, P]), dw[0:DT, cs],
                                                    start=True, stop=True)
                        last.then_inc(*S("bc_ps").one)
                    pe.wait_ge(*S("wm").next("pe", 2))
                    if g == 0 and c:
                        pe.wait_ge(*S("y_sb").next("pe"))
                    for h in range(4):
                        hh = 4 * g + h
                        out = ps[64 * (hh % 2):64 * (hh % 2) + 64, 4, (hh // 2) * MC:(hh // 2 + 1) * MC]
                        for d in range(2):
                            nc.tensor.matmul(out, xdt[:, d, hh * 64:(hh + 1) * 64],
                                             wm[:, d, h * MC:(h + 1) * MC], start=(d == 0), stop=False)
                            last = nc.tensor.matmul(out, hin[:, d, c, hh * 64:(hh + 1) * 64],
                                                    cm_[:, d, h * MC:(h + 1) * MC], start=False, stop=(d == 1))
                    last.then_inc(*S("y_pe").one)

        def dve_mbout(dve, link):
            dve.wait_ge(*S("y_sb").next("dve", 4))
            dve.wait_ge(*S("zg_act").next("dve"))
            for i in range(4):
                y = o0[:, 4 + i, :]
                link(nc.vector.scalar_tensor_tensor(y, xc[:, i, :], pc("mbd", i, 1), y, ALU.mult, ALU.add))
                link(nc.vector.tensor_tensor(y, y, zg[:, i, :], ALU.mult))
                link(nc.vector.tensor_tensor(zg[:, i, :], y, y, ALU.mult))
            dve.sem_inc(S("mb_sq").sem, 1)
            dve.wait_ge(*S("mb_ss").next("dve"))
            for g in range(2):
                link(nc.vector.tensor_scalar(zg[:, g, :], ps[:, 2 + g, :], 1.0 / 256, EPS, ALU.mult, ALU.add))
            dve.sem_inc(S("mb_ms").sem, 1)
            dve.wait_ge(*S("mb_rt").next("dve"))
            link(nc.vector.reciprocal(zg[:, 0:2, :], zg[:, 0:2, :]))
            for i in range(4):
                y = o0[:, 4 + i, :]
                link(nc.vector.scalar_tensor_tensor(y, y, pc("mbn", i, 1), zg[:, i // 2, :], ALU.mult, ALU.mult))

        def pe_mbout(pe):
            pe.wait_ge(*S("mb_sq").next("pe"))
            for g in range(2):
                for i in range(2):
                    last = nc.tensor.matmul(ps[:, 2 + g, :], ones[:], zg[:, 2 * g + i, :],
                                            start=(i == 0), stop=(i == 1))
            last.then_inc(*S("mb_ss").one)

        def act_mbout(act):
            act.wait_ge(*S("mb_ms").next("act"))
            nc.scalar.activation(zg[:, 0:2, :], zg[:, 0:2, :], ACT.Sqrt).then_inc(*S("mb_rt").one)

        ar, bt, kt, _ = lay(area, [("ar", [P, 2, 4, NRC, 2, RC]), ("bt", [P, 2, 4, SEG]), ("kt", [P, 2, 4, SEG])])
        vv, bon, lwa, lg, st, dls, t0_ = lay(zx_at, [
            ("vv", [P, 4, SEG]), ("bon", [P, 4, SEG]), ("lwa", [P, SEG]), ("lg", [P, SEG]),
            ("st", [P, 2, 4, RC]), ("dls", [P, 2, 4, NRC])])
        lora, gup, t0_ = lay(t0_, [("lora", [P, 512]), ("gup", [P, 512])])
        rr, kk_, kn, ld, cu, ic, ee, bs, _r = lay(t0_, [(n, [P, 4, SEG]) for n in
                                                     ("rr", "kk_", "kn", "ld", "cu", "ic", "ee", "bs")])
        assert _r <= ob, (_r, ob)
        yb = sb("yb", [P, 4, SEG], at=_r - 4 * SEG * 4)
        br, kr, tt, xs, nl, btt, ktt, vtt, rh, uu, _r = lay(t0_, [
            ("br", [P, 2, 4, P]), ("kr", [P, 2, 4, P]), ("tt", [P, 2, 2, 4, RC]),
            ("xs", [P, 2, 4, RC]), ("nl", [P, 2, 2, 4, RC]), ("btt", [P, 2, 4, RC]),
            ("ktt", [P, 2, 4, RC]), ("vtt", [P, 2, 4, RC]), ("rh", [P, 2, 4, RC]), ("uu", [P, 2, 4, RC])])
        assert _r <= ob - 4 * SEG * 4

        def dve_shift(link, dst, i, seg):
            z = zrw[:, i, seg, :]
            link(nc.vector.tensor_scalar(dst, z[:, 2:258], c0[:, i:i + 1], None, ALU.mult))
            link(nc.vector.scalar_tensor_tensor(dst, z[:, 1:257], pc("mu_p", i, 1), dst, ALU.mult, ALU.add))
            return nc.vector.scalar_tensor_tensor(dst, z[:, 3:259], pc("mu_n", i, 1), dst, ALU.mult, ALU.add)

        c0 = sb("c0", [P, 14], at=END - 64)

        def fl(ap):
            return ap.rearrange("p m t -> p (m t)")

        def dve_rwprep(dve, link, seg):
            if seg == 0:
                link(nc.vector.tensor_tensor(c0[:], pc("mu_p"), pc("mu_n"), ALU.add))
                link(nc.vector.tensor_scalar(c0[:], c0[:], -1.0, 1.0, ALU.mult, ALU.add))
                link(nc.vector.memset(st[:], 0.0))
            link(dve_shift(link, lwa[:], 12, seg))
            link(dve_shift(link, lg[:], 13, seg))
            dve.sem_inc(S("lw_in").sem, 1)
            for m in range(4):
                link(dve_shift(link, rr[:, m, :], m, seg))
                link(dve_shift(link, kk_[:, m, :], 4 + m, seg))
                link(dve_shift(link, vv[:, m, :], 8 + m, seg))
            par4 = lambda n, i=0: bc(pc(n, i, 4).unsqueeze(2), [P, 4, SEG])
            link(nc.vector.tensor_tensor(kn[:], kk_[:], par4("kk"), ALU.mult))
            link(nc.vector.tensor_tensor(ee[:], kn[:], kn[:], ALU.mult))
            dve.sem_inc(S("kk_sq").sem, 1)
            dve.wait_ge(*S("kk_rt").next("dve"))
            link(nc.vector.tensor_scalar(fl(ee[:]), fl(ee[:]), 1e-12, None, ALU.max))
            link(nc.vector.reciprocal(ee[:], ee[:]))
            link(nc.vector.tensor_tensor(kn[:], kn[:], ee[:], ALU.mult))
            chm = lambda a: a.rearrange("p m (c l) -> p m c l", l=RC)
            flc = lambda a: a.rearrange("p m (c l) -> p (m c) l", l=RC)
            for d in range(2):
                dve.wait_ge(*S("wa_sig").next("dve"))
                link(nc.vector.tensor_scalar(fl(ld[:]), fl(ld[:]), -E05, None, ALU.mult))
                link(nc.vector.tensor_tensor_scan(fl(cu[:]), cc("scan64"), fl(ld[:]), 0.0, ALU.mult, ALU.add))
                tot = flc(cu[:])[:, :, RC - 1:RC]
                link(nc.vector.tensor_copy(dls[:, d, :, :].rearrange("p m c -> p (m c)"),
                                           tot.rearrange("p a o -> p (a o)")))
                if d == 0:
                    link(nc.vector.tensor_tensor(fl(ld[:]), fl(cu[:]), fl(ld[:]), ALU.subtract))
                    inc, exc = cu, ld
                else:
                    link(nc.vector.tensor_tensor(flc(ee[:]), bc(tot, [P, 16, RC]), flc(cu[:]), ALU.subtract))
                    link(nc.vector.tensor_tensor(ld[:], ee[:], ld[:], ALU.add))
                    link(nc.vector.tensor_copy(cu[:], ee[:]))
                    inc, exc = ld, cu
                dve.sem_inc(S("rw_dec").sem, 1)
                dve.wait_ge(*S("rw_exp").next("dve"))
                arv = lambda q: ar[:, d, :, :, q, :]
                link(nc.vector.scalar_tensor_tensor(flc(exc[:]), flc(kn[:]), -1.0, flc(exc[:]), ALU.mult, ALU.mult))
                for m in range(4):
                    link(nc.vector.tensor_copy(ar[:, d, m, :, 0, :], exc[:, m, :].rearrange("p (c l) -> p c l", l=RC)))
                    link(nc.vector.tensor_tensor(ar[:, d, m, :, 1, :], rr[:, m, :].rearrange("p (c l) -> p c l", l=RC),
                                                 ee[:, m, :].rearrange("p (c l) -> p c l", l=RC), ALU.mult))
                link(nc.vector.tensor_tensor(ee[:], kn[:], ic[:], ALU.mult))
                link(nc.vector.tensor_tensor(bt[:, d, :, :], ee[:], inc[:], ALU.mult))
                for m in range(4):
                    link(nc.vector.tensor_scalar(ic[:, m, :], ic[:, m, :], -1.0, pc("ka", m, 1), ALU.add, ALU.mult))
                link(nc.vector.scalar_tensor_tensor(fl(ic[:]), fl(ic[:]), 1.0, fl(kk_[:]), ALU.add, ALU.mult))
                link(nc.vector.tensor_tensor(kt[:, d, :, :], ic[:], inc[:], ALU.mult))
                if d == 0:
                    link(nc.vector.tensor_tensor(bs[:], ic[:], par4("rk", 0), ALU.mult))
                else:
                    link(nc.vector.tensor_tensor(ic[:], ic[:], par4("rk", 4), ALU.mult))
                    link(nc.vector.tensor_tensor(bs[:], bs[:], ic[:], ALU.add))
                dve.sem_inc(S("wa_free").sem, 1)
            nc.vector.tensor_tensor(bs[:], bs[:], rr[:], ALU.mult).then_inc(*S("bon_in").one)
            dve.wait_ge(*S("bon_ps").next("dve"))
            dve.wait_ge(*S("bon_in").next("dve"))
            for b_ in range(2):
                link(nc.vector.tensor_tensor(fl(bon[:, 2 * b_:2 * b_ + 2, :]), ps[:, b_, :],
                                             fl(vv[:, 2 * b_:2 * b_ + 2, :]), ALU.mult))
            dve.sem_inc(S("rw_prep").sem, 1)

        def act_rwprep(act, seg):
            act.wait_ge(*S("lw_in").next("act"))
            nc.scalar.activation(lwa[0:64, :], lwa[0:64, :], ACT.Tanh).then_inc(*S("lw_act").one)
            nc.scalar.activation(lg[:], lg[:], ACT.Sigmoid).then_inc(*S("lw_act").one)
            act.wait_ge(*S("kk_ps").next("act"))
            for b_ in range(2):
                last = nc.scalar.activation(fl(ee[:, 2 * b_:2 * b_ + 2, :]), ps[:, b_, :], ACT.Sqrt)
            last.then_inc(*S("kk_rt").one)
            for d in range(2):
                act.wait_ge(*S("wa_ps").next("act"))
                if d:
                    act.wait_ge(*S("wa_free").next("act"))
                for m in range(4):
                    cs = slice((m % 2) * SEG, (m % 2 + 1) * SEG)
                    nc.scalar.activation(ld[:, m, :], ps[:, 4 + m // 2, cs], ACT.Sigmoid, bias=pc("w0", 4 * d + m, 1))
                    last = nc.scalar.activation(ic[:, m, :], ps[:, 6 + m // 2, cs], ACT.Sigmoid,
                                                bias=pc("a0", 4 * d + m, 1))
                last.then_inc(*S("wa_sig").one)
                act.wait_ge(*S("rw_dec").next("act"))
                inc, exc = (cu, ld) if d == 0 else (ld, cu)
                nc.scalar.activation(ee[:], inc[:], ACT.Exp)
                nc.scalar.activation(exc[:], exc[:], ACT.Exp)
                nc.scalar.activation(dls[:, d, :, :], dls[:, d, :, :], ACT.Exp).then_inc(*S("rw_e").one)
                act.wait_ge(*S("rw_e").next("act"))
                nc.scalar.activation(inc[:], inc[:], ACT.Exp, scale=-1.0).then_inc(*S("rw_exp").one)
            act.wait_ge(*S("wa_free").next("act"))

        def pe_rwprep(pe, seg):
            if seg == 0:
                pe.wait_ge(S("lora").sem, 32)
            pe.wait_ge(*S("kk_sq").next("pe"))
            for b_ in range(2):
                last = nc.tensor.matmul(ps[:, b_, :], bones[:], fl(ee[:, 2 * b_:2 * b_ + 2, :]), start=True, stop=True)
            last.then_inc(*S("kk_ps").one)
            pe.wait_ge(*S("lw_act").next("pe", 2))
            for d in range(2):
                if d:
                    pe.wait_ge(*S("wa_sig").next("pe"))
                for m in range(4):
                    cs = slice((m % 2) * SEG, (m % 2 + 1) * SEG)
                    for q in range(2):
                        rows = slice(64 * q + 32 * d, 64 * q + 32 * d + 32)
                        last = nc.tensor.matmul(ps[:, 4 + 2 * q + m // 2, cs], lora[rows, m * P:(m + 1) * P],
                                                lwa[rows, :], start=True, stop=True)
                last.then_inc(*S("wa_ps").one)
            pe.wait_ge(*S("wa_sig").next("pe"))
            pe.wait_ge(*S("bon_in").next("pe"))
            for b_ in range(2):
                last = nc.tensor.matmul(ps[:, b_, :], bones[:], fl(bs[:, 2 * b_:2 * b_ + 2, :]), start=True, stop=True)
            last.then_inc(*S("bon_ps").one)

        def hp(e):
            return slice(64 * e, 64 * e + 64)

        def pairs(fn):
            for d in range(2):
                for m in range(4):
                    for e in range(2):
                        last = fn(d, m, e)
            return last

        def heads_of(d, fn):
            for m in range(4):
                for e in range(2):
                    last = fn(d, m, e)
            return last

        def col(m, half=0):
            return slice((half * 4 + m) * RC, (half * 4 + m + 1) * RC)

        def pe_solve(pe, seg, n):
            ch = (n, NRC - 1 - n)
            cs = [slice(c * RC, (c + 1) * RC) for c in ch]
            if n == 0:
                pe.wait_ge(*S("rw_prep").next("pe"))
            for d in range(2):
                if n > 0:
                    pe.wait_ge(*S("st_done").next("pe"))
                both = lambda d, m, e: ar[hp(e), d, m, ch[d], :, :].rearrange("p q l -> p (q l)")
                heads_of(d, lambda d, m, e: nc.tensor.matmul(
                    ps[hp(e), d, m * P:(m + 1) * P], bt[hp(e), d, m, cs[d]], both(d, m, e), start=True, stop=True))
                heads_of(d, lambda d, m, e: nc.tensor.matmul(
                    ps[hp(e), 2 + d, m * P:(m + 1) * P], kt[hp(e), d, m, cs[d]], both(d, m, e), start=True, stop=True))
                heads_of(d, lambda d, m, e: nc.tensor.matmul(
                    ps[hp(e), 4 + d, col(m)], ar[hp(e), d, m, ch[d], 0, :], bt[hp(e), d, m, cs[d]],
                    start=True, stop=True)).then_inc(*S("n_ps").one)
            for b_, src in ((6, bt), (7, kt)):
                pairs(lambda d, m, e: nc.tensor.matmul(ps[hp(e), b_, col(m, d)], src[hp(e), d, m, cs[d]],
                                                       ident[hp(e), hp(e)], start=True, stop=True)
                      ).then_inc(*S("tm_ps2").one)
            pe.wait_ge(*S("tm_sb").next("pe"))
            pairs(lambda d, m, e: nc.tensor.matmul(ps[hp(e), 6, col(m, d)], vv[hp(e), m, cs[d]],
                                                   ident[hp(e), hp(e)], start=True, stop=True)
                  ).then_inc(*S("tm_ps2").one)
            for lv in range(RLEV):
                for d in range(2):
                    pe.wait_ge(*S("lv_in").next("pe"))
                    heads_of(d, lambda d, m, e: nc.tensor.matmul(ps[hp(e), d, col(m)], nl[hp(e), lv % 2, d, m, :],
                                                                 tt[hp(e), d, 0, m, :], start=True, stop=True)
                             ).then_inc(*S("x_ps").one)
                for d in range(2):
                    pe.wait_ge(*S("x_sb").next("pe"))
                    if lv < RLEV - 1:
                        heads_of(d, lambda d, m, e: nc.tensor.matmul(
                            ps[hp(e), 2 + d, col(m)], tt[hp(e), d, 1, m, :], xs[hp(e), d, m, :],
                            start=True, stop=True))
                    heads_of(d, lambda d, m, e: nc.tensor.matmul(
                        ps[hp(e), 2 + d, col(m, 1)], xs[hp(e), d, m, :], tt[hp(e), d, 1, m, :],
                        start=True, stop=True)).then_inc(*S("t_ps").one)
            pe.wait_ge(*S("tm_sb").next("pe", 2))

            def rhs(d, m, e):
                nc.tensor.matmul(ps[hp(e), 4 + d, col(m)], ar[hp(e), d, m, ch[d], 0, :], st[hp(e), d, m, :],
                                 start=True, stop=False)
                return nc.tensor.matmul(ps[hp(e), 4 + d, col(m)], kr[hp(e), d, m, 0:RC], vtt[hp(e), d, m, :],
                                        start=False, stop=True)
            for d in range(2):
                heads_of(d, rhs).then_inc(*S("rh_ps").one)
            for d in range(2):
                pe.wait_ge(*S("tT_done").next("pe"))
                pe.wait_ge(*S("rh_sb").next("pe"))
                heads_of(d, lambda d, m, e: nc.tensor.matmul(ps[hp(e), 6 + d, col(m)], tt[hp(e), d, 1, m, :],
                                                             rh[hp(e), d, m, :], start=True, stop=True)
                         ).then_inc(*S("u_ps").one)

            def yy(d, m, e):
                o = ps[hp(e), d, col(m)]
                nc.tensor.matmul(o, st[hp(e), d, m, :], ar[hp(e), d, m, ch[d], 1, :], start=True, stop=False)
                nc.tensor.matmul(o, uu[hp(e), d, m, :], br[hp(e), d, m, RC:2 * RC], start=False, stop=False)
                return nc.tensor.matmul(o, vtt[hp(e), d, m, :], kr[hp(e), d, m, RC:2 * RC], start=False, stop=True)

            def ss(d, m, e):
                o = ps[hp(e), 2 + d, col(m)]
                nc.tensor.matmul(o, btt[hp(e), d, m, :], uu[hp(e), d, m, :], start=True, stop=False)
                return nc.tensor.matmul(o, ktt[hp(e), d, m, :], vtt[hp(e), d, m, :], start=False, stop=True)
            for d in range(2):
                pe.wait_ge(*S("u_sb").next("pe"))
                heads_of(d, yy).then_inc(*S("yr_ps").one)
                heads_of(d, ss).then_inc(*S("s_ps").one)

        def bank(i, half=0, n=4):
            return ps[:, i, half * 256:half * 256 + n * RC].rearrange("p (m l) -> p m l", l=RC)

        def act_solve(act, n):
            for dst, b_ in ((btt, 6), (ktt, 7), (vtt, 6)):
                act.wait_ge(*S("tm_ps2").next("act"))
                nc.scalar.activation(dst[:].rearrange("p d m l -> p (d m l)"), ps[:, b_, :], ACT.Copy
                                     ).then_inc(*S("tm_sb").one)
            for lv in range(RLEV):
                for d in range(2):
                    act.wait_ge(*S("x_ps").next("act"))
                    nc.scalar.activation(xs[:, d, :, :], bank(d), ACT.Copy).then_inc(*S("x_sb").one)
            for d in range(2):
                act.wait_ge(*S("rh_ps").next("act"))
                nc.scalar.activation(rh[:, d, :, :], bank(4 + d), ACT.Copy).then_inc(*S("rh_sb").one)
            for d in range(2):
                act.wait_ge(*S("u_ps").next("act"))
                nc.scalar.activation(uu[:, d, :, :], bank(6 + d), ACT.Copy).then_inc(*S("u_sb").one)

        def dve_solve(dve, link, seg, n):
            ch = (n, NRC - 1 - n)
            lvm = cc("lv").rearrange("p (s v d l) -> p s v d l", s=2, v=RLEV + 1, d=2)
            mx = cc("mx").rearrange("p (d l) -> p d l", d=2)
            e4 = bc(cc("i64").unsqueeze(1), [P, 4, RC])

            def mask_n(lv, d):
                return nc.vector.tensor_tensor(nl[:, lv % 2, d, :, :], br[:, d, :, 0:RC],
                                               bc(lvm[:, 1, lv + 1, d, :].unsqueeze(1), [P, 4, RC]), ALU.mult)
            for d in range(2):
                dve.wait_ge(*S("n_ps").next("dve"))
                b4 = lambda i: ps[:, i, :].rearrange("p (m l) -> p m l", m=4)
                link(nc.vector.tensor_tensor(br[:, d, :, :], b4(d), bc(mx[:, d, :].unsqueeze(1), [P, 4, P]), ALU.mult))
                link(nc.vector.tensor_tensor(tt[:, d, 0, :, :], bank(4 + d),
                                             bc(lvm[:, 0, 0, d, :].unsqueeze(1), [P, 4, RC]), ALU.mult))
                link(nc.vector.tensor_tensor(tt[:, d, 0, :, :], tt[:, d, 0, :, :], e4, ALU.add))
                link(nc.vector.tensor_tensor(tt[:, d, 1, :, :], br[:, d, :, 0:RC],
                                             bc(lvm[:, 1, 0, d, :].unsqueeze(1), [P, 4, RC]), ALU.mult))
                link(nc.vector.tensor_tensor(tt[:, d, 1, :, :], tt[:, d, 1, :, :], e4, ALU.add))
                link(nc.vector.tensor_tensor(kr[:, d, :, :], b4(2 + d), bc(mx[:, d, :].unsqueeze(1), [P, 4, P]),
                                             ALU.mult))
                link(mask_n(0, d))
                dve.sem_inc(S("lv_in").sem, 1)
            for lv in range(RLEV):
                if lv < RLEV - 1:
                    for d in range(2):
                        link(mask_n(lv + 1, d))
                for d in range(2):
                    dve.wait_ge(*S("t_ps").next("dve"))
                    if lv < RLEV - 1:
                        t2_ = tt[:, d, :, :, :].rearrange("p s m l -> p (s m) l")
                        link(nc.vector.tensor_tensor(t2_, t2_, bank(2 + d, 0, 8), ALU.add))
                        dve.sem_inc(S("lv_in").sem, 1)
                    else:
                        nc.vector.tensor_tensor(tt[:, d, 1, :, :], tt[:, d, 1, :, :], bank(2 + d, 1), ALU.add
                                                ).then_inc(*S("tT_done").one)
            for d in range(2):
                dve.wait_ge(*S("yr_ps").next("dve"))
                c = ch[d]
                if d == 0:
                    dst = o0[:, 0:4, seg * SEG + c * RC:seg * SEG + (c + 1) * RC]
                else:
                    dst = yb[:, :, c * RC:(c + 1) * RC]
                link(nc.vector.tensor_copy(dst, bank(d)))
                dve.wait_ge(*S("s_ps").next("dve"))
                link(nc.vector.tensor_tensor(st[:, d, :, :], st[:, d, :, :], bank(2 + d), ALU.add))
                link(nc.vector.tensor_tensor(st[:, d, :, :], st[:, d, :, :],
                                             bc(dls[:, d, :, ch[d]:ch[d] + 1], [P, 4, RC]), ALU.mult))
                dve.sem_inc(S("st_done").sem, 1)

        def dve_rwout(dve, link, seg):
            y = o0[:, 0:4, seg_cols(seg)]
            link(nc.vector.tensor_tensor(yb[:], yb[:], y, ALU.add))
            dve.sem_inc(S("gn_in").sem, 1)
            dve.wait_ge(*S("gn_mu").next("dve"))
            for b_ in range(2):
                v = fl(yb[:, 2 * b_:2 * b_ + 2, :])
                link(nc.vector.scalar_tensor_tensor(v, ps[:, b_, :], -1.0 / 64, v, ALU.mult, ALU.add))
            link(nc.vector.tensor_tensor(ee[:], yb[:], yb[:], ALU.mult))
            dve.sem_inc(S("gn_sq").sem, 1)
            dve.wait_ge(*S("gn_var").next("dve"))
            for b_ in range(2):
                link(nc.vector.tensor_scalar(fl(ee[:, 2 * b_:2 * b_ + 2, :]), ps[:, b_, :], 1.0 / 64, 64e-5,
                                             ALU.mult, ALU.add))
            dve.sem_inc(S("gn_ve").sem, 1)
            dve.wait_ge(*S("gn_rt").next("dve"))
            link(nc.vector.reciprocal(ee[:], ee[:]))
            link(nc.vector.tensor_tensor(yb[:], yb[:], ee[:], ALU.mult))
            for m in range(4):
                link(nc.vector.tensor_scalar(yb[:, m, :], yb[:, m, :], pc("gnw", m, 1), pc("gnb", m, 1),
                                             ALU.mult, ALU.add))
            link(nc.vector.tensor_tensor(yb[:], yb[:], bon[:], ALU.add))
            dve.wait_ge(*S("gate_ps").next("dve"))
            for m in range(4):
                link(nc.vector.tensor_tensor(y[:, m, :], yb[:, m, :],
                                             ps[:, 2 + m // 2, (m % 2) * SEG:(m % 2 + 1) * SEG], ALU.mult))

        def pe_rwout(pe, seg):
            pe.wait_ge(*S("st_done").next("pe", 2))
            for m in range(4):
                last = nc.tensor.matmul(ps[:, 2 + m // 2, (m % 2) * SEG:(m % 2 + 1) * SEG], gup[:, m * P:(m + 1) * P],
                                        lg[:], start=True, stop=True)
            last.then_inc(*S("gate_ps").one)
            for a, src, b in (("gn_in", yb, "gn_mu"), ("gn_sq", ee, "gn_var")):
                pe.wait_ge(*S(a).next("pe"))
                for b_ in range(2):
                    last = nc.tensor.matmul(ps[:, b_, :], bones[:], fl(src[:, 2 * b_:2 * b_ + 2, :]),
                                            start=True, stop=True)
                last.then_inc(*S(b).one)

        def act_rwout(act, seg):
            act.wait_ge(*S("gn_ve").next("act"))
            nc.scalar.activation(ee[:], ee[:], ACT.Sqrt).then_inc(*S("gn_rt").one)

        def act_osplit(act, src, cols):
            act.wait_ge(*S("o_ready").next("act"))
            nc.scalar.activation(a_hi[:, :, cols], src, ACT.Copy).then_inc(*S("ohi").one)

        def dve_osplit(dve, src, cols):
            dve.sem_inc(S("o_ready").sem, 1)
            dve.wait_ge(*S("ohi").next("dve"))
            nc.vector.tensor_tensor(a_lo[:, :, cols], src, a_hi[:, :, cols].bitcast(F32),
                                    ALU.subtract).then_inc(*S("alo_ready").one)
            dve.wait_ge(*S("alo_ready").next("dve"))

        NH = 16
        qT, kT, vT, bia, sS, pP, pT, mxv, nmx, sm, rc_, oA, _r = lay(arena + 8192, [
            ("qT", [P, 8, SEG]), ("kT", [P, 8, T2]), ("vT", [P, 4, D]), ("bia", [P, NH, 512]),
            ("sS", [P, 2, 512]), ("pP", [P, 2, 512]), ("pT", [P, 2, 512]), ("mxv", [P, 32]), ("nmx", [P, 32]),
            ("sm", [P, 32]), ("rc_", [P, 32]), ("oA", [P, 8, SEG])])
        assert _r <= END - 64

        def pool_bias(pool):
            pool.wait_ge(*S("arena_free").next("pool"))
            pool.dma_start(bia[:], io["bias"]).then_inc(*S("bias").dma)

        def pe_qkv(pe):
            pe.wait_ge(*S("alo_ready").next("pe", 2))
            pe_gemm(pe, BASE["qkv"], 8, "act", None, lambda b: [(ps[:, b, 0:SEG], True, a_cols([LAT]))])
            pe_gemm(pe, BASE["qkv"] + 8, 8, "act", None, lambda b: [(ps[:, b, :], True, a_cols([CTX, LAT]))])
            pe_gemm(pe, BASE["qkv"] + 16, 8, "act", None, lambda b: tok_major(b, 0, 4))

        def tok_major(b, first, n):
            def group(tt):
                c = slice((first + tt) * P, (first + tt + 1) * P)
                return (ps[:, b, tt * P:(tt + 1) * P], False, lambda k: (a_hi[:, k, c], a_lo[:, k, c]))
            return [group(tt) for tt in range(n)]

        def act_copies(act, base, runs):
            first = 0
            for n, dst, src in runs:
                def after(t, slot, dst=dst, src=src, first=first):
                    act.wait_ge(tile_used.sem, used(base, t))
                    nc.scalar.activation(dst(t - first), src(5 + slot), ACT.Copy).then_inc(act_evac.sem, 1)
                run_tiles(act, "act", base, n, t0=first, after=after)
                first += n

        def flat1(ap):
            return ap.rearrange("p o t -> p (o t)")

        def dyn(t, n):
            return slice(t * n, t * n + n) if isinstance(t, int) else bass.ds(t * n, n)

        def act_qkv(act):
            act_copies(act, BASE["qkv"], [
                (8, lambda t: flat1(qT[:, one(t), :]), lambda b: ps[:, b, 0:SEG]),
                (8, lambda t: flat1(kT[:, one(t), :]), lambda b: ps[:, b, :]),
                (8, lambda t: vT[:, :, dyn(t, P)], lambda b: ps[:, b, :].rearrange("p (a c) -> p a c", a=4))])

        def sbank(u):
            return (0, 1, 6)[u % 3]

        def pe_attn(pe, evac0):
            pe.wait_ge(act_evac.sem, evac0)

            def scores(u):
                h, qt = u // 2, u % 2
                if u >= 3:
                    pe.wait_ge(*S("sc_read").next("pe"))
                nc.tensor.matmul(ps[:, sbank(u), :], qT[hp(h % 2), h // 2, qt * P:(qt + 1) * P],
                                 kT[hp(h % 2), h // 2, :], start=True, stop=True).then_inc(*S("sc_ps").one)

            def transposes(u):
                pe.wait_ge(*S("p_ready").next("pe"))
                for kt_ in range(4):
                    last = nc.tensor.transpose(ps[:, 2 + u % 2, kt_ * P:(kt_ + 1) * P],
                                               pP[:, u % 2, kt_ * P:(kt_ + 1) * P], ident[:])
                last.then_inc(*S("pT_ps").one)

            def values(u):
                h, qt = u // 2, u % 2
                pe.wait_ge(*S("pT_sb").next("pe"))
                if u % 4 == 0 and u >= 8:
                    pe.wait_ge(*S("at_sb").next("pe"))
                m = h // 2
                for kt_ in range(4):
                    last = nc.tensor.matmul(ps[hp(h % 2), 4 + m % 2, qt * P:(qt + 1) * P],
                                            vT[:, kt_, h * 64:(h + 1) * 64], pT[:, u % 2, kt_ * P:(kt_ + 1) * P],
                                            start=(kt_ == 0), stop=(kt_ == 3))
                last.then_inc(*S("at_ps").one)
            scores(0)
            scores(1)
            for u in range(2 * NH):
                if u + 2 < 2 * NH:
                    scores(u + 2)
                transposes(u)
                if u >= 1:
                    values(u - 1)
            values(2 * NH - 1)
            pe.wait_ge(*S("sc_read").next("pe", 3))
            pe.wait_ge(*S("at_sb").next("pe", 2))

        def dve_attn(dve, link):
            dve.wait_ge(S("bias").sem, 16)

            def soft(u):
                h, qt = u // 2, u % 2
                dve.wait_ge(*S("sc_ps").next("dve"))
                link(nc.vector.tensor_scalar(sS[:, u % 2, 0:SEG], ps[:, sbank(u), 0:SEG], 0.125, None, ALU.mult))
                nc.vector.scalar_tensor_tensor(sS[:, u % 2, SEG:T2], ps[:, sbank(u), SEG:T2], 0.125,
                                               bia[:, h, qt * 256:(qt + 1) * 256], ALU.mult, ALU.add
                                               ).then_inc(*S("sc_read").one)
                dve.wait_ge(*S("sc_read").next("dve"))
                link(nc.vector.tensor_reduce(mxv[:, u:u + 1], sS[:, u % 2, :], AX.X, ALU.max))
                nc.vector.tensor_scalar(nmx[:, u:u + 1], mxv[:, u:u + 1], -1.0, None, ALU.mult
                                        ).then_inc(*S("nmx").one)

            def norm(u):
                dve.wait_ge(*S("exp_done").next("dve"))
                link(nc.vector.reciprocal(rc_[:, u:u + 1], sm[:, u:u + 1]))
                nc.vector.tensor_scalar(pP[:, u % 2, :], pP[:, u % 2, :], rc_[:, u:u + 1], None, ALU.mult
                                        ).then_inc(*S("p_ready").one)

            def out(m):
                dve.wait_ge(*S("at_ps").next("dve", 4))
                nc.vector.tensor_copy(oA[:, m, :], ps[:, 4 + m % 2, 0:SEG]).then_inc(*S("at_sb").one)
            soft(0)
            for u in range(2 * NH):
                if u + 1 < 2 * NH:
                    soft(u + 1)
                norm(u)
                if u % 4 == 1 and u >= 5:
                    out(u // 4 - 1)
            out(KT - 1)
            dve.wait_ge(*S("at_sb").next("dve", 8))

        def act_attn(act):
            def ex(u):
                act.wait_ge(*S("nmx").next("act"))
                nc.scalar.activation(pP[:, u % 2, :], sS[:, u % 2, :], ACT.Exp, bias=nmx[:, u:u + 1],
                                     accum_out=sm[:, u:u + 1]).then_inc(*S("exp_done").one)

            def cp(u):
                act.wait_ge(*S("pT_ps").next("act"))
                if u >= 2:
                    act.wait_ge(*S("at_ps").next("act"))
                nc.scalar.activation(pT[:, u % 2, :], ps[:, 2 + u % 2, :], ACT.Copy).then_inc(*S("pT_sb").one)
            ex(0)
            for u in range(2 * NH):
                if u + 1 < 2 * NH:
                    ex(u + 1)
                cp(u)

        gate, lgt, t1, t2, oh1, oh2, wv, gr, _r = lay(arena + 8192, [
            ("gate", [P, NE, SEG]), ("lgt", [P, 2, NE]), ("t1", [P, 2, NE]), ("t2", [P, 2, NE]),
            ("oh1", [P, 2, NE]), ("oh2", [P, 2, NE]), ("wv", [P, 8]), ("gr", [P, SEG])])

        def pe_router(pe):
            for tt_ in range(2):
                for k in range(KT):
                    last = nc.tensor.matmul(ps[:, 5, tt_ * NE:(tt_ + 1) * NE], normw[:, k, tt_ * P:(tt_ + 1) * P],
                                            pc("rw", k * NE, NE), start=(k == 0), stop=(k == KT - 1))
            last.then_inc(*S("lg_ps").one)
            pe.wait_ge(*S("gates").next("pe"))
            for tt_ in range(2):
                last = nc.tensor.transpose(ps[0:NE, 6, tt_ * P:(tt_ + 1) * P], lgt[:, tt_, :], ident[:])
            last.then_inc(*S("gr_ps").one)
            pe.wait_ge(*S("gr_sb").next("pe"))
            for e in range(NE):
                last = nc.tensor.matmul(ps[:, e // 2, (e % 2) * SEG:(e % 2 + 1) * SEG],
                                        ident[0:NE, e:e + 1].broadcast_to([NE, P]), gr[0:NE, :], start=True, stop=True)
            last.then_inc(*S("gate_bc").one)
            pe.wait_ge(*S("gate_sb").next("pe"))

        def dve_router(dve, link):
            dve.wait_ge(*S("lg_ps").next("dve"))
            dve.wait_ge(S("conb").sem, 16)
            iota = conb[:, BCOL["iota"][0]:BCOL["iota"][1]].rearrange("p (a e) -> p a e", a=2)
            col = lambda i: wv[:, 2 * i:2 * i + 2].unsqueeze(2)
            b8 = lambda i: bc(col(i), [P, 2, NE])
            link(nc.vector.tensor_tensor(lgt[:], ps[:, 5, 0:16].rearrange("p (a e) -> p a e", a=2),
                                         bc(pc("rb").unsqueeze(1), [P, 2, NE]), ALU.add))
            for q, oh in enumerate((oh1, oh2)):
                link(nc.vector.tensor_reduce(wv[:, 2 * q:2 * q + 2], lgt[:], AX.X, ALU.max))
                link(nc.vector.tensor_tensor(t1[:], lgt[:], b8(q), ALU.is_equal))
                link(nc.vector.scalar_tensor_tensor(t1[:], t1[:], -100.0, iota, ALU.mult, ALU.add))
                link(nc.vector.tensor_reduce(wv[:, 4:6], t1[:], AX.X, ALU.min))
                link(nc.vector.tensor_tensor(oh[:], t1[:], b8(2), ALU.is_equal))
                if q == 0:
                    link(nc.vector.scalar_tensor_tensor(lgt[:], oh[:], -BIG, lgt[:], ALU.mult, ALU.add))
            link(nc.vector.tensor_tensor(wv[:, 4:6], wv[:, 2:4], wv[:, 0:2], ALU.subtract))
            dve.sem_inc(S("r_dif").sem, 1)
            dve.wait_ge(*S("r_exp").next("dve"))
            link(nc.vector.tensor_scalar(wv[:, 0:2], wv[:, 4:6], 1.0, None, ALU.add))
            link(nc.vector.reciprocal(wv[:, 0:2], wv[:, 0:2]))
            link(nc.vector.tensor_tensor(wv[:, 2:4], wv[:, 4:6], wv[:, 0:2], ALU.mult))
            link(nc.vector.tensor_tensor(oh1[:], oh1[:], b8(0), ALU.mult))
            link(nc.vector.tensor_tensor(oh2[:], oh2[:], b8(1), ALU.mult))
            nc.vector.tensor_tensor(lgt[:], oh1[:], oh2[:], ALU.add).then_inc(*S("gates").one)
            dve.wait_ge(*S("gr_ps").next("dve"))
            nc.vector.tensor_copy(gr[0:NE, :], ps[0:NE, 6, 0:SEG]).then_inc(*S("gr_sb").one)
            dve.wait_ge(*S("gate_bc").next("dve"))
            for e2 in range(4):
                last = nc.vector.tensor_copy(fl(gate[:, 2 * e2:2 * e2 + 2, :]), ps[:, e2, :])
                if e2 < 3:
                    link(last)
            last.then_inc(*S("gate_sb").one)
            dve.wait_ge(*S("gate_sb").next("dve"))

        def act_router(act):
            act.wait_ge(*S("r_dif").next("act"))
            nc.scalar.activation(wv[:, 4:6], wv[:, 4:6], ACT.Exp).then_inc(*S("r_exp").one)

        conb = sb("conb", [P, NCONB], at=END - 64 - (NCONB * 4 + 63) // 64 * 64)
        z2, v2, vpad, o2, sg2, yc, _r = lay(arena + 8192, [
            ("z2", [P, 18, SEG]), ("v2", [P, 2, 768]), ("vpad", [P, 2, SEG + CONV2 - 1]), ("o2", [P, KT, SEG]),
            ("sg2", [P, 2, SEG]), ("yc", [P, 2, SEG])])
        zs, ex_, sp_, wv2, rt_, yr, sg3, _r = lay(_r, [
            ("zs", [P, 2, 384]), ("ex_", [P, 2, 384]), ("sp_", [P, 2, 384]), ("wv2", [P, 2, 384]),
            ("rt_", [P, 4, SEG]), ("yr", [P, 2, SEG]), ("sg3", [P, 2, SEG])])
        assert _r <= END - 64 - (NCONB * 4 + 63) // 64 * 64, _r

        def cb(name):
            return conb[:, BCOL[name][0]:BCOL[name][1]]

        def pool_conb(pool):
            pool.wait_ge(*S("arena_free2").next("pool"))
            pool.dma_start(conb[:], io["constsb"]).then_inc(*S("conb").dma)

        def pe_in2(pe, l):
            pe.wait_ge(*S("alo_ready").next("pe"))
            pe_gemm(pe, BASE[f"in_{l}"], 18, "act", None, lambda b: [(ps[:, b, 0:SEG], True, a_cols([LAT]))])
            pe_gemm(pe, BASE[f"in_{l}"] + 18, 6, "act", None, lambda b: tok_major(b, 2, 2))

        def act_in2(act, l):
            act_copies(act, BASE[f"in_{l}"], [
                (18, lambda t: flat1(z2[:, one(t), :]), lambda b: ps[:, b, 0:SEG]),
                (6, lambda t: v2[:, :, dyn(t, P)], lambda b: ps[:, b, 0:256].rearrange("p (a c) -> p a c", a=2))])

        def conv2_taps(link, l, first, n):
            for j in range(first, min(first + n, 2 * CONV2)):
                tap, i = j // 2, j % 2
                x, w = vpad[:, i, tap:tap + SEG], pc("c2w", l * 62 + i * 31 + tap, 1)
                if tap == 0:
                    link(nc.vector.tensor_scalar(yc[:, i, :], x, w, pc("c2b", 2 * l + i, 1), ALU.mult, ALU.add))
                else:
                    link(nc.vector.scalar_tensor_tensor(yc[:, i, :], x, w, yc[:, i, :], ALU.mult, ALU.add))

        def dve_conv2_in(dve, link, evac0):
            dve.wait_ge(act_evac.sem, evac0)
            link(nc.vector.memset(vpad[:, :, 0:CONV2 - 1], 0.0))
            dve.wait_ge(*S("c2_sig").next("dve"))
            link(nc.vector.tensor_tensor(vpad[:, :, CONV2 - 1:], z2[:, 0:2, :], sg2[:], ALU.mult))

        def dve_conv2(dve, link, l):
            dve.sem_inc(S("c2_y").sem, 1)
            dve.wait_ge(*S("c2_mu").next("dve"))
            for i in range(2):
                link(nc.vector.scalar_tensor_tensor(yc[:, i, :], ps[:, 4, 0:SEG], -1.0 / 256, yc[:, i, :],
                                                    ALU.mult, ALU.add))
            link(nc.vector.tensor_tensor(sg2[:], yc[:], yc[:], ALU.mult))
            dve.sem_inc(S("c2_sq").sem, 1)
            dve.wait_ge(*S("c2_var").next("dve"))
            link(nc.vector.tensor_scalar(rs[:, 0:SEG], ps[:, 4, 0:SEG], 1.0 / 256, EPS, ALU.mult, ALU.add))
            dve.sem_inc(S("c2_ve").sem, 1)
            dve.wait_ge(*S("c2_rt").next("dve"))
            link(nc.vector.reciprocal(rs[:, 0:SEG], rs[:, 0:SEG]))
            link(nc.vector.tensor_tensor(yc[:], yc[:], bc(rs[:, 0:SEG].unsqueeze(1), [P, 2, SEG]), ALU.mult))
            for i in range(2):
                link(nc.vector.tensor_scalar(yc[:, i, :], yc[:, i, :], pc("c2g", 2 * l + i, 1),
                                             pc("c2bb", 2 * l + i, 1), ALU.mult, ALU.add))
            dve.sem_inc(S("c2_ln").sem, 1)

        def act_conv2_in(act, evac0):
            act.wait_ge(act_evac.sem, evac0)
            nc.scalar.activation(sg2[:], z2[:, 2:4, :], ACT.Sigmoid).then_inc(*S("c2_sig").one)

        def act_conv2(act):
            act.wait_ge(*S("c2_ve").next("act"))
            nc.scalar.activation(rs[:, 0:SEG], rs[:, 0:SEG], ACT.Sqrt).then_inc(*S("c2_rt").one)
            act.wait_ge(*S("c2_ln").next("act"))
            nc.scalar.activation(o2[:, 0:2, :], yc[:], ACT.Silu).then_inc(*S("o2_conv").one)

        def pe_conv2(pe):
            for a, src, b in (("c2_y", yc, "c2_mu"), ("c2_sq", sg2, "c2_var")):
                pe.wait_ge(*S(a).next("pe"))
                for i in range(2):
                    last = nc.tensor.matmul(ps[:, 4, 0:SEG], ones[:], src[:, i, :], start=(i == 0), stop=(i == 1))
                last.then_inc(*S(b).one)

        def pe_stick(pe, evac0):
            pe.wait_ge(act_evac.sem, evac0)

            def scores(h):
                m, e, b_ = h // 2, h % 2, h % 2
                q, k = z2[hp(e), 4 + m, :], z2[hp(e), 8 + m, :]
                nc.tensor.matmul(ps[:, b_, 0:256], k[:, 0:P], q, start=True, stop=True)
                nc.tensor.matmul(ps[:, b_, 256:384], k[:, P:SEG], q[:, P:SEG], start=True, stop=True
                                 ).then_inc(*S("sk_ps").one)

            def sums(h):
                b_ = h % 2
                pe.wait_ge(*S("sk_sp").next("pe"))
                nc.tensor.matmul(ps[:, 2 + b_, 0:256], cb("tri"), sp_[:, b_, 0:256], start=True, stop=False,
                                 skip_group_check=True)
                nc.tensor.matmul(ps[:, 2 + b_, 128:256], ones[:], sp_[:, b_, 256:384], start=False, stop=True,
                                 skip_group_check=True)
                nc.tensor.matmul(ps[:, 2 + b_, 256:384], cb("tri"), sp_[:, b_, 256:384], start=True, stop=True,
                                 skip_group_check=True).then_inc(*S("sk_rc").one)

            def outputs(h):
                m, e, b_ = h // 2, h % 2, h % 2
                pe.wait_ge(*S("sk_w").next("pe"))
                if e == 0 and m >= 2:
                    pe.wait_ge(*S("sk_o").next("pe"))
                nc.tensor.matmul(ps[hp(e), 5 + m % 2, 0:256], v2[:, 0, h * 64:(h + 1) * 64], wv2[:, b_, 0:256],
                                 start=True, stop=False, skip_group_check=True)
                nc.tensor.matmul(ps[hp(e), 5 + m % 2, 128:256], v2[:, 1, h * 64:(h + 1) * 64], wv2[:, b_, 256:384],
                                 start=False, stop=True, skip_group_check=True).then_inc(*S("sk_y").one)
            scores(0)
            for h in range(8):
                if h < 7:
                    scores(h + 1)
                sums(h)
                if h >= 1:
                    outputs(h - 1)
            outputs(7)

        def act_stick(act):
            def softplus(h):
                b_ = h % 2
                act.wait_ge(*S("sk_ps").next("act"))
                if h >= 2:
                    act.wait_ge(*S("sk_t1").next("act"))
                nc.scalar.activation(zs[:, b_, :], ps[:, b_, 0:384], ACT.Copy, scale=0.125).then_inc(*S("sk_z").one)
                act.wait_ge(*S("sk_z").next("act"))
                nc.scalar.activation(ex_[:, b_, :], zs[:, b_, :], ACT.Abs).then_inc(*S("sk_c").one)
                act.wait_ge(*S("sk_c").next("act"))
                nc.scalar.activation(ex_[:, b_, :], ex_[:, b_, :], ACT.Exp, scale=-1.0).then_inc(*S("sk_c").one)
                act.wait_ge(*S("sk_c").next("act"))
                nc.scalar.activation(ex_[:, b_, :], ex_[:, b_, :], ACT.Ln, bias=1.0).then_inc(*S("sk_l").one)

            def weights(h):
                act.wait_ge(*S("sk_t").next("act"))
                if h >= 2:
                    act.wait_ge(*S("sk_y").next("act"))
                nc.scalar.activation(wv2[:, h % 2, :], ex_[:, h % 2, :], ACT.Exp).then_inc(*S("sk_e").one)
            softplus(0)
            for h in range(8):
                if h < 7:
                    softplus(h + 1)
                weights(h)
            act.wait_ge(*S("sk_t1").next("act", 2))
            act.wait_ge(*S("sk_y").next("act", 2))

        def dve_stick(dve, link, l):
            def masked(t, h):
                a, b = t[:, h % 2, 0:P], t[:, h % 2, 256:384]
                link(nc.vector.tensor_tensor(a, a, cb("smask"), ALU.mult))
                return nc.vector.tensor_tensor(b, b, cb("smask"), ALU.mult)

            def softplus(h):
                b_ = h % 2
                dve.wait_ge(*S("sk_z").next("dve"))
                link(nc.vector.tensor_scalar(sp_[:, b_, :], zs[:, b_, :], 0.0, None, ALU.max))
                dve.wait_ge(*S("sk_l").next("dve"))
                link(nc.vector.tensor_tensor(sp_[:, b_, :], sp_[:, b_, :], ex_[:, b_, :], ALU.add))
                masked(sp_, h).then_inc(*S("sk_sp").one)

            def logs(h):
                b_ = h % 2
                dve.wait_ge(*S("sk_rc").next("dve"))
                nc.vector.scalar_tensor_tensor(ex_[:, b_, :], ps[:, 2 + b_, 0:384], -1.0, zs[:, b_, :],
                                               ALU.mult, ALU.add).then_inc(*S("sk_t1").one)
                dve.wait_ge(*S("sk_t1").next("dve"))
                nc.vector.tensor_scalar(ex_[:, b_, :], ex_[:, b_, :], 0.0, None, ALU.min).then_inc(*S("sk_t").one)

            def out(m):
                dve.wait_ge(*S("sk_y").next("dve", 2))
                nc.vector.tensor_copy(o2[:, 2 + m, :], ps[:, 5 + m % 2, 0:SEG]).then_inc(*S("sk_o").one)
            softplus(0)
            for h in range(8):
                conv2_taps(link, l, 8 * h, 8)
                logs(h)
                if h < 7:
                    softplus(h + 1)
                dve.wait_ge(*S("sk_e").next("dve"))
                masked(wv2, h).then_inc(*S("sk_w").one)
                if h % 2 == 0 and h >= 2:
                    out(h // 2 - 1)
            out(3)
            dve.wait_ge(*S("sk_o").next("dve", 4))

        def pe_ret(pe):
            pe.wait_ge(*S("sk_o").next("pe", 2))
            for i in range(4):
                last = nc.tensor.matmul(ps[:, i // 2, (i % 2) * SEG:(i % 2 + 1) * SEG], cb("rot"), z2[:, 12 + i, :],
                                        start=True, stop=True)
            last.then_inc(*S("rt_ps").one)
            pe.wait_ge(*S("rt_sb").next("pe"))
            for h in range(4):
                m, e, b_ = h // 2, h % 2, 2 + h % 2
                q, k = rt_[hp(e), m, :], rt_[hp(e), 2 + m, :]
                nc.tensor.matmul(ps[:, b_, 0:256], k[:, 0:P], q, start=True, stop=True)
                nc.tensor.matmul(ps[:, b_, 256:384], k[:, P:SEG], q[:, P:SEG], start=True, stop=True
                                 ).then_inc(*S("re_ps").one)
                pe.wait_ge(*S("re_sc").next("pe"))
                out = ps[hp(e), 5 + m, 0:256]
                nc.tensor.matmul(out, v2[:, 0, 512 + h * 64:512 + (h + 1) * 64], sp_[:, h % 2, 0:256],
                                 start=True, stop=False, skip_group_check=True)
                nc.tensor.matmul(ps[hp(e), 5 + m, 128:256], v2[:, 1, 512 + h * 64:512 + (h + 1) * 64],
                                 sp_[:, h % 2, 256:384], start=False, stop=True, skip_group_check=True
                                 ).then_inc(*S("re_y").one)
            for a, src, b in (("re_in", yr, "re_mu"), ("re_sq", sg2, "re_var")):
                pe.wait_ge(*S(a).next("pe"))
                nc.tensor.matmul(ps[:, 0, :], bones[:], fl(src[:]), start=True, stop=True).then_inc(*S(b).one)

        def dve_ret(dve, link, l):
            dve.wait_ge(*S("rt_ps").next("dve"))
            sn = bc(cb("sin").unsqueeze(1), [P, 2, SEG])
            for b_ in range(2):
                link(nc.vector.tensor_tensor(rt_[:, 2 * b_:2 * b_ + 2, :], ps[:, b_, :].rearrange("p (a t) -> p a t", a=2),
                                             sn, ALU.mult))
            link(nc.vector.tensor_tensor(z2[:, 12:16, :], z2[:, 12:16, :], bc(cb("cos").unsqueeze(1), [P, 4, SEG]), ALU.mult))
            nc.vector.tensor_tensor(rt_[:], rt_[:], z2[:, 12:16, :], ALU.add).then_inc(*S("rt_sb").one)
            for h in range(4):
                dve.wait_ge(*S("re_ps").next("dve"))
                if h >= 2:
                    dve.wait_ge(*S("re_y").next("dve"))
                nc.vector.tensor_tensor(sp_[:, h % 2, :], ps[:, 2 + h % 2, 0:384],
                                        cb("dret")[:, h * 384:(h + 1) * 384], ALU.mult).then_inc(*S("re_sc").one)
            dve.wait_ge(*S("re_y").next("dve", 2))
            dve.wait_ge(*S("c2_lnd").next("dve"))
            for m in range(2):
                link(nc.vector.tensor_copy(yr[:, m, :], ps[:, 5 + m, 0:SEG]))
            dve.sem_inc(S("re_in").sem, 1)
            dve.wait_ge(*S("re_mu").next("dve"))
            link(nc.vector.scalar_tensor_tensor(fl(yr[:]), ps[:, 0, :], -1.0 / 64, fl(yr[:]), ALU.mult, ALU.add))
            link(nc.vector.tensor_tensor(sg2[:], yr[:], yr[:], ALU.mult))
            dve.sem_inc(S("re_sq").sem, 1)
            dve.wait_ge(*S("re_var").next("dve"))
            link(nc.vector.tensor_scalar(fl(sg2[:]), ps[:, 0, :], 1.0 / 64, EPS, ALU.mult, ALU.add))
            dve.sem_inc(S("re_ve").sem, 1)
            dve.wait_ge(*S("re_rt").next("dve"))
            link(nc.vector.reciprocal(sg2[:], sg2[:]))
            link(nc.vector.tensor_tensor(yr[:], yr[:], sg2[:], ALU.mult))
            for m in range(2):
                link(nc.vector.scalar_tensor_tensor(o2[:, 6 + m, :], yr[:, m, :], pc("rtg", 2 * l + m, 1),
                                                    sg3[:, m, :], ALU.mult, ALU.mult))
            dve.wait_ge(*S("o2_conv").next("dve"))

        def act_ret(act):
            nc.scalar.activation(sg3[:], z2[:, 16:18, :], ACT.Silu).then_inc(*S("c2_lnd").one)
            act.wait_ge(*S("re_ve").next("act"))
            nc.scalar.activation(sg2[:], sg2[:], ACT.Sqrt).then_inc(*S("re_rt").one)

        E_ADA = RING
        E_WIN = E_ADA + 27
        E_QKV = E_WIN + 24
        E_IN = [E_QKV + 24, E_QKV + 48]

        @block.sync
        def _(sp):
            load_list(sp)
            sp_stream(sp)
            sp.wait_ge(*S("out_ready").next("sp"))
            sp.dma_start(io["out"], hT[:, :, seg_cols(LAT)]).then_inc(*S("stored").dma)
            sp.wait_ge(*S("stored").next("sp", 16))

        @block.gpsimd
        def _(pool):
            pool.wait_ge(*S("mb_done").next("pool"))
            pool.dma_start(lora[:], io["lora"]).then_inc(*S("lora").dma)
            pool.dma_start(gup[:], io["gup"]).then_inc(*S("lora").dma)
            pool_bias(pool)
            pool_conb(pool)

        @block.tensor
        def _(pe):
            pe.sem_inc(tile_used.sem, RING)
            pe.wait_ge(S("par").sem, NLOAD)
            pe_ada(pe)
            for s in (CTX, LAT):
                pe_norm(pe)
            pe.wait_ge(*S("alo_ready").next("pe", 2))
            pe_gemm(pe, BASE["w_in"], 27, "act", None, lambda b: [(ps[:, b, :], True, a_cols([CTX, LAT]))])
            pe_dt(pe)
            pe_states(pe)
            pe_ssd(pe)
            pe_mbout(pe)
            for s in (CTX, LAT):
                pe_rwprep(pe, s)
                for n in range(NRC):
                    pe_solve(pe, s, n)
                pe_rwout(pe, s)
            pe.wait_ge(*S("alo_ready").next("pe"))
            pe_gemm(pe, BASE["w_out"], 8, "dve", None, lambda b: [(ps[:, b, :], True, a_cols([CTX, LAT]))])
            for s, nm in ((CTX, "ffn_ctx"), (LAT, "ffn_lat")):
                pe_norm(pe)
                pe.wait_ge(*S("alo_ready").next("pe"))
                pe_ffn(pe, BASE[nm], s, FT)
            for s in (CTX, LAT):
                pe_norm(pe)
            pe_qkv(pe)
            pe_attn(pe, E_QKV)
            pe.wait_ge(*S("alo_ready").next("pe"))
            pe_gemm(pe, BASE["na_out"], 8, "dve", None, lambda b: [(ps[:, b, 0:SEG], True, a_cols([LAT]))])
            pe_norm(pe)
            pe.wait_ge(*S("alo_ready").next("pe"))
            pe_router(pe)
            pe_ffn(pe, BASE["moe"], LAT, FT * NE)
            pe_norm(pe)
            for l in range(2):
                pe_norm(pe)
                pe.wait_ge(*S("alo_ready").next("pe"))
                pe_ffn(pe, BASE[f"f1_{l}"], LAT, FT)
                pe_norm(pe)
                pe_in2(pe, l)
                pe_stick(pe, E_IN[l])
                pe_conv2(pe)
                pe_ret(pe)
                pe.wait_ge(*S("alo_ready").next("pe"))
                pe_gemm(pe, BASE[f"out_{l}"], 8, "dve", None, lambda b: [(ps[:, b, 0:SEG], True, a_cols([LAT]))])
                pe_norm(pe)
                pe.wait_ge(*S("alo_ready").next("pe"))
                pe_ffn(pe, BASE[f"f2_{l}"], LAT, FT)
            pe_norm(pe)

        @block.scalar
        def _(act):
            act.sem_inc(act_evac.sem, RING)
            for n in range(LEAD):
                act_split(act, n, 0, n)
            act_ada(act)
            for s in (CTX, LAT):
                act_norm(act, s, normw)
            act_win(act)
            act_conv(act)
            act_dt(act)
            act_ssd(act)
            act_mbout(act)
            for s in (CTX, LAT):
                act_rwprep(act, s)
                for n in range(NRC):
                    act_solve(act, n)
                act_rwout(act, s)
            act_osplit(act, o0[:], slice(0, T2))
            run_tiles(act, "act", BASE["w_out"], 8)
            for s, nm in ((CTX, "ffn_ctx"), (LAT, "ffn_lat")):
                act_norm(act, s, normw)
                act_ffn(act, BASE[nm], FT)
            for s in (CTX, LAT):
                act_norm(act, s, normw)
            act_qkv(act)
            act_attn(act)
            act_osplit(act, oA[:], seg_cols(LAT))
            run_tiles(act, "act", BASE["na_out"], 8)
            act_norm(act, LAT, normw)
            act_router(act)
            act_ffn(act, BASE["moe"], FT * NE)
            act_norm(act, LAT, normw, to_a=False)
            for l in range(2):
                act_norm(act, LAT, normw)
                act_ffn(act, BASE[f"f1_{l}"], FT)
                act_norm(act, LAT, normw)
                act_in2(act, l)
                act_conv2_in(act, E_IN[l])
                act_stick(act)
                act_conv2(act)
                act_ret(act)
                act_osplit(act, o2[:], seg_cols(LAT))
                run_tiles(act, "act", BASE[f"out_{l}"], 8)
                act_norm(act, LAT, normw)
                act_ffn(act, BASE[f"f2_{l}"], FT)
            act_norm(act, LAT, normw, to_a=False)

        @block.vector
        def _(dve):
            link = Chain(dve, "dve_chain")
            dve.sem_inc(dve_evac.sem, RING)
            for n in range(LEAD):
                dve_split(dve, n, n)
            dve_ada(dve, link)
            for s in (CTX, LAT):
                dve.sem_inc(S("h_ready").sem, 1)
                dve_norm(dve, link, s, normw, gain_of(0, 0, s), shift_of(0, 0, s))
            dve_win(dve, link)
            dve_conv(dve, link)
            dve_dt(dve, link)
            dve_tm(dve, link)
            dve_states(dve, link)
            dve_ssd(dve, link)
            dve_mbout(dve, link)
            dve.sem_inc(S("mb_done").sem, 1)
            for s in (CTX, LAT):
                dve_rwprep(dve, link, s)
                for n in range(NRC):
                    dve_solve(dve, link, s, n)
                dve_rwout(dve, link, s)
            dve_osplit(dve, o0[:], slice(0, T2))
            dve_resid(dve, link, BASE["w_out"], 8, (CTX, LAT), lambda t, s: m_col(0, 2, t, s))
            for s, nm in ((CTX, "ffn_ctx"), (LAT, "ffn_lat")):
                dve.sem_inc(S("h_ready").sem, 1)
                dve_norm(dve, link, s, normw, gain_of(0, 1, s), shift_of(0, 1, s))
                dve_ffn(dve, BASE[nm], FT)
                dve_ffn_out(dve, link, BASE[nm], FT, s, lambda m, s=s: m_col(0, 5, m, s))
            dve.sem_inc(S("arena_free").sem, 1)
            for s in (CTX, LAT):
                dve.sem_inc(S("h_ready").sem, 1)
                dve_norm(dve, link, s, normw, gain_of(1, 0, s), shift_of(1, 0, s))
            run_tiles(dve, "dve", BASE["qkv"], 24)
            dve_attn(dve, link)
            dve_osplit(dve, oA[:], seg_cols(LAT))
            dve_resid(dve, link, BASE["na_out"], 8, (LAT,), lambda t, s: m_col(1, 2, t, s))
            dve.sem_inc(S("arena_free2").sem, 1)
            dve.sem_inc(S("h_ready").sem, 1)
            dve_norm(dve, link, LAT, normw, gain_of(1, 1, LAT), shift_of(1, 1, LAT))
            dve_router(dve, link)
            dve_ffn(dve, BASE["moe"], FT * NE, gate)
            dve_ffn_out(dve, link, BASE["moe"], FT * NE, LAT, lambda m: m_col(1, 5, m, LAT))
            dve.sem_inc(S("h_ready").sem, 1)
            dve_norm(dve, link, LAT, normw, lambda k: pc("n_fin", k, 1), None, final="x2")
            dve.wait_ge(*S("x2").next("dve"))
            for l in range(2):
                dve.sem_inc(S("h_ready").sem, 1)
                dve_norm(dve, link, LAT, normw, lambda k, l=l: pc("n1", 8 * l + k, 1), None)
                dve_ffn(dve, BASE[f"f1_{l}"], FT)
                dve_ffn_out(dve, link, BASE[f"f1_{l}"], FT, LAT, lambda m: 0.5)
                dve.sem_inc(S("h_ready").sem, 1)
                dve_norm(dve, link, LAT, normw, lambda k, l=l: pc("nm", 8 * l + k, 1), None)
                run_tiles(dve, "dve", BASE[f"in_{l}"], 24)
                dve_conv2_in(dve, link, E_IN[l])
                dve_stick(dve, link, l)
                dve_conv2(dve, link, l)
                dve_ret(dve, link, l)
                dve_osplit(dve, o2[:], seg_cols(LAT))
                dve_resid(dve, link, BASE[f"out_{l}"], 8, (LAT,), lambda t, s: 1.0)
                dve.sem_inc(S("h_ready").sem, 1)
                dve_norm(dve, link, LAT, normw, lambda k, l=l: pc("n2", 8 * l + k, 1), None)
                dve_ffn(dve, BASE[f"f2_{l}"], FT)
                dve_ffn_out(dve, link, BASE[f"f2_{l}"], FT, LAT, lambda m: 0.5)
            dve.sem_inc(S("h_ready").sem, 1)
            dve_norm(dve, link, LAT, normw, lambda k: pc("nf2", k, 1), None, final="out_ready")


def vec(v):
    return v.reshape(-1, P).T


def pad_to(a, n, axis=-1):
    w = [(0, 0)] * a.ndim
    w[axis] = (0, n - a.shape[axis])
    return np.pad(a, w)


def tiles_of(w):
    n = w.shape[1] // P
    return w.reshape(KT, P, n, P).transpose(2, 1, 0, 3).reshape(n, P, KT * P)


def ffn_tiles(w1, w3, w2):
    h1, h3 = tiles_of(w1), tiles_of(w3)
    o = w2.reshape(-1, P, D)
    n = len(o)
    out = np.empty((3 * n, P, D), np.float32)
    out[0], out[1] = h1[0], h3[0]
    out[2:3 * n - 1:3], out[3:3 * n - 1:3], out[4:3 * n - 1:3] = h1[1:], h3[1:], o[:-1]
    out[3 * n - 1] = o[-1]
    return out


def rw_cols(a):
    return pad_to(a[..., :1760], 14 * P)


def consts_a():
    i = np.arange(RC)
    ident = np.eye(P, dtype=np.float32)
    bones = np.kron(np.eye(2), np.ones((64, 64)))
    i64 = np.tile(np.eye(RC), (2, 1))
    s, t = i[:, None], i[None, :]
    mx = np.concatenate([s < t, s <= t, s > t, s >= t], 1)
    mn = np.concatenate([t < s, t > s], 1)
    lv = np.zeros((2, RLEV + 1, 2, RC, RC))
    for v in range(RLEV + 1):
        m = 1 << v
        low = (s // (2 * m) == t // (2 * m)) & ((s // m) % 2 == 1) & ((t // m) % 2 == 0)
        for d in range(2):
            nn = low if d == 0 else low.T
            lv[0, v, d], lv[1, v, d] = nn, nn.T
    lv = lv.transpose(3, 0, 1, 2, 4).reshape(RC, -1)
    scan64 = np.tile((np.arange(1024) % RC != 0).astype(np.float32), (P, 1))
    scan128 = np.tile((np.arange(T2) % MC != 0).astype(np.float32), (P, 1))
    j = np.arange(P)
    mssd = np.concatenate([j[:, None] <= j[None, :], j[:, None] >= j[None, :]], 1)
    two = lambda a: np.tile(a, (2, 1))
    return np.concatenate([ident, np.ones((P, P)), bones, i64, two(mx), two(mn), two(lv), scan64, scan128, mssd],
                          1).astype(np.float32)


def consts_b():
    j = np.arange(P)
    iota = np.tile(np.arange(NE), (P, 2))
    tri = j[:, None] >= j[None, :]
    smask = j[:, None] < j[None, :]
    rot = np.zeros((P, P))
    for c in range(P):
        base, r = c // 64 * 64, c % 64
        if r < 32:
            rot[base + r + 32, c] = -1.0
        else:
            rot[base + r - 32, c] = 1.0
    half = 32
    inv = (1.0 / (np.float32(10000.0) ** (np.arange(half, dtype=np.float32) / half))).astype(np.float32)
    ang = np.arange(SEG, dtype=np.float32)[:, None] * inv[None, :]
    cos = np.tile(np.cos(ang).T, (4, 1))
    sin = np.tile(np.sin(ang).T, (4, 1))
    lg = np.log1p(-np.exp2(-5.0 - np.arange(4)))
    s, t = np.arange(SEG)[:, None], np.arange(SEG)[None, :]
    dret = []
    for h in range(4):
        same = s // 64 == t // 64
        w = np.where(same | (s // 64 < t // 64), np.exp(lg[h] * np.abs(t - s)), 0.0) * 0.125
        dret.append(np.concatenate([w[0:P, :], w[P:, P:]], 1))
    return np.concatenate([iota, tri, smask, rot, cos, sin] + dret, 1).astype(np.float32)


def lay_out(i):
    c = {}
    z = lambda a: np.asarray(a)
    cols = {}
    cols["b_ada"] = np.concatenate([vec(z(i["b_ada"])[l]) for l in range(2)], 1)
    for nm, src in (("n_mix", "norm_mix"), ("n_ffn", "norm_ffn"), ("n1", "ffn1_norm_2"), ("nm", "mix_norm_2"),
                    ("n2", "ffn2_norm_2")):
        cols[nm] = np.concatenate([vec(i[src][l]) for l in range(2)], 1)
    cols["n_fin"], cols["nf2"] = vec(i["norm_final"]), vec(i["final_norm_2"])
    mu = rw_cols(i["rw_mu"][0])
    cols["mu_p"], cols["mu_n"] = vec(mu[0]), vec(mu[1])
    for nm, src in (("w0", "rw_w0"), ("a0", "rw_a0")):
        cols[nm] = np.concatenate([vec(i[src][0, d]) for d in range(2)], 1)
    cols["rk"] = np.concatenate([vec(i["rw_r_k"][0, d].reshape(-1)) for d in range(2)], 1)
    for nm, src in (("kk", "rw_k_k"), ("ka", "rw_k_a"), ("gnw", "rw_gn_w"), ("gnb", "rw_gn_b"), ("cb", "mb_conv_b"),
                    ("mbn", "mb_norm_w")):
        cols[nm] = vec(i[src][0])
    cols["cw"] = i["mb_conv_w"][0].reshape(5, 8, P).transpose(2, 1, 0).reshape(P, 40)
    cols["mbd"] = vec(np.repeat(i["mb_d"][0], 64))
    for nm, src in (("dtb", "mb_dt_bias"), ("alog", "mb_a_log")):
        v = np.zeros((P, 1), np.float32)
        v[0:8, 0], v[32:40, 0] = i[src][0, 0], i[src][0, 1]
        cols[nm] = v
    cols["c2w"] = i["conv_w_2"].reshape(2, CONV2, 2, P).transpose(3, 0, 2, 1).reshape(P, 124)
    for nm, src in (("c2b", "conv_b_2"), ("c2g", "conv_ln_g_2"), ("c2bb", "conv_ln_b_2"), ("rtg", "ret_norm_g_2")):
        cols[nm] = np.concatenate([vec(i[src][l]) for l in range(2)], 1)
    cols["rb"] = np.tile(i["moe_router_b"], (P, 1))
    cols["rw"] = i["moe_router_w"][0].reshape(KT, P, NE).transpose(1, 0, 2).reshape(P, -1)
    cols["cvec"] = np.stack([vec(i["c_ctx"]), vec(i["c"][0])], 2).reshape(P, 16)
    c["params"] = np.concatenate([cols[n] for n, _ in PARAMS], 1)
    c["consts"], c["constsb"] = consts_a(), consts_b()
    for nm, src in (("ctxT", "ctx"), ("xT", "x")):
        c[nm] = i[src][0].T.reshape(KT, P, SEG).transpose(1, 0, 2)
    c["lora"] = np.concatenate([i["rw_w_up"][0].reshape(64, 512), i["rw_a_up"][0].reshape(64, 512)], 0)
    c["gup"] = pad_to(i["rw_g_up"][0], P, 0)
    qr, qc = np.arange(SEG) // 64, np.arange(SEG) % 64
    start = np.clip(qc - 8, 0, 48)
    inside = (qc[None, :] >= start[:, None]) & (qc[None, :] < start[:, None] + 16)
    rpb = np.concatenate([i["na_rpb"][0].reshape(16, -1), np.full((16, 1), -BIG, np.float32)], 1)
    idx = (qr[None, :] - qr[:, None] + 7) * 31 + np.clip(qc[None, :] - qc[:, None] + 15, 0, 30)
    idx = np.where(inside, idx, 15 * 31)
    bias = rpb[:, idx]
    c["bias"] = bias.reshape(16, 2, P, SEG).transpose(2, 0, 1, 3).reshape(P, 16, 512)
    w = i["mix_w_in"][0]
    mb = w[:, 1760:]
    dtc = np.zeros((D, P), np.float32)
    dtc[:, 0:8], dtc[:, 32:40] = mb[:, 1536:1544], mb[:, 1544:1552]
    w_in = np.concatenate([mb[:, 512:1536], mb[:, 0:512], dtc, rw_cols(w)], 1)
    q = i["na_w_qkv"][0]
    parts = {"ada": np.asarray(i["w_ada"]).reshape(2, KT, P, 6, D).transpose(0, 3, 1, 2, 4).reshape(96, P, D), "w_in": tiles_of(w_in),
             "w_out": tiles_of(i["mix_w_out"][0]), "qkv": tiles_of(q), "na_out": tiles_of(i["na_w_out"][0])}
    f0 = ffn_tiles(i["ffn_w1"][0], i["ffn_w3"][0], i["ffn_w2"][0])
    parts["ffn_ctx"] = parts["ffn_lat"] = f0
    st = lambda a: np.asarray(a[0]).transpose(1, 0, 2).reshape(D, NE * DFF)
    parts["moe"] = ffn_tiles(st(i["moe_w1"]), st(i["moe_w3"]), np.asarray(i["moe_w2"][0]).reshape(NE * DFF, D))
    for l in range(2):
        for f, nm in ((1, "f1"), (2, "f2")):
            wi = i[f"ffn{f}_w_in_2"][l]
            parts[f"{nm}_{l}"] = ffn_tiles(wi[:, :DFF], wi[:, DFF:], i[f"ffn{f}_w_out_2"][l])
        wi = i["mix_w_in_2"][l]
        order = [slice(0, 512), slice(512, 1536), slice(2048, 2560), slice(2816, 3072), slice(1536, 2048),
                 slice(2560, 2816)]
        parts[f"in_{l}"] = tiles_of(np.concatenate([wi[:, o] for o in order], 1))
        parts[f"out_{l}"] = tiles_of(i["mix_w_out_2"][l])
    stream = np.zeros((NTILES, P, D), np.float32)
    for nm, n in STREAM:
        stream[BASE[nm]:BASE[nm] + n] = parts[nm]
    c["wstream"] = stream
    return c


def kernel(**inputs):
    import concourse.bacc as _bacc
    from concourse.bass_utils import run_bass_kernel_spmd as _run

    arrays = {k: np.ascontiguousarray(v, dtype=np.float32) for k, v in
              lay_out({k: np.asarray(v) for k, v in inputs.items()}).items()}
    nc = _bacc.Bacc("TRN2", target_bir_lowering=False, num_devices=1)
    io = {k: nc.dram_tensor(k, v.shape, F32, kind="ExternalInput").ap() for k, v in arrays.items()}
    io["out"] = nc.dram_tensor("outT", (P, KT, SEG), F32, kind="ExternalOutput").ap()
    build(nc, io)
    r = _run(nc, [arrays], core_ids=[0]).results[0]
    return r["outT"].transpose(2, 1, 0).reshape(1, SEG, D)
```

```python
from contextlib import ExitStack

import numpy as np
import concourse.bass as bass
from concourse import mybir

F32 = mybir.dt.float32
F32R = mybir.dt.float32r
ACT = mybir.ActivationFunctionType
ALU = mybir.AluOpType
AX = mybir.AxisListType

P = 128
D = 1024
KT = D // P
SEG = 256
CTX, LAT = 0, 1
T2 = 2 * SEG
DFF = 2816
FT = DFF // P
NE = 8
RING = 3
LEAD = 2
EPS = 1e-6
E05 = float(np.exp(np.float32(-0.5)))
RC = 64
NRC = SEG // RC
RLEV = 5
MC = 128
NMC = T2 // MC
CONV2 = 31
BIG = 1e30

PARAMS = [("b_ada", 96), ("n_mix", 16), ("n_ffn", 16), ("n_fin", 8), ("mu_p", 14), ("mu_n", 14),
          ("w0", 8), ("a0", 8), ("kk", 4), ("ka", 4), ("rk", 8), ("gnw", 4), ("gnb", 4),
          ("cw", 40), ("cb", 8), ("mbd", 4), ("mbn", 4), ("dtb", 1), ("alog", 1),
          ("n1", 16), ("nm", 16), ("n2", 16), ("c2w", 124), ("c2b", 4), ("c2g", 4), ("c2bb", 4),
          ("rtg", 4), ("nf2", 8), ("rb", 8), ("rw", 64), ("cvec", 16)]
COL = {}
_c = 0
for _n, _w in PARAMS:
    COL[_n] = (_c, _c + _w)
    _c += _w
NPAR = _c

CONSTS = [("ident", 128), ("ones", 128), ("bones", 128), ("i64", 64),
          ("mx", 256), ("lv", 2 * (RLEV + 1) * 2 * 64), ("scan64", 1024),
          ("scan128", 512), ("mssd", 256)]
CCOL = {}
_c = 0
for _n, _w in CONSTS:
    CCOL[_n] = (_c, _c + _w)
    _c += _w
NCON = _c
CONSTS_B = [("iota", 16), ("tri", 128), ("smask", 128), ("rot", 128), ("cos", 256), ("sin", 256),
            ("dret", 4 * 384)]
BCOL = {}
_c = 0
for _n, _w in CONSTS_B:
    BCOL[_n] = (_c, _c + _w)
    _c += _w
NCONB = _c

STREAM = [("ada", 96), ("w_in", 27), ("w_out", 8), ("ffn_ctx", 3 * FT), ("ffn_lat", 3 * FT), ("qkv", 24),
          ("na_out", 8), ("moe", 3 * FT * NE)]
for _l in range(2):
    STREAM += [(f"f1_{_l}", 3 * FT), (f"in_{_l}", 24), (f"out_{_l}", 8), (f"f2_{_l}", 3 * FT)]
ADA = STREAM[0][1]
ADA_RING = 6
assert ADA % (2 * ADA_RING) == 0 and ADA % RING == 0
BASE = {}
_c = 0
for _n, _w in STREAM:
    BASE[_n] = _c
    _c += _w
NTILES = _c + LEAD


def build(nc, io):
    with ExitStack() as es:
        cursor = [nc.sbuf_base + (-nc.sbuf_base) % 64]

        def sb(name, shape, dt=F32, at=None):
            size = int(np.prod(shape[1:])) * 4
            off = cursor[0] if at is None else at
            if at is None:
                cursor[0] += (size + 31) // 32 * 32
            assert off + size <= nc.sbuf_usable_end, (name, off + size)
            return nc.alloc_sbuf_tensor_at(name, list(shape), dt, offset=off)

        raw = sb("w_raw", [P, RING, 1024])
        whi = sb("w_hi", [P, RING, 1024], F32R)
        wlo = sb("w_lo", [P, RING, 1024], F32R)
        hT = sb("hT", [P, KT, T2])
        g_hi = sb("g_hi", [P, 2, SEG], F32R)
        g_lo = sb("g_lo", [P, 2, SEG], F32R)
        g_f = sb("g_f", [P, 2, SEG])
        sil = sb("sil", [P, 2, SEG])
        rs = sb("rs", [P, T2])
        mod = sb("mod", [P, 96, 2])
        gsm = sb("gsm", [P, 4, KT, 2])
        par = sb("par", [P, NPAR])
        cv = sb("cv", [P, 16])
        cv_hi = sb("cv_hi", [P, 8, 2], F32R)
        cv_lo = sb("cv_lo", [P, 8, 2], F32R)
        ident = sb("ident", [P, 128])
        ones = sb("ones", [P, 128])
        bones = sb("bones", [P, 128])
        area = cursor[0]
        a_hi = sb("a_hi", [P, KT, T2], F32R)
        a_lo = sb("a_lo", [P, KT, T2], F32R)
        arena = cursor[0]
        END = nc.sbuf_usable_end // 64 * 64

        def lay(start, items):
            out = []
            for name, shape in items:
                out.append(sb(name, shape, at=start))
                start += (int(np.prod(shape[1:])) * 4 + 31) // 32 * 32
            return out + [start]

        zrw, con, zx, zg, zdt, m0 = lay(arena, [
            ("zrw", [P, 14, 2, 260]), ("con", [P, NCON - 384]), ("zx", [P, 8, 2, 260]),
            ("zg", [P, 4, T2]), ("zdt", [P, T2])])
        zx_at = m0 - (4 * T2 + T2 + 8 * 520) * 4
        ps = es.enter_context(nc.psum_tensor("ps", [P, 8, 512], F32))

        def pc(name, i=0, n=None):
            a, b = COL[name]
            return par[:, a + i:(a + i + n) if n else b]

        def cc(name):
            a, b = CCOL[name]
            return con[:, a - 384:b - 384]

        class Signal:

            def __init__(self, name):
                self.sem = es.enter_context(nc.semaphore(name))
                self.taken = {}
                self.made = 0
                self.one = (self.sem, 1)
                self.dma = (self.sem, 16)

            def next(self, who, n=1):
                self.taken[who] = self.taken.get(who, 0) + n
                return self.sem, self.taken[who]

        names = {}

        def S(name):
            if name not in names:
                names[name] = Signal(name)
            return names[name]

        ada_raw = sb("ada_raw", [P, ADA_RING, 1024], at=zx_at)
        ada_loaded = [S(f"ada_loaded{i}") for i in range(ADA_RING)]
        raw_loaded = [S(f"raw_loaded{i}") for i in range(RING)]
        hi_ready, lo_ready, tile_used = S("hi_ready"), S("lo_ready"), S("tile_used")
        act_evac, dve_evac = S("act_evac"), S("dve_evac")

        block = es.enter_context(nc.Block())

        def repeat(eng, n, unroll, body, first=0):
            full = (n - first) // unroll
            if full >= 2:
                with eng.Fori(0, full) as i:
                    for j in range(unroll):
                        body(i * unroll + (first + j), j)
            else:
                full = 0
            for t in range(first + full * unroll, n):
                body(t, (t - first) % unroll)

        def one(t):
            return slice(t, t + 1) if isinstance(t, int) else bass.ds(t, 1)

        def sp_stream(sp):
            w = io["wstream"]

            def ada_tile(n, j):
                if not (isinstance(n, int) and n < ADA_RING):
                    sp.wait_ge(lo_ready.sem, n - (ADA_RING - 1))
                sp.dma_start(ada_raw[:, j % ADA_RING, :], w[one(n)].rearrange("o p c -> p (o c)")
                             ).then_inc(ada_loaded[j % ADA_RING].sem, 16)
            for n in range(ADA_RING):
                ada_tile(n, n)
            for n in range(RING):
                sp.dma_start(raw[:, n, :], w[ADA + n]).then_inc(raw_loaded[n].sem, 16)
            repeat(sp, ADA, ADA_RING, ada_tile, first=ADA_RING)

            def tile(n, j):
                sp.wait_ge(lo_ready.sem, n - (RING - 1))
                sp.dma_start(raw[:, j % RING, :], w[one(n)].rearrange("o p c -> p (o c)")
                             ).then_inc(raw_loaded[j % RING].sem, 16)
            repeat(sp, NTILES, RING, tile, first=ADA + RING)

        def act_split(act, n, i3, slot):
            act.wait_ge(raw_loaded[slot].sem, i3 * 16 + (16 - ADA // RING * 16))
            act.wait_ge(tile_used.sem, n + 1)
            nc.scalar.activation(whi[:, slot, :], raw[:, slot, :], ACT.Copy).then_inc(hi_ready.sem, 1)

        def act_split_ada(act, n, rounds, j):
            act.wait_ge(ada_loaded[j % ADA_RING].sem, rounds * 16 + 16)
            act.wait_ge(tile_used.sem, n + 1)
            nc.scalar.activation(whi[:, j % RING, :], ada_raw[:, j % ADA_RING, :], ACT.Copy
                                 ).then_inc(hi_ready.sem, 1)

        def dve_split_ada(dve, n, j):
            dve.wait_ge(hi_ready.sem, n + 1)
            nc.vector.tensor_tensor(wlo[:, j % RING, :], ada_raw[:, j % ADA_RING, :],
                                    whi[:, j % RING, :].bitcast(F32), ALU.subtract).then_inc(lo_ready.sem, 1)

        def dve_split(dve, n, slot):
            dve.wait_ge(hi_ready.sem, n + 1)
            nc.vector.tensor_tensor(wlo[:, slot, :], raw[:, slot, :], whi[:, slot, :].bitcast(F32),
                                    ALU.subtract).then_inc(lo_ready.sem, 1)

        def run_tiles(eng, who, base, count, before=None, after=None, t0=0):
            full = count // RING
            if full < 2:
                full = 0

            def step(t, i, j):
                n = t + (base + LEAD)
                c = base + t0 + j + LEAD
                slot = c % RING
                if i is None:
                    i3 = n // RING
                else:
                    i3 = i + c // RING
                if before:
                    before(t)
                if who == "act":
                    act_split(eng, n, i3, slot)
                else:
                    dve_split(eng, n, slot)
                if after:
                    after(t, (base + t0 + j) % RING)
            if full:
                with eng.Fori(0, full) as i:
                    for j in range(RING):
                        step(i * RING + (t0 + j), i, j)
            for r in range(full * RING, count):
                step(t0 + r, None, r % RING)

        def pe_triple(out, lhs, rhs, start, stop, skip=True):
            nc.tensor.matmul(out, lhs[0], rhs[0], start=start, stop=False, skip_group_check=skip)
            nc.tensor.matmul(out, lhs[0], rhs[1], start=False, stop=False, skip_group_check=skip)
            return nc.tensor.matmul(out, lhs[1], rhs[0], start=False, stop=stop, skip_group_check=skip)

        evacs = {"act": 0, "dve": 0}

        def pe_gemm(pe, base, count, evac, by, outs):
            sig = act_evac if evac == "act" else dve_evac
            e0 = evacs[evac]
            evacs[evac] += count

            def tile(t, j):
                slot = (base + j) % RING
                pe.wait_ge(lo_ready.sem, t + (base + 1))
                pe.wait_ge(sig.sem, t + (e0 + 1))
                last = None
                groups = outs(5 + slot)
                for gi, (out, wfirst, operand) in enumerate(groups):
                    for k in range(KT):
                        w = (whi[:, slot, k * P:(k + 1) * P], wlo[:, slot, k * P:(k + 1) * P])
                        o = operand(k)
                        last = pe_triple(out, w if wfirst else o, o if wfirst else w, k == 0, k == KT - 1)
                last.then_inc(tile_used.sem, 1)
            repeat(pe, count, RING, tile)

        def used(base, t):
            return t + (base + RING + 1)

        def span(segs):
            return (slice(0, T2) if len(segs) == 2 else slice(segs[0] * SEG, segs[0] * SEG + SEG))

        def a_cols(segs):
            c = span(segs)
            return lambda k: (a_hi[:, k, c], a_lo[:, k, c])

        def pe_ffn(pe, base, seg, F):
            a = a_cols([seg])

            def h_tile(t, j, bank):
                slot = (base + j) % RING
                pe.wait_ge(lo_ready.sem, t + (base + 1))
                for k in range(KT):
                    w = (whi[:, slot, k * P:(k + 1) * P], wlo[:, slot, k * P:(k + 1) * P])
                    last = pe_triple(ps[:, bank, 0:SEG], w, a(k), k == 0, k == KT - 1)
                last.then_inc(tile_used.sem, 1)

            def out_tile(t, j, par_, f, first, lastf):
                slot = (base + j) % RING
                pe.wait_ge(lo_ready.sem, t + (base + 1))
                pe.wait_ge(S("g_ready").sem, f + (g0 + 1))
                for m in range(KT):
                    w = (whi[:, slot, m * P:(m + 1) * P], wlo[:, slot, m * P:(m + 1) * P])
                    g = (g_hi[:, par_, :], g_lo[:, par_, :])
                    last = pe_triple(ps[:, m // 2, (m % 2) * SEG:(m % 2 + 1) * SEG], w, g,
                                     first and m % 2 == 0, lastf)
                last.then_inc(tile_used.sem, 1)

            g0 = gcount["pe"]
            gcount["pe"] += F
            h_tile(0, 0, 4)
            h_tile(1, 1, 6)
            h_tile(2, 2, 5)
            h_tile(3, 0, 7)
            out_tile(4, 1, 0, 0, True, False)

            with pe.Fori(0, (F - 2) // 2) as i:
                for u in range(2):
                    t = i * 6 + (5 + 3 * u)
                    h_tile(t, 2, 4 + u)
                    h_tile(t + 1, 0, 6 + u)
                    out_tile(t + 2, 1, 1 - u, i * 2 + (1 + u), False, False)
            out_tile(3 * F - 1, 2, (F - 1) % 2, F - 1, False, True)

        gcount = {"pe": 0, "act": 0, "dve": 0}

        def act_ffn(act, base, F):
            g0 = gcount["act"]
            gcount["act"] += F

            def split(t, i, j):
                c = base + j + LEAD
                n = t + (base + LEAD)
                i3 = n // RING if i is None else i * 2 + c // RING
                act_split(act, n, i3, c % RING)

            def silu(f, th1, par_):
                act.wait_ge(tile_used.sem, used(base, th1))
                if not (isinstance(f, int) and f + g0 < 2):
                    act.wait_ge(S("g_ready").sem, f + (g0 - 1))
                nc.scalar.activation(sil[:, par_, :], ps[:, 4 + par_, 0:SEG], ACT.Silu
                                     ).then_inc(S("silu_ready").sem, 1)
            split(0, None, 0)
            split(1, None, 1)
            silu(0, 0, 0)
            split(2, None, 2)
            split(3, None, 3)
            split(4, None, 4)
            with act.Fori(0, (F - 2) // 2) as i:
                for u in range(2):
                    silu(i * 2 + (1 + u), i * 6 + (2 + 3 * u), 1 - u)
                    for v in range(3):
                        j = 5 + 3 * u + v
                        split(i * 6 + j, i, j)
            silu(F - 1, 3 * (F - 1) - 1, (F - 1) % 2)
            split(3 * F - 1, None, 3 * F - 1)

        def dve_ffn(dve, base, F, gate=None):
            g0 = gcount["dve"]
            gcount["dve"] += F

            def hidden(f, th3, tout, par_, e=None):
                dve.wait_ge(S("silu_ready").sem, f + (g0 + 1))
                dve.wait_ge(tile_used.sem, used(base, th3))
                nc.vector.tensor_tensor(g_f[:, par_, :], sil[:, par_, :], ps[:, 6 + par_, 0:SEG],
                                        ALU.mult).then_inc(S("g_f").sem, 1)
                cnt = 1
                if gate is not None:
                    dve.wait_ge(S("g_f").sem, f * 2 + (gf0 + 1))
                    nc.vector.tensor_tensor(g_f[:, par_, :], g_f[:, par_, :],
                                            gate[:, one(e), :].rearrange("p o t -> p (o t)"),
                                            ALU.mult).then_inc(S("g_f").sem, 1)
                    cnt = 2
                dve.wait_ge(S("g_f").sem, f * cnt + (gf0 + cnt))
                if tout is not None:
                    dve.wait_ge(tile_used.sem, used(base, tout))
                nc.vector.tensor_copy(g_hi[:, par_, :], g_f[:, par_, :]).then_inc(S("g_hi").sem, 1)
                dve.wait_ge(S("g_hi").sem, f + (g0 + 1))
                nc.vector.tensor_tensor(g_lo[:, par_, :], g_f[:, par_, :], g_hi[:, par_, :].bitcast(F32),
                                        ALU.subtract).then_inc(S("g_ready").sem, 1)

            def split(t, j):
                dve_split(dve, t + (base + LEAD), (base + j + LEAD) % RING)
            gf0 = gfc[0]
            gfc[0] += F * (2 if gate is not None else 1)
            split(0, 0)
            split(1, 1)
            hidden(0, 1, None, 0, 0)
            for t in (2, 3, 4):
                split(t, t)

            def pair(i, f0, e0, e1, first):
                for u in range(2):
                    f = i * 2 + (f0 + u)
                    t = i * 6 + (3 * (f0 + u) + 2)
                    hidden(f, t - 2, None if (first and u == 0) else t - 4, 1 - u, (e0, e1)[u])
                    for v in range(3):
                        split(t + v, 2 + v)
            if gate is None:
                pair(0, 1, 0, 0, True)
                with dve.Fori(0, (F - 4) // 2) as i:
                    pair(i, 3, 0, 0, False)
            else:
                pair(0, 1, 0, 0, True)
                with dve.Fori(0, 9) as i:
                    pair(i, 3, 0, 0, False)
                with dve.Fori(0, NE - 1) as e:
                    pair(e * 11, 21, e, e + 1, False)
                    with dve.Fori(0, 10) as i:
                        pair(e * 11 + i, 23, e + 1, e + 1, False)
            hidden(F - 1, 3 * (F - 1), 3 * (F - 3) + 4, (F - 1) % 2, NE - 1)
            split(3 * F - 1, 3 * F - 1)

        gfc = [0]

        class Chain:
            def __init__(self, eng, name):
                self.eng, self.sig, self.n = eng, S(name), 0

            def __call__(self, ins, also=None):
                self.n += 1
                ins.then_inc(self.sig.sem, 1)
                self.eng.wait_ge(self.sig.sem, self.n)

        def bc(ap, shape):
            return ap.broadcast_to(list(shape))

        def seg_cols(seg):
            return slice(seg * SEG, seg * SEG + SEG)

        def act_norm(act, seg, work, shift=None, to_a=True):
            for k in range(KT):
                act.wait_ge(*S("h_ready").next("act"))
                nc.scalar.activation(work[:, k, :], hT[:, k, seg_cols(seg)], ACT.Square).then_inc(*S("sq_ready").one)
            act.wait_ge(*S("ms_ready").next("act"))
            nc.scalar.activation(rs[:, 0:SEG], rs[:, 0:SEG], ACT.Sqrt).then_inc(*S("rt_ready").one)
            if to_a:
                for k in range(KT):
                    act.wait_ge(*S("a_ready").next("act"))
                    dst = a_hi[:, k, seg_cols(seg)]
                    if shift is None:
                        nc.scalar.activation(dst, work[:, k, :], ACT.Copy).then_inc(*S("ahi_ready").one)
                    else:
                        nc.scalar.activation(dst, work[:, k, :], ACT.Identity, bias=shift(k)
                                             ).then_inc(*S("ahi_ready").one)

        def pe_norm(pe):
            for k in range(KT):
                pe.wait_ge(*S("sq_ready").next("pe"))
                last = nc.tensor.matmul(ps[:, 4, 0:SEG], ones[:], normw[:, k, :],
                                        start=(k == 0), stop=(k == KT - 1))
            last.then_inc(*S("ss_ready").one)

        def dve_norm(dve, link, seg, work, gain, shift, final=None, full=False):
            dve.wait_ge(*S("ss_ready").next("dve"))
            nc.vector.tensor_scalar(rs[:, 0:SEG], ps[:, 4, 0:SEG], 1.0 / D, EPS, ALU.mult, ALU.add
                                    ).then_inc(*S("ms_ready").one)
            dve.wait_ge(*S("rt_ready").next("dve"))
            link(nc.vector.reciprocal(rs[:, 0:SEG], rs[:, 0:SEG]))
            for k in range(KT):
                h = hT[:, k, seg_cols(seg)]
                dst = work[:, k, :] if final is None else h
                ins = nc.vector.scalar_tensor_tensor(dst, h, gain(k), rs[:, 0:SEG], ALU.mult, ALU.mult)
                if full:
                    link(ins)
                    ins = nc.vector.tensor_scalar(dst, dst, shift(k), None, ALU.add)
                if final is None:
                    ins.then_inc(*S("a_ready").one)
                elif k < KT - 1:
                    link(ins)
                else:
                    ins.then_inc(*S(final).one)
            if final is None:
                dve.wait_ge(*S("a_ready").next("dve", KT))
                for k in range(KT):
                    dve.wait_ge(*S("ahi_ready").next("dve"))
                    dst, hi = a_lo[:, k, seg_cols(seg)], a_hi[:, k, seg_cols(seg)].bitcast(F32)
                    if shift is None or full:
                        ins = nc.vector.tensor_tensor(dst, work[:, k, :], hi, ALU.subtract)
                    else:
                        ins = nc.vector.scalar_tensor_tensor(dst, work[:, k, :], shift(k), hi, ALU.add, ALU.subtract)
                ins.then_inc(*S("alo_ready").one)
                dve.wait_ge(*S("alo_ready").next("dve"))

        normw = sb("normw", [P, KT, SEG], at=arena)

        def load_list(sp):
            sp.dma_start(par[:], io["params"]).then_inc(*S("par").dma)
            sp.dma_start(ident[:], io["consts"][:, 0:128]).then_inc(*S("par").dma)
            sp.dma_start(ones[:], io["consts"][:, 128:256]).then_inc(*S("par").dma)
            sp.dma_start(bones[:], io["consts"][:, 256:384]).then_inc(*S("par").dma)
            sp.dma_start(con[:], io["consts"][:, 384:NCON]).then_inc(*S("par").dma)
            sp.dma_start(hT[:, :, 0:SEG], io["ctxT"]).then_inc(*S("par").dma)
            sp.dma_start(hT[:, :, SEG:T2], io["xT"]).then_inc(*S("par").dma)

        NLOAD = 7 * 16

        NJ = 6 * D // 1024
        GROUPS = 2 * NJ
        modr = sb("modr", [P, GROUPS, 1024], at=area)

        def ada_tiles(eng, tile, group_end):
            def three_groups(i):
                for g in range(3):
                    for k in range(KT):
                        tile(i, g * KT + k)
                    group_end(i, g)
            with eng.Fori(0, GROUPS // 3 - 1) as i:
                three_groups(i)
            three_groups(GROUPS // 3 - 1)

        def act_ada(act):
            act.wait_ge(S("par").sem, NLOAD)
            nc.scalar.activation(cv[:], pc("cvec"), ACT.Silu).then_inc(*S("cv").one)
            act.wait_ge(*S("cv").next("act"))
            nc.scalar.activation(cv_hi[:].rearrange("p k s -> p (k s)"), cv[:], ACT.Copy).then_inc(*S("cvh").one)
            act.sem_inc(S("row_sb").sem, 3)

            def group_end(i, g):
                act.wait_ge(tile_used.sem, i * 3 * KT + used(0, (g + 1) * KT - 1))
                nc.scalar.activation(modr[0:2, one(i * 3 + g), :].rearrange("p o c -> p (o c)"),
                                     ps[0:2, 2 * g:2 * g + 2, :].rearrange("p b c -> p (b c)"),
                                     ACT.Copy).then_inc(S("row_sb").sem, 1)

            def tile(i, j):
                n = i * 3 * KT + (j + LEAD)
                if isinstance(n, int) and n >= ADA:
                    act_split(act, n, n // RING, n % RING)
                else:
                    act_split_ada(act, n, i * (3 * KT // ADA_RING) + (j + LEAD) // ADA_RING, j + LEAD)
            ada_tiles(act, tile, group_end)

        def pe_ada(pe):
            pe.wait_ge(*S("cvl").next("pe"))

            def tile(i, j):
                k, g, slot = j % KT, j // KT, j % RING
                if k == 0:
                    pe.wait_ge(S("row_sb").sem, i * 3 + (g + 1))
                pe.wait_ge(lo_ready.sem, i * 3 * KT + (j + 1))
                for half in range(2):
                    c = slice(half * 512, half * 512 + 512)
                    last = pe_triple(ps[0:2, 2 * g + half, :], (cv_hi[:, k, :], cv_lo[:, k, :]),
                                     (whi[:, slot, c], wlo[:, slot, c]), k == 0, k == KT - 1)
                last.then_inc(tile_used.sem, 1)
            ada_tiles(pe, tile, lambda i, g: None)
            pe.wait_ge(S("row_sb").sem, GROUPS + 3)
            for g in range(GROUPS):
                for c in range(8):
                    j = g * 8 + c
                    last = nc.tensor.transpose(ps[:, 6, 2 * j:2 * j + 2], modr[0:2, g, c * P:(c + 1) * P],
                                               ident[0:2, 0:2])
            last.then_inc(*S("mod_ps").one)

        def dve_ada(dve, link):
            dve.wait_ge(S("par").sem, NLOAD)
            dve.wait_ge(*S("cvh").next("dve"))
            nc.vector.tensor_tensor(cv_lo[:].rearrange("p k s -> p (k s)"), cv[:],
                                    cv_hi[:].rearrange("p k s -> p (k s)").bitcast(F32),
                                    ALU.subtract).then_inc(*S("cvl").one)

            def tile(i, j):
                n = i * 3 * KT + (j + LEAD)
                if isinstance(n, int) and n >= ADA:
                    dve_split(dve, n, n % RING)
                else:
                    dve_split_ada(dve, n, j + LEAD)
            ada_tiles(dve, tile, lambda i, g: None)
            dve.wait_ge(*S("mod_ps").next("dve"))
            link(nc.vector.tensor_tensor(mod[:], ps[:, 6, 0:192].rearrange("p (j s) -> p j s", s=2),
                                         bc(pc("b_ada").unsqueeze(2), [P, 96, 2]), ALU.add))
            for L in range(2):
                for h in range(2):
                    sc = mod[:, L * 48 + (3 * h + 1) * 8:L * 48 + (3 * h + 2) * 8, :]
                    dst = gsm[:, 2 * L + h, :, :]
                    g = pc("n_mix" if h == 0 else "n_ffn", 8 * L, 8)
                    link(nc.vector.tensor_scalar(dst, sc, 1.0, None, ALU.add))
                    link(nc.vector.tensor_tensor(dst, dst, bc(g.unsqueeze(2), [P, KT, 2]), ALU.mult))

        def m_col(L, j, k, s):
            return mod[:, L * 48 + j * 8 + k, s:s + 1]

        def gain_of(L, h, s):
            return lambda k: gsm[:, 2 * L + h, k, s:s + 1]

        def shift_of(L, h, s):
            return lambda k: m_col(L, 3 * h, k, s)

        def dve_resid(dve, link, base, count, segs, coef):
            def evac(t, slot):
                dve.wait_ge(tile_used.sem, used(base, t))
                for i, s in enumerate(segs):
                    dst = hT[:, t, seg_cols(s)]
                    c0 = s * SEG if len(segs) == 2 else 0
                    ins = nc.vector.scalar_tensor_tensor(dst, ps[:, 5 + slot, c0:c0 + SEG], coef(t, s), dst,
                                                         ALU.mult, ALU.add)
                    if i == len(segs) - 1:
                        ins.then_inc(dve_evac.sem, 1)
                    else:
                        link(ins)
            for t in range(count):
                dve_split(dve, base + t + LEAD, (base + t + LEAD) % RING)
                evac(t, (base + t) % RING)
            dve.wait_ge(dve_evac.sem, RING + evd["n"] + count)
            evd["n"] += count

        evd = {"n": 0}

        def dve_ffn_out(dve, link, base, F, seg, coef, normed=True):
            dve.wait_ge(tile_used.sem, used(base, 3 * F - 1))
            for m in range(KT):
                dst = hT[:, m, seg_cols(seg)]
                src = ps[:, m // 2, (m % 2) * SEG:(m % 2 + 1) * SEG]
                c = coef(m)
                link(nc.vector.scalar_tensor_tensor(dst, src, c, dst, ALU.mult, ALU.add))
                if normed:
                    dve.sem_inc(S("h_ready").sem, 1)

        ob = END - 16 * 1024 - 64
        o0 = sb("o0", [P, KT, T2], at=ob)
        xc, hin, _ = lay(area, [("xc", [P, 8, T2]), ("hin", [P, 2, NMC, 512])])
        xtm, btm, xdt, _ = lay(zx_at, [("xtm", [P, NMC, 512]), ("btm", [P, NMC, 2, P]), ("xdt", [P, 2, 512])])
        wm, cm_, e1, dd, gm, tmv, du, dw, dl_, _m = lay(m0, [
            ("wm", [P, 2, 512]), ("cm_", [P, 2, 512]), ("e1", [P, 512]), ("dd", [P, 512]),
            ("gm", [P, 2, P]), ("tmv", [P, 3, NMC, 40]), ("du", [P, T2]), ("dw", [P, T2]), ("dl_", [P, T2])])
        assert _m <= ob, (_m, ob)
        e1s, dds = (e1, du), (dd, dl_)
        wms = (wm, sb("wm_b", [P, 2, 512], at=ob))
        cms = (cm_, sb("cm_b", [P, 2, 512], at=ob + 4096))
        DT = 40

        def act_win(act):
            def evac_to(dst, pads):
                def evac(t, slot, first):
                    act.wait_ge(tile_used.sem, used(BASE["w_in"], t))
                    src = ps[:, 5 + slot, :]
                    if pads:
                        d = dst[:, one(t - first), :, 2:258].rearrange("p o s t -> p (o s) t")
                        src = src.rearrange("p (s t) -> p s t", s=2)
                    else:
                        d = dst[:, one(t - first), :].rearrange("p o t -> p (o t)")
                    nc.scalar.activation(d, src, ACT.Copy).then_inc(act_evac.sem, 1)
                return evac
            for n, dst, pads, first in ((8, zx, True, 0), (4, zg, False, 8), (1, zdt.rearrange("p (o t) -> p o t", o=1), False, 12),
                                        (14, zrw, True, 13)):
                ev = evac_to(dst, pads)
                run_tiles(act, "act", BASE["w_in"], n, t0=first,
                          after=lambda t, slot, ev=ev, first=first: ev(t, slot, first))

        def dve_win(dve, link):
            for sl in (slice(0, 2), slice(258, 260)):
                link(nc.vector.memset(zx[:, :, :, sl], 0.0))
            run_tiles(dve, "dve", BASE["w_in"], 9)
            dve.wait_ge(act_evac.sem, RING + 8)
            for t in range(9, 27):
                n = BASE["w_in"] + t + LEAD
                dve_split(dve, n, n % RING)
                dve_conv(link, 3 * (t - 9), 3)
            dve.wait_ge(act_evac.sem, RING + 27)

        def dve_conv(link, first, count):
            for j in range(first, min(first + count, 40)):
                i, tap = j // 5, j % 5
                x = zx[:, i, :, tap:tap + SEG]
                dst = o0[:, i, :].rearrange("p (s t) -> p s t", s=2)
                w = pc("cw", i * 5 + tap, 1)
                if tap == 0:
                    link(nc.vector.tensor_scalar(dst, x, w, None, ALU.mult))
                elif tap < 4:
                    link(nc.vector.scalar_tensor_tensor(dst, x, w, dst, ALU.mult, ALU.add))
                else:
                    nc.vector.scalar_tensor_tensor(dst, x, w, dst, ALU.mult, ALU.add
                                                   ).then_inc(*S("conv_ready").one)

        def act_conv(act):
            for i in range(8):
                act.wait_ge(*S("conv_ready").next("act"))
                nc.scalar.activation(xc[:, i, :], o0[:, i, :], ACT.Silu, bias=pc("cb", i, 1)
                                     ).then_inc(*S("xc_ready").one)

        def dve_dt(dve, link):
            z, u, w, l = zdt[0:DT, :], du[0:DT, :], dw[0:DT, :], dl_[0:DT, :]
            link(nc.vector.tensor_scalar(z, z, pc("dtb", 0, 1)[0:DT], None, ALU.add))
            link(nc.vector.scalar_tensor_tensor(w, z, -1.0, z, ALU.mult, ALU.max))
            dve.wait_ge(*S("aneg").next("dve"))
            dve.sem_inc(S("dt_abs").sem, 1)
            dve.wait_ge(*S("dt_u").next("dve"))
            nc.vector.tensor_scalar(w, u, 1.0, None, ALU.add).then_inc(*S("dt_w").one)
            dve.wait_ge(*S("dt_l").next("dve"))
            link(nc.vector.scalar_tensor_tensor(u, w, -1.0, u, ALU.add, ALU.subtract))
            link(nc.vector.reciprocal(w, w))
            link(nc.vector.tensor_tensor(u, u, w, ALU.mult))
            link(nc.vector.tensor_tensor(l, l, u, ALU.subtract))
            link(nc.vector.scalar_tensor_tensor(z, z, 0.0, l, ALU.max, ALU.add))
            link(nc.vector.tensor_scalar(u, z, pc("alog", 0, 1)[0:DT], -1.0, ALU.mult, ALU.mult))
            link(nc.vector.tensor_tensor_scan(w, cc("scan128")[0:DT], u, 0.0, ALU.mult, ALU.add))
            ch = lambda a: a.rearrange("p (c l) -> p c l", l=MC)
            tot = ch(w)[:, :, MC - 1:MC]
            link(nc.vector.tensor_tensor(ch(l), bc(tot, [DT, NMC, MC]), ch(w), ALU.subtract))
            b = slice(32, DT)
            link(nc.vector.tensor_tensor(du[b], dw[b], du[b], ALU.subtract))
            link(nc.vector.tensor_tensor(ch(dw[b]), bc(ch(dw[b])[:, :, MC - 1:MC], [8, NMC, MC]),
                                         ch(du[b]), ALU.subtract))
            link(nc.vector.tensor_copy(dl_[b], du[b]))
            dg = e1[0:DT, 0:NMC * DT].rearrange("p (c j) -> p c j", c=NMC)
            link(nc.vector.tensor_copy(dg, bc(ident[0:DT, 0:DT].unsqueeze(1), [DT, NMC, DT])))
            f = slice(0, 32)
            link(nc.vector.tensor_tensor(dg[f], dg[f], bc(ch(dw[f])[:, :, MC - 1:MC], [32, NMC, DT]), ALU.mult))
            nc.vector.tensor_tensor(dg[b], dg[b], bc(ch(dw[b])[:, :, 0:1], [8, NMC, DT]), ALU.mult
                                    ).then_inc(*S("dt_rows").one)
            dve.wait_ge(*S("dt_rows").next("dve"))

        def act_dt(act):
            act.wait_ge(S("par").sem, NLOAD)
            al = pc("alog", 0, 1)[0:DT]
            nc.scalar.activation(al, al, ACT.Exp).then_inc(*S("aneg").one)
            act.wait_ge(*S("dt_abs").next("act"))
            nc.scalar.activation(du[0:DT], dw[0:DT], ACT.Exp, scale=-1.0).then_inc(*S("dt_u").one)
            act.wait_ge(*S("dt_w").next("act"))
            nc.scalar.activation(dl_[0:DT], dw[0:DT], ACT.Ln).then_inc(*S("dt_l").one)
            act.wait_ge(*S("dt_rows").next("act"))
            nc.scalar.activation(dl_[0:DT], dl_[0:DT], ACT.Exp).then_inc(*S("dec_rows").one)
            act.wait_ge(*S("tot_ps").next("act"))
            nc.scalar.activation(dd[:, 0:NMC * DT], ps[:, 4, 0:NMC * DT], ACT.Exp).then_inc(*S("etot").one)

        def pe_dt(pe):
            pe.wait_ge(*S("dt_rows").next("pe"))
            nc.tensor.matmul(ps[:, 4, 0:NMC * DT], ones[0:DT, :], e1[0:DT, 0:NMC * DT],
                             start=True, stop=True).then_inc(*S("tot_ps").one)
            pe.wait_ge(*S("dec_rows").next("pe"))
            for q, rows in enumerate((zdt, dw, dl_)):
                for c in range(NMC):
                    last = nc.tensor.transpose(ps[:, 5 + q, c * DT:(c + 1) * DT], rows[0:DT, c * MC:(c + 1) * MC],
                                               ident[0:DT, 0:DT])
            last.then_inc(*S("tm_ps").one)
            pe.wait_ge(*S("xc_ready").next("pe", 8))
            for c in range(NMC):
                for i in range(4):
                    last = nc.tensor.transpose(ps[:, c, i * P:(i + 1) * P], xc[:, i, c * MC:(c + 1) * MC], ident[:])
            last.then_inc(*S("xtm_ps").one)
            pe.wait_ge(*S("xtm_sb").next("pe"))
            for c in range(NMC):
                for g in range(2):
                    last = nc.tensor.transpose(ps[:, c // 2, ((c % 2) * 2 + g) * P:((c % 2) * 2 + g + 1) * P],
                                               xc[:, 4 + g, c * MC:(c + 1) * MC], ident[:])
            last.then_inc(*S("btm_ps").one)

        def dve_tm(dve, link):
            dve.wait_ge(*S("tm_ps").next("dve"))
            for q in range(3):
                link(nc.vector.tensor_copy(tmv[:, q, :, :].rearrange("p c j -> p (c j)"),
                                           ps[:, 5 + q, 0:NMC * DT]))
            dve.wait_ge(*S("xtm_ps").next("dve"))
            for c in range(NMC):
                last = nc.vector.tensor_copy(xtm[:, c, :], ps[:, c, :])
            last.then_inc(*S("xtm_sb").one)
            dve.wait_ge(*S("btm_ps").next("dve"))
            dve.wait_ge(*S("xtm_sb").next("dve"))
            for b_ in range(2):
                link(nc.vector.tensor_copy(btm[:, 2 * b_:2 * b_ + 2, :, :].rearrange("p c g n -> p (c g n)"),
                                           ps[:, b_, :]))

        def heads8(ap):
            return ap.rearrange("p (h e) -> p h e", h=8)

        def dve_states(dve, link):
            dve.wait_ge(*S("etot").next("dve"))
            link(nc.vector.memset(hin[:, 0, 0, :], 0.0))
            link(nc.vector.memset(hin[:, 1, 1, :], 0.0))
            et = dd[:, 0:NMC * DT].rearrange("p (c j) -> p c j", c=NMC)
            order = ((0, 1, 2, 3), (1, 0, 3, 2))
            for step in range(NMC - 1):
                for d in range(2):
                    c, nxt = order[d][step], order[d][step + 1]
                    if not (step == 0 and d == 0):
                        dve.wait_ge(*S("st_ps").next("dve"))
                        add_state(dve, link, *pend[0])
                    x = heads8(xdt[:, 0, :])
                    link(nc.vector.tensor_tensor(x, heads8(xtm[:, c, :]),
                                                 bc(tmv[:, 0, c, 32 * d:32 * d + 8].unsqueeze(2), [P, 8, 64]), ALU.mult))
                    nc.vector.tensor_tensor(x, x, bc(tmv[:, 2, c, 32 * d:32 * d + 8].unsqueeze(2), [P, 8, 64]),
                                            ALU.mult).then_inc(*S("xdd").one)
                    pend[0] = (d, c, nxt, et)
            dve.wait_ge(*S("st_ps").next("dve"))
            add_state(dve, link, *pend[0])

        pend = [None]

        def add_state(dve, link, d, c, nxt, et):
            dst = heads8(hin[:, d, nxt, :])
            link(nc.vector.tensor_tensor(dst, heads8(hin[:, d, c, :]),
                                         bc(et[:, c, 32 * d:32 * d + 8].unsqueeze(2), [P, 8, 64]), ALU.mult))
            link(nc.vector.tensor_tensor(hin[:, d, nxt, :], hin[:, d, nxt, :], ps[:, 0, :], ALU.add))

        def pe_states(pe):
            order = ((0, 1, 2, 3), (1, 0, 3, 2))
            for step in range(NMC - 1):
                for d in range(2):
                    c = order[d][step]
                    pe.wait_ge(*S("xdd").next("pe"))
                    for g in range(2):
                        last = nc.tensor.matmul(ps[:, 0, g * 256:(g + 1) * 256], btm[:, c, g, :],
                                                xdt[:, 0, g * 256:(g + 1) * 256], start=True, stop=True)
                    last.then_inc(*S("st_ps").one)

        STEPS = [(c, g) for c in range(NMC) for g in range(2)]

        def h4(ap):
            return ap.rearrange("p (h t) -> p h t", h=4)

        def dve_ssd(dve, link):
            y_pe = S("y_pe").sem
            for n, (c, g) in enumerate(STEPS):
                cs = slice(c * MC, (c + 1) * MC)
                gb, db = (1, 2) if n % 2 == 0 else (5, 6)
                dve.wait_ge(*S("g_ps").next("dve"))
                link(nc.vector.tensor_tensor(gm[:], bc(ps[:, gb, 0:P].unsqueeze(1), [P, 2, P]),
                                             cc("mssd").rearrange("p (d t) -> p d t", d=2), ALU.mult))
                if n >= 2:
                    dve.wait_ge(y_pe, n - 1)
                for d in range(2):
                    dve.wait_ge(*S("e1").next("dve"))
                    h0 = 32 * d + 4 * g
                    link(nc.vector.tensor_tensor(h4(cms[n % 2][:, d, :]), h4(e1s[d][:]),
                                                 bc(xc[:, 6 + g, cs].unsqueeze(1), [P, 4, MC]), ALU.mult))
                    link(nc.vector.tensor_tensor(h4(dds[d][:]), h4(ps[:, db + d, :]),
                                                 bc(tmv[:, 1, c, h0:h0 + 4].unsqueeze(2), [P, 4, MC]), ALU.subtract))
                    nc.vector.tensor_scalar(dds[d][:], dds[d][:], 0.0, None, ALU.min).then_inc(*S("dd").one)
                if g == 0:
                    if c:
                        dve.wait_ge(y_pe, n)
                    for d in range(2):
                        link(nc.vector.tensor_tensor(heads8(xdt[:, d, :]), heads8(xtm[:, c, :]),
                                                     bc(tmv[:, 0, c, 32 * d:32 * d + 8].unsqueeze(2), [P, 8, 64]),
                                                     ALU.mult))
                for d in range(2):
                    dve.wait_ge(*S("e2").next("dve"))
                    nc.vector.tensor_tensor(h4(wms[n % 2][:, d, :]), h4(e1s[d][:]),
                                            bc(gm[:, d, :].unsqueeze(1), [P, 4, MC]), ALU.mult
                                            ).then_inc(*S("wm").one)
                dve.wait_ge(*S("wm").next("dve", 2))
            dve.wait_ge(y_pe, len(STEPS))

        def act_ssd(act):
            def y_out(c):
                act.wait_ge(S("y_pe").sem, 2 * c + 2)
                nc.scalar.activation(o0[:, 4:8, c * MC:(c + 1) * MC],
                                     ps[:, 4, :].rearrange("p (i t) -> p i t", i=4), ACT.Copy
                                     ).then_inc(*S("y_sb").one)
            for n, (c, g) in enumerate(STEPS):
                db = 2 if n % 2 == 0 else 6
                for d in range(2):
                    act.wait_ge(*S("bc_ps").next("act"))
                    if n:
                        act.wait_ge(*S("wm").next("act"))
                    nc.scalar.activation(e1s[d][:], ps[:, db + d, :], ACT.Exp).then_inc(*S("e1").one)
                for d in range(2):
                    act.wait_ge(*S("dd").next("act"))
                    nc.scalar.activation(e1s[d][:], dds[d][:], ACT.Exp).then_inc(*S("e2").one)
                if g == 0 and c:
                    y_out(c - 1)
            y_out(NMC - 1)
            act.wait_ge(*S("wm").next("act", 2))
            for i in range(4):
                last = nc.scalar.activation(zg[:, i, :], zg[:, i, :], ACT.Silu)
            last.then_inc(*S("zg_act").one)

        def pe_ssd(pe):
            def prepare(n):
                c, g = STEPS[n]
                cs = slice(c * MC, (c + 1) * MC)
                gb, db = (1, 2) if n % 2 == 0 else (5, 6)
                nc.tensor.matmul(ps[:, gb, 0:P], xc[:, 4 + g, cs], xc[:, 6 + g, cs], start=True, stop=True
                                 ).then_inc(*S("g_ps").one)
                for d in range(2):
                    for h in range(4):
                        j = 32 * d + 4 * g + h
                        last = nc.tensor.matmul(ps[:, db + d, h * MC:(h + 1) * MC],
                                                ident[0:DT, j:j + 1].broadcast_to([DT, P]), dw[0:DT, cs],
                                                start=True, stop=True)
                    last.then_inc(*S("bc_ps").one)
            prepare(0)
            for n, (c, g) in enumerate(STEPS):
                if n + 1 < len(STEPS):
                    prepare(n + 1)
                pe.wait_ge(*S("wm").next("pe", 2))
                if g == 0 and c:
                    pe.wait_ge(*S("y_sb").next("pe"))
                for h in range(4):
                    hh = 4 * g + h
                    out = ps[64 * (hh % 2):64 * (hh % 2) + 64, 4, (hh // 2) * MC:(hh // 2 + 1) * MC]
                    for d in range(2):
                        nc.tensor.matmul(out, xdt[:, d, hh * 64:(hh + 1) * 64],
                                         wms[n % 2][:, d, h * MC:(h + 1) * MC], start=(d == 0), stop=False)
                        last = nc.tensor.matmul(out, hin[:, d, c, hh * 64:(hh + 1) * 64],
                                                cms[n % 2][:, d, h * MC:(h + 1) * MC], start=False, stop=(d == 1))
                last.then_inc(*S("y_pe").one)

        def dve_mbout(dve, link):
            dve.wait_ge(*S("y_sb").next("dve", 4))
            dve.wait_ge(*S("zg_act").next("dve"))
            for i in range(4):
                y = o0[:, 4 + i, :]
                link(nc.vector.scalar_tensor_tensor(y, xc[:, i, :], pc("mbd", i, 1), y, ALU.mult, ALU.add))
                link(nc.vector.tensor_tensor(y, y, zg[:, i, :], ALU.mult))
                link(nc.vector.tensor_tensor(zg[:, i, :], y, y, ALU.mult))
            dve.sem_inc(S("mb_sq").sem, 1)
            dve.wait_ge(*S("mb_ss").next("dve"))
            for g in range(2):
                link(nc.vector.tensor_scalar(zg[:, g, :], ps[:, 2 + g, :], 1.0 / 256, EPS, ALU.mult, ALU.add))
            dve.sem_inc(S("mb_ms").sem, 1)
            dve.wait_ge(*S("mb_rt").next("dve"))
            link(nc.vector.reciprocal(zg[:, 0:2, :], zg[:, 0:2, :]))
            for i in range(4):
                y = o0[:, 4 + i, :]
                link(nc.vector.scalar_tensor_tensor(y, y, pc("mbn", i, 1), zg[:, i // 2, :], ALU.mult, ALU.mult))

        def pe_mbout(pe):
            pe.wait_ge(*S("mb_sq").next("pe"))
            for g in range(2):
                for i in range(2):
                    last = nc.tensor.matmul(ps[:, 2 + g, :], ones[:], zg[:, 2 * g + i, :],
                                            start=(i == 0), stop=(i == 1))
            last.then_inc(*S("mb_ss").one)

        def act_mbout(act):
            act.wait_ge(*S("mb_ms").next("act"))
            nc.scalar.activation(zg[:, 0:2, :], zg[:, 0:2, :], ACT.Sqrt).then_inc(*S("mb_rt").one)

        ar, bt, kt, _ = lay(area, [("ar", [P, 2, 4, NRC, 2, RC]), ("bt", [P, 2, 4, SEG]), ("kt", [P, 2, 4, SEG])])
        bon, st, dls, t0_ = lay(zx_at, [
            ("bon", [P, 4, SEG]), ("st", [P, 2, 4, RC]), ("dls", [P, 2, 4, NRC])])
        lora, gup, t0_ = lay(t0_, [("lora", [P, 512]), ("gup", [P, 512])])
        kn, ld, cu, ic, ee, bs, _r = lay(t0_, [(n, [P, 4, SEG]) for n in ("kn", "ld", "cu", "ic", "ee", "bs")])
        assert _r <= ob, (_r, ob)
        br, kr, tt, xs, nl, btt, ktt, vtt, rh, uu, _r = lay(t0_, [
            ("br", [P, 2, 4, P]), ("kr", [P, 2, 4, P]), ("tt", [P, 2, 2, 4, RC]),
            ("xs", [P, 2, 4, RC]), ("nl", [P, 2, 2, 4, RC]), ("btt", [P, 2, 4, RC]),
            ("ktt", [P, 2, 4, RC]), ("vtt", [P, 2, 4, RC]), ("rh", [P, 2, 4, RC]), ("uu", [P, 2, 4, RC])])
        yb = sb("yb", [P, 4, SEG], at=_r)
        assert _r <= ob - 4 * SEG * 4

        def zseg(i, seg, rows=slice(0, P)):
            return zrw[rows, i, seg, 2:258]

        ptmp = sb("ptmp", [P, 2, SEG], at=_m)
        assert _m + 2 * SEG * 4 <= ob

        def pool_shift(pool):
            link = Chain(pool, "pool_chain")
            pool.wait_ge(act_evac.sem, RING + 27)
            for sl in (slice(0, 2), slice(258, 260)):
                link(nc.gpsimd.memset(zrw[:, :, :, sl], 0.0))
            link(nc.gpsimd.tensor_tensor(c0[:], pc("mu_p"), pc("mu_n"), ALU.add))
            link(nc.gpsimd.tensor_scalar(c0[:], c0[:], -1.0, 1.0, ALU.mult, ALU.add))
            for seg in (CTX, LAT):
                for i in range(14):
                    z, total, term = zrw[:, i, seg, :], ptmp[:, 0, :], ptmp[:, 1, :]
                    link(nc.gpsimd.tensor_scalar(total, z[:, 2:258], c0[:, i:i + 1], None, ALU.mult))
                    link(nc.gpsimd.tensor_scalar(term, z[:, 1:257], pc("mu_p", i, 1), None, ALU.mult))
                    link(nc.gpsimd.tensor_tensor(total, total, term, ALU.add))
                    link(nc.gpsimd.tensor_scalar(term, z[:, 3:259], pc("mu_n", i, 1), None, ALU.mult))
                    link(nc.gpsimd.tensor_tensor(z[:, 2:258], total, term, ALU.add))
            pool.sem_inc(S("z_shifted").sem, 1)

        c0 = sb("c0", [P, 14], at=END - 64)

        def fl(ap):
            return ap.rearrange("p m t -> p (m t)")

        def dve_rwprep(dve, link, seg):
            if seg == 0:
                dve.wait_ge(*S("z_shifted").next("dve"))
                link(nc.vector.memset(st[:], 0.0))
            dve.sem_inc(S("lw_in").sem, 1)
            zr, zk, zv = (zseg(slice(4 * q, 4 * q + 4), seg) for q in range(3))
            par4 = lambda n, i=0: bc(pc(n, i, 4).unsqueeze(2), [P, 4, SEG])
            link(nc.vector.tensor_tensor(kn[:], zk, par4("kk"), ALU.mult))
            link(nc.vector.tensor_tensor(ee[:], kn[:], kn[:], ALU.mult))
            dve.sem_inc(S("kk_sq").sem, 1)
            dve.wait_ge(*S("kk_rt").next("dve"))
            link(nc.vector.tensor_scalar(fl(ee[:]), fl(ee[:]), 1e-12, None, ALU.max))
            link(nc.vector.reciprocal(ee[:], ee[:]))
            link(nc.vector.tensor_tensor(kn[:], kn[:], ee[:], ALU.mult))
            flc = lambda a: a.rearrange("p m (c l) -> p (m c) l", l=RC)
            for d in range(2):
                dve.wait_ge(*S("wa_sig").next("dve"))
                link(nc.vector.tensor_scalar(fl(ld[:]), fl(ld[:]), -E05, None, ALU.mult))
                link(nc.vector.tensor_tensor_scan(fl(cu[:]), cc("scan64"), fl(ld[:]), 0.0, ALU.mult, ALU.add))
                tot = flc(cu[:])[:, :, RC - 1:RC]
                link(nc.vector.tensor_copy(dls[:, d, :, :].rearrange("p m c -> p (m c)"),
                                           tot.rearrange("p a o -> p (a o)")))
                if d == 0:
                    link(nc.vector.tensor_tensor(fl(ld[:]), fl(cu[:]), fl(ld[:]), ALU.subtract))
                    inc, exc = cu, ld
                else:
                    link(nc.vector.tensor_tensor(flc(ee[:]), bc(tot, [P, 16, RC]), flc(cu[:]), ALU.subtract))
                    link(nc.vector.tensor_tensor(ld[:], ee[:], ld[:], ALU.add))
                    link(nc.vector.tensor_copy(cu[:], ee[:]))
                    inc, exc = ld, cu
                dve.sem_inc(S("rw_dec").sem, 1)
                dve.wait_ge(*S("rw_exp").next("dve"))
                for m in range(4):
                    link(nc.vector.scalar_tensor_tensor(
                        ar[:, d, m, :, 0, :], kn[:, m, :].rearrange("p (c l) -> p c l", l=RC), -1.0,
                        exc[:, m, :].rearrange("p (c l) -> p c l", l=RC), ALU.mult, ALU.mult))
                    link(nc.vector.tensor_tensor(ar[:, d, m, :, 1, :], zr[:, m, :].rearrange("p (c l) -> p c l", l=RC),
                                                 ee[:, m, :].rearrange("p (c l) -> p c l", l=RC), ALU.mult))
                link(nc.vector.tensor_tensor(ee[:], kn[:], ic[:], ALU.mult))
                link(nc.vector.tensor_tensor(bt[:, d, :, :], ee[:], inc[:], ALU.mult))
                for m in range(4):
                    link(nc.vector.tensor_scalar(ic[:, m, :], ic[:, m, :], -1.0, pc("ka", m, 1), ALU.add, ALU.mult))
                link(nc.vector.scalar_tensor_tensor(ic[:], ic[:], 1.0, zk, ALU.add, ALU.mult))
                link(nc.vector.tensor_tensor(kt[:, d, :, :], ic[:], inc[:], ALU.mult))
                if d == 0:
                    link(nc.vector.tensor_tensor(bs[:], ic[:], par4("rk", 0), ALU.mult))
                else:
                    link(nc.vector.tensor_tensor(ic[:], ic[:], par4("rk", 4), ALU.mult))
                    link(nc.vector.tensor_tensor(bs[:], bs[:], ic[:], ALU.add))
                dve.sem_inc(S("wa_free").sem, 1)
            nc.vector.tensor_tensor(bs[:], bs[:], zr, ALU.mult).then_inc(*S("bon_in").one)
            dve.wait_ge(*S("bon_ps").next("dve"))
            dve.wait_ge(*S("bon_in").next("dve"))
            for b_ in range(2):
                link(nc.vector.tensor_tensor(bon[:, 2 * b_:2 * b_ + 2, :],
                                             ps[:, b_, :].rearrange("p (m t) -> p m t", m=2),
                                             zv[:, 2 * b_:2 * b_ + 2, :], ALU.mult))
            dve.sem_inc(S("rw_prep").sem, 1)

        def act_rwprep(act, seg):
            act.wait_ge(*S("lw_in").next("act"))
            w = zseg(12, seg, slice(0, 64))
            nc.scalar.activation(w, w, ACT.Tanh).then_inc(*S("lw_act").one)
            nc.scalar.activation(zseg(13, seg), zseg(13, seg), ACT.Sigmoid).then_inc(*S("lw_act").one)
            act.wait_ge(*S("kk_ps").next("act"))
            for b_ in range(2):
                last = nc.scalar.activation(fl(ee[:, 2 * b_:2 * b_ + 2, :]), ps[:, b_, :], ACT.Sqrt)
            last.then_inc(*S("kk_rt").one)
            for d in range(2):
                act.wait_ge(*S("wa_ps").next("act"))
                if d:
                    act.wait_ge(*S("wa_free").next("act"))
                for m in range(4):
                    cs = slice((m % 2) * SEG, (m % 2 + 1) * SEG)
                    nc.scalar.activation(ld[:, m, :], ps[:, 4 + m // 2, cs], ACT.Sigmoid, bias=pc("w0", 4 * d + m, 1))
                    last = nc.scalar.activation(ic[:, m, :], ps[:, 6 + m // 2, cs], ACT.Sigmoid,
                                                bias=pc("a0", 4 * d + m, 1))
                last.then_inc(*S("wa_sig").one)
                act.wait_ge(*S("rw_dec").next("act"))
                inc, exc = (cu, ld) if d == 0 else (ld, cu)
                nc.scalar.activation(ee[:], inc[:], ACT.Exp)
                nc.scalar.activation(exc[:], exc[:], ACT.Exp)
                nc.scalar.activation(dls[:, d, :, :], dls[:, d, :, :], ACT.Exp).then_inc(*S("rw_e").one)
                act.wait_ge(*S("rw_e").next("act"))
                nc.scalar.activation(inc[:], inc[:], ACT.Exp, scale=-1.0).then_inc(*S("rw_exp").one)
            act.wait_ge(*S("wa_free").next("act"))

        def pe_rwprep(pe, seg):
            if seg == 0:
                pe.wait_ge(S("lora").sem, 32)
            pe.wait_ge(*S("kk_sq").next("pe"))
            for b_ in range(2):
                last = nc.tensor.matmul(ps[:, b_, :], bones[:], fl(ee[:, 2 * b_:2 * b_ + 2, :]), start=True, stop=True)
            last.then_inc(*S("kk_ps").one)
            pe.wait_ge(*S("lw_act").next("pe", 2))
            for d in range(2):
                if d:
                    pe.wait_ge(*S("wa_sig").next("pe"))
                for m in range(4):
                    cs = slice((m % 2) * SEG, (m % 2 + 1) * SEG)
                    for q in range(2):
                        rows = slice(64 * q + 32 * d, 64 * q + 32 * d + 32)
                        last = nc.tensor.matmul(ps[:, 4 + 2 * q + m // 2, cs], lora[rows, m * P:(m + 1) * P],
                                                zseg(12, seg, rows), start=True, stop=True)
                last.then_inc(*S("wa_ps").one)
            pe.wait_ge(*S("wa_sig").next("pe"))
            pe.wait_ge(*S("bon_in").next("pe"))
            for b_ in range(2):
                last = nc.tensor.matmul(ps[:, b_, :], bones[:], fl(bs[:, 2 * b_:2 * b_ + 2, :]), start=True, stop=True)
            last.then_inc(*S("bon_ps").one)

        def hp(e):
            return slice(64 * e, 64 * e + 64)

        def pairs(fn):
            for d in range(2):
                for m in range(4):
                    for e in range(2):
                        last = fn(d, m, e)
            return last

        def heads_of(d, fn):
            for m in range(4):
                for e in range(2):
                    last = fn(d, m, e)
            return last

        def col(m, half=0):
            return slice((half * 4 + m) * RC, (half * 4 + m + 1) * RC)

        def pe_solve(pe, seg, n):
            ch = (n, NRC - 1 - n)
            cs = [slice(c * RC, (c + 1) * RC) for c in ch]
            if n == 0:
                pe.wait_ge(*S("rw_prep").next("pe"))
            for d in range(2):
                if n > 0:
                    pe.wait_ge(*S("st_done").next("pe"))
                both = lambda d, m, e: ar[hp(e), d, m, ch[d], :, :].rearrange("p q l -> p (q l)")
                heads_of(d, lambda d, m, e: nc.tensor.matmul(
                    ps[hp(e), d, m * P:(m + 1) * P], bt[hp(e), d, m, cs[d]], both(d, m, e), start=True, stop=True))
                heads_of(d, lambda d, m, e: nc.tensor.matmul(
                    ps[hp(e), 2 + d, m * P:(m + 1) * P], kt[hp(e), d, m, cs[d]], both(d, m, e), start=True, stop=True))
                heads_of(d, lambda d, m, e: nc.tensor.matmul(
                    ps[hp(e), 4 + d, col(m)], ar[hp(e), d, m, ch[d], 0, :], bt[hp(e), d, m, cs[d]],
                    start=True, stop=True)).then_inc(*S("n_ps").one)
            for b_, src in ((6, bt), (7, kt)):
                pairs(lambda d, m, e: nc.tensor.matmul(ps[hp(e), b_, col(m, d)], src[hp(e), d, m, cs[d]],
                                                       ident[hp(e), hp(e)], start=True, stop=True)
                      ).then_inc(*S("bkv_ps").one)
            pe.wait_ge(*S("tm_sb").next("pe"))
            pairs(lambda d, m, e: nc.tensor.matmul(ps[hp(e), 6, col(m, d)], zseg(8 + m, seg, hp(e))[:, cs[d]],
                                                   ident[hp(e), hp(e)], start=True, stop=True)
                  ).then_inc(*S("bkv_ps").one)
            for lv in range(RLEV):
                for d in range(2):
                    pe.wait_ge(*S("lv_in").next("pe"))
                    heads_of(d, lambda d, m, e: nc.tensor.matmul(ps[hp(e), d, col(m)], nl[hp(e), lv % 2, d, m, :],
                                                                 tt[hp(e), d, 0, m, :], start=True, stop=True)
                             ).then_inc(*S("x_ps").one)
                for d in range(2):
                    pe.wait_ge(*S("x_sb").next("pe"))
                    if lv < RLEV - 1:
                        heads_of(d, lambda d, m, e: nc.tensor.matmul(
                            ps[hp(e), 2 + d, col(m)], tt[hp(e), d, 1, m, :], xs[hp(e), d, m, :],
                            start=True, stop=True))
                    heads_of(d, lambda d, m, e: nc.tensor.matmul(
                        ps[hp(e), 2 + d, col(m, 1)], xs[hp(e), d, m, :], tt[hp(e), d, 1, m, :],
                        start=True, stop=True)).then_inc(*S("t_ps").one)
            pe.wait_ge(*S("tm_sb").next("pe", 2))

            def rhs(d, m, e):
                nc.tensor.matmul(ps[hp(e), 4 + d, col(m)], ar[hp(e), d, m, ch[d], 0, :], st[hp(e), d, m, :],
                                 start=True, stop=False)
                return nc.tensor.matmul(ps[hp(e), 4 + d, col(m)], kr[hp(e), d, m, 0:RC], vtt[hp(e), d, m, :],
                                        start=False, stop=True)
            for d in range(2):
                heads_of(d, rhs).then_inc(*S("rh_ps").one)
            for d in range(2):
                pe.wait_ge(*S("tT_done").next("pe"))
                pe.wait_ge(*S("rh_sb").next("pe"))
                heads_of(d, lambda d, m, e: nc.tensor.matmul(ps[hp(e), 6 + d, col(m)], tt[hp(e), d, 1, m, :],
                                                             rh[hp(e), d, m, :], start=True, stop=True)
                         ).then_inc(*S("u_ps").one)

            def yy(d, m, e):
                o = ps[hp(e), d, col(m)]
                nc.tensor.matmul(o, st[hp(e), d, m, :], ar[hp(e), d, m, ch[d], 1, :], start=True, stop=False)
                nc.tensor.matmul(o, uu[hp(e), d, m, :], br[hp(e), d, m, RC:2 * RC], start=False, stop=False)
                return nc.tensor.matmul(o, vtt[hp(e), d, m, :], kr[hp(e), d, m, RC:2 * RC], start=False, stop=True)

            def ss(d, m, e):
                o = ps[hp(e), 2 + d, col(m)]
                nc.tensor.matmul(o, btt[hp(e), d, m, :], uu[hp(e), d, m, :], start=True, stop=False)
                return nc.tensor.matmul(o, ktt[hp(e), d, m, :], vtt[hp(e), d, m, :], start=False, stop=True)
            for d in range(2):
                pe.wait_ge(*S("u_sb").next("pe"))
                heads_of(d, yy).then_inc(*S("yr_ps").one)
                heads_of(d, ss).then_inc(*S("s_ps").one)

        def bank(i, half=0, n=4):
            return ps[:, i, half * 256:half * 256 + n * RC].rearrange("p (m l) -> p m l", l=RC)

        def act_solve(act, n):
            for dst, b_ in ((btt, 6), (ktt, 7), (vtt, 6)):
                act.wait_ge(*S("bkv_ps").next("act"))
                nc.scalar.activation(dst[:].rearrange("p d m l -> p (d m l)"), ps[:, b_, :], ACT.Copy
                                     ).then_inc(*S("tm_sb").one)
            for lv in range(RLEV):
                for d in range(2):
                    act.wait_ge(*S("x_ps").next("act"))
                    nc.scalar.activation(xs[:, d, :, :], bank(d), ACT.Copy).then_inc(*S("x_sb").one)
            for d in range(2):
                act.wait_ge(*S("rh_ps").next("act"))
                nc.scalar.activation(rh[:, d, :, :], bank(4 + d), ACT.Copy).then_inc(*S("rh_sb").one)
            for d in range(2):
                act.wait_ge(*S("u_ps").next("act"))
                nc.scalar.activation(uu[:, d, :, :], bank(6 + d), ACT.Copy).then_inc(*S("u_sb").one)

        def dve_solve(dve, link, seg, n):
            ch = (n, NRC - 1 - n)
            lvm = cc("lv").rearrange("p (s v d l) -> p s v d l", s=2, v=RLEV + 1, d=2)
            mx = cc("mx").rearrange("p (d l) -> p d l", d=2)
            e4 = bc(cc("i64").unsqueeze(1), [P, 4, RC])

            def mask_n(lv, d):
                return nc.vector.tensor_tensor(nl[:, lv % 2, d, :, :], br[:, d, :, 0:RC],
                                               bc(lvm[:, 1, lv + 1, d, :].unsqueeze(1), [P, 4, RC]), ALU.mult)
            for d in range(2):
                dve.wait_ge(*S("n_ps").next("dve"))
                b4 = lambda i: ps[:, i, :].rearrange("p (m l) -> p m l", m=4)
                link(nc.vector.tensor_tensor(br[:, d, :, :], b4(d), bc(mx[:, d, :].unsqueeze(1), [P, 4, P]), ALU.mult))
                link(nc.vector.tensor_tensor(tt[:, d, 0, :, :], bank(4 + d),
                                             bc(lvm[:, 0, 0, d, :].unsqueeze(1), [P, 4, RC]), ALU.mult))
                link(nc.vector.tensor_tensor(tt[:, d, 0, :, :], tt[:, d, 0, :, :], e4, ALU.add))
                link(nc.vector.tensor_tensor(tt[:, d, 1, :, :], br[:, d, :, 0:RC],
                                             bc(lvm[:, 1, 0, d, :].unsqueeze(1), [P, 4, RC]), ALU.mult))
                link(nc.vector.tensor_tensor(tt[:, d, 1, :, :], tt[:, d, 1, :, :], e4, ALU.add))
                link(nc.vector.tensor_tensor(kr[:, d, :, :], b4(2 + d), bc(mx[:, d, :].unsqueeze(1), [P, 4, P]),
                                             ALU.mult))
                link(mask_n(0, d))
                dve.sem_inc(S("lv_in").sem, 1)
            for lv in range(RLEV):
                if lv < RLEV - 1:
                    for d in range(2):
                        link(mask_n(lv + 1, d))
                for d in range(2):
                    dve.wait_ge(*S("t_ps").next("dve"))
                    if lv < RLEV - 1:
                        t2_ = tt[:, d, :, :, :].rearrange("p s m l -> p (s m) l")
                        link(nc.vector.tensor_tensor(t2_, t2_, bank(2 + d, 0, 8), ALU.add))
                        dve.sem_inc(S("lv_in").sem, 1)
                    else:
                        nc.vector.tensor_tensor(tt[:, d, 1, :, :], tt[:, d, 1, :, :], bank(2 + d, 1), ALU.add
                                                ).then_inc(*S("tT_done").one)
            for d in range(2):
                dve.wait_ge(*S("yr_ps").next("dve"))
                c = ch[d]
                if d == 0:
                    dst = o0[:, 0:4, seg * SEG + c * RC:seg * SEG + (c + 1) * RC]
                else:
                    dst = yb[:, :, c * RC:(c + 1) * RC]
                link(nc.vector.tensor_copy(dst, bank(d)))
                dve.wait_ge(*S("s_ps").next("dve"))
                link(nc.vector.tensor_tensor(st[:, d, :, :], st[:, d, :, :], bank(2 + d), ALU.add))
                link(nc.vector.tensor_tensor(st[:, d, :, :], st[:, d, :, :],
                                             bc(dls[:, d, :, ch[d]:ch[d] + 1], [P, 4, RC]), ALU.mult))
                dve.sem_inc(S("st_done").sem, 1)

        def dve_rwout(dve, link, seg):
            y = o0[:, 0:4, seg_cols(seg)]
            link(nc.vector.tensor_tensor(yb[:], yb[:], y, ALU.add))
            dve.sem_inc(S("ln_in").sem, 1)
            dve.wait_ge(*S("ln_mu").next("dve"))
            for b_ in range(2):
                v = fl(yb[:, 2 * b_:2 * b_ + 2, :])
                link(nc.vector.scalar_tensor_tensor(v, ps[:, b_, :], -1.0 / 64, v, ALU.mult, ALU.add))
            link(nc.vector.tensor_tensor(ee[:], yb[:], yb[:], ALU.mult))
            dve.sem_inc(S("ln_sq").sem, 1)
            dve.wait_ge(*S("ln_var").next("dve"))
            for b_ in range(2):
                link(nc.vector.tensor_scalar(fl(ee[:, 2 * b_:2 * b_ + 2, :]), ps[:, b_, :], 1.0 / 64, 64e-5,
                                             ALU.mult, ALU.add))
            dve.sem_inc(S("ln_ve").sem, 1)
            dve.wait_ge(*S("ln_rt").next("dve"))
            link(nc.vector.reciprocal(ee[:], ee[:]))
            link(nc.vector.tensor_tensor(yb[:], yb[:], ee[:], ALU.mult))
            for m in range(4):
                link(nc.vector.tensor_scalar(yb[:, m, :], yb[:, m, :], pc("gnw", m, 1), pc("gnb", m, 1),
                                             ALU.mult, ALU.add))
            link(nc.vector.tensor_tensor(yb[:], yb[:], bon[:], ALU.add))
            dve.wait_ge(*S("gate_ps").next("dve"))
            for m in range(4):
                link(nc.vector.tensor_tensor(y[:, m, :], yb[:, m, :],
                                             ps[:, 2 + m // 2, (m % 2) * SEG:(m % 2 + 1) * SEG], ALU.mult))

        def pe_rwout(pe, seg):
            pe.wait_ge(*S("st_done").next("pe", 2))
            for m in range(4):
                last = nc.tensor.matmul(ps[:, 2 + m // 2, (m % 2) * SEG:(m % 2 + 1) * SEG], gup[:, m * P:(m + 1) * P],
                                        zseg(13, seg), start=True, stop=True)
            last.then_inc(*S("gate_ps").one)
            for a, src, b in (("ln_in", yb, "ln_mu"), ("ln_sq", ee, "ln_var")):
                pe.wait_ge(*S(a).next("pe"))
                for b_ in range(2):
                    last = nc.tensor.matmul(ps[:, b_, :], bones[:], fl(src[:, 2 * b_:2 * b_ + 2, :]),
                                            start=True, stop=True)
                last.then_inc(*S(b).one)

        def act_rwout(act, seg):
            act.wait_ge(*S("ln_ve").next("act"))
            nc.scalar.activation(ee[:], ee[:], ACT.Sqrt).then_inc(*S("ln_rt").one)

        def act_osplit(act, src, cols):
            act.wait_ge(*S("o_ready").next("act"))
            nc.scalar.activation(a_hi[:, :, cols], src, ACT.Copy).then_inc(*S("ohi").one)

        def dve_osplit(dve, src, cols):
            dve.sem_inc(S("o_ready").sem, 1)
            dve.wait_ge(*S("ohi").next("dve"))
            nc.vector.tensor_tensor(a_lo[:, :, cols], src, a_hi[:, :, cols].bitcast(F32),
                                    ALU.subtract).then_inc(*S("alo_ready").one)
            dve.wait_ge(*S("alo_ready").next("dve"))

        NH = 16
        qT, kT, vT, bia, sS, pP, pT, mxv, nmx, sm, rc_, oA, _r = lay(arena + 8192, [
            ("qT", [P, 8, SEG]), ("kT", [P, 8, T2]), ("vT", [P, 4, D]), ("bia", [P, NH, 512]),
            ("sS", [P, 2, 512]), ("pP", [P, 2, 512]), ("pT", [P, 2, 512]), ("mxv", [P, 32]), ("nmx", [P, 32]),
            ("sm", [P, 32]), ("rc_", [P, 32]), ("oA", [P, 8, SEG])])
        assert _r <= END - 64

        def pool_bias(pool):
            pool.wait_ge(*S("arena_free").next("pool"))
            pool.dma_start(bia[:], io["bias"]).then_inc(*S("bias").dma)

        def pe_qkv(pe):
            pe.wait_ge(*S("alo_ready").next("pe", 2))
            pe_gemm(pe, BASE["qkv"], 8, "act", None, lambda b: [(ps[:, b, 0:SEG], True, a_cols([LAT]))])
            pe_gemm(pe, BASE["qkv"] + 8, 8, "act", None, lambda b: [(ps[:, b, :], True, a_cols([CTX, LAT]))])
            pe_gemm(pe, BASE["qkv"] + 16, 8, "act", None, lambda b: tok_major(b, 0, 4))

        def tok_major(b, first, n):
            def group(tt):
                c = slice((first + tt) * P, (first + tt + 1) * P)
                return (ps[:, b, tt * P:(tt + 1) * P], False, lambda k: (a_hi[:, k, c], a_lo[:, k, c]))
            return [group(tt) for tt in range(n)]

        def act_copies(act, base, runs):
            first = 0
            for n, dst, src in runs:
                def after(t, slot, dst=dst, src=src, first=first):
                    act.wait_ge(tile_used.sem, used(base, t))
                    nc.scalar.activation(dst(t - first), src(5 + slot), ACT.Copy).then_inc(act_evac.sem, 1)
                run_tiles(act, "act", base, n, t0=first, after=after)
                first += n

        def flat1(ap):
            return ap.rearrange("p o t -> p (o t)")

        def dyn(t, n):
            return slice(t * n, t * n + n) if isinstance(t, int) else bass.ds(t * n, n)

        def act_qkv(act):
            act_copies(act, BASE["qkv"], [
                (8, lambda t: flat1(qT[:, one(t), :]), lambda b: ps[:, b, 0:SEG]),
                (8, lambda t: flat1(kT[:, one(t), :]), lambda b: ps[:, b, :]),
                (8, lambda t: vT[:, :, dyn(t, P)], lambda b: ps[:, b, :].rearrange("p (a c) -> p a c", a=4))])

        def sbank(u):
            return (0, 1, 6)[u % 3]

        def pe_attn(pe, evac0):
            pe.wait_ge(act_evac.sem, evac0)

            def scores(u):
                h, qt = u // 2, u % 2
                if u >= 3:
                    pe.wait_ge(*S("sc_read").next("pe"))
                nc.tensor.matmul(ps[:, sbank(u), :], qT[hp(h % 2), h // 2, qt * P:(qt + 1) * P],
                                 kT[hp(h % 2), h // 2, :], start=True, stop=True).then_inc(*S("sc_ps").one)

            def transposes(u):
                pe.wait_ge(*S("p_ready").next("pe"))
                for kt_ in range(4):
                    last = nc.tensor.transpose(ps[:, 2 + u % 2, kt_ * P:(kt_ + 1) * P],
                                               pP[:, u % 2, kt_ * P:(kt_ + 1) * P], ident[:])
                last.then_inc(*S("pT_ps").one)

            def values(u):
                h, qt = u // 2, u % 2
                pe.wait_ge(*S("pT_sb").next("pe"))
                if u % 4 == 0 and u >= 8:
                    pe.wait_ge(*S("at_sb").next("pe"))
                m = h // 2
                for kt_ in range(4):
                    last = nc.tensor.matmul(ps[hp(h % 2), 4 + m % 2, qt * P:(qt + 1) * P],
                                            vT[:, kt_, h * 64:(h + 1) * 64], pT[:, u % 2, kt_ * P:(kt_ + 1) * P],
                                            start=(kt_ == 0), stop=(kt_ == 3))
                last.then_inc(*S("at_ps").one)
            scores(0)
            scores(1)
            for u in range(2 * NH):
                if u + 2 < 2 * NH:
                    scores(u + 2)
                transposes(u)
                if u >= 1:
                    values(u - 1)
            values(2 * NH - 1)
            pe.wait_ge(*S("sc_read").next("pe", 3))
            pe.wait_ge(*S("at_sb").next("pe", 2))

        def dve_attn(dve, link):
            dve.wait_ge(S("bias").sem, 16)

            def soft(u):
                h, qt = u // 2, u % 2
                dve.wait_ge(*S("sc_ps").next("dve"))
                link(nc.vector.tensor_scalar(sS[:, u % 2, 0:SEG], ps[:, sbank(u), 0:SEG], 0.125, None, ALU.mult))
                nc.vector.scalar_tensor_tensor(sS[:, u % 2, SEG:T2], ps[:, sbank(u), SEG:T2], 0.125,
                                               bia[:, h, qt * 256:(qt + 1) * 256], ALU.mult, ALU.add
                                               ).then_inc(*S("sc_read").one)
                dve.wait_ge(*S("sc_read").next("dve"))
                link(nc.vector.tensor_reduce(mxv[:, u:u + 1], sS[:, u % 2, :], AX.X, ALU.max))
                nc.vector.tensor_scalar(nmx[:, u:u + 1], mxv[:, u:u + 1], -1.0, None, ALU.mult
                                        ).then_inc(*S("nmx").one)

            def norm(u):
                dve.wait_ge(*S("exp_done").next("dve"))
                link(nc.vector.reciprocal(rc_[:, u:u + 1], sm[:, u:u + 1]))
                nc.vector.tensor_scalar(pP[:, u % 2, :], pP[:, u % 2, :], rc_[:, u:u + 1], None, ALU.mult
                                        ).then_inc(*S("p_ready").one)

            def out(m):
                dve.wait_ge(*S("at_ps").next("dve", 4))
                nc.vector.tensor_copy(oA[:, m, :], ps[:, 4 + m % 2, 0:SEG]).then_inc(*S("at_sb").one)
            soft(0)
            for u in range(2 * NH):
                if u + 1 < 2 * NH:
                    soft(u + 1)
                norm(u)
                if u % 4 == 1 and u >= 5:
                    out(u // 4 - 1)
            out(KT - 1)
            dve.wait_ge(*S("at_sb").next("dve", 8))

        def act_attn(act):
            def ex(u):
                act.wait_ge(*S("nmx").next("act"))
                nc.scalar.activation(pP[:, u % 2, :], sS[:, u % 2, :], ACT.Exp, bias=nmx[:, u:u + 1],
                                     accum_out=sm[:, u:u + 1]).then_inc(*S("exp_done").one)

            def cp(u):
                act.wait_ge(*S("pT_ps").next("act"))
                if u >= 2:
                    act.wait_ge(*S("at_ps").next("act"))
                nc.scalar.activation(pT[:, u % 2, :], ps[:, 2 + u % 2, :], ACT.Copy).then_inc(*S("pT_sb").one)
            ex(0)
            for u in range(2 * NH):
                if u + 1 < 2 * NH:
                    ex(u + 1)
                cp(u)

        gate, lgt, t1, t2, oh1, oh2, wv, gr, _r = lay(arena + 8192, [
            ("gate", [P, NE, SEG]), ("lgt", [P, 2, NE]), ("t1", [P, 2, NE]), ("t2", [P, 2, NE]),
            ("oh1", [P, 2, NE]), ("oh2", [P, 2, NE]), ("wv", [P, 8]), ("gr", [P, SEG])])

        def pe_router(pe):
            for tt_ in range(2):
                for k in range(KT):
                    last = nc.tensor.matmul(ps[:, 5, tt_ * NE:(tt_ + 1) * NE], normw[:, k, tt_ * P:(tt_ + 1) * P],
                                            pc("rw", k * NE, NE), start=(k == 0), stop=(k == KT - 1))
            last.then_inc(*S("lg_ps").one)
            pe.wait_ge(*S("gates").next("pe"))
            for tt_ in range(2):
                last = nc.tensor.transpose(ps[0:NE, 6, tt_ * P:(tt_ + 1) * P], lgt[:, tt_, :], ident[:])
            last.then_inc(*S("gr_ps").one)
            pe.wait_ge(*S("gr_sb").next("pe"))
            for e in range(NE):
                last = nc.tensor.matmul(ps[:, e // 2, (e % 2) * SEG:(e % 2 + 1) * SEG],
                                        ident[0:NE, e:e + 1].broadcast_to([NE, P]), gr[0:NE, :], start=True, stop=True)
            last.then_inc(*S("gate_bc").one)
            pe.wait_ge(*S("gate_sb").next("pe"))

        def dve_router(dve, link):
            dve.wait_ge(*S("lg_ps").next("dve"))
            dve.wait_ge(S("conb").sem, 16)
            iota = conb[:, BCOL["iota"][0]:BCOL["iota"][1]].rearrange("p (a e) -> p a e", a=2)
            col = lambda i: wv[:, 2 * i:2 * i + 2].unsqueeze(2)
            b8 = lambda i: bc(col(i), [P, 2, NE])
            link(nc.vector.tensor_tensor(lgt[:], ps[:, 5, 0:16].rearrange("p (a e) -> p a e", a=2),
                                         bc(pc("rb").unsqueeze(1), [P, 2, NE]), ALU.add))
            for q, oh in enumerate((oh1, oh2)):
                link(nc.vector.tensor_reduce(wv[:, 2 * q:2 * q + 2], lgt[:], AX.X, ALU.max))
                link(nc.vector.tensor_tensor(t1[:], lgt[:], b8(q), ALU.is_equal))
                link(nc.vector.scalar_tensor_tensor(t1[:], t1[:], -100.0, iota, ALU.mult, ALU.add))
                link(nc.vector.tensor_reduce(wv[:, 4:6], t1[:], AX.X, ALU.min))
                link(nc.vector.tensor_tensor(oh[:], t1[:], b8(2), ALU.is_equal))
                if q == 0:
                    link(nc.vector.scalar_tensor_tensor(lgt[:], oh[:], -BIG, lgt[:], ALU.mult, ALU.add))
            link(nc.vector.tensor_tensor(wv[:, 4:6], wv[:, 2:4], wv[:, 0:2], ALU.subtract))
            dve.sem_inc(S("r_dif").sem, 1)
            dve.wait_ge(*S("r_exp").next("dve"))
            link(nc.vector.tensor_scalar(wv[:, 0:2], wv[:, 4:6], 1.0, None, ALU.add))
            link(nc.vector.reciprocal(wv[:, 0:2], wv[:, 0:2]))
            link(nc.vector.tensor_tensor(wv[:, 2:4], wv[:, 4:6], wv[:, 0:2], ALU.mult))
            link(nc.vector.tensor_tensor(oh1[:], oh1[:], b8(0), ALU.mult))
            link(nc.vector.tensor_tensor(oh2[:], oh2[:], b8(1), ALU.mult))
            nc.vector.tensor_tensor(lgt[:], oh1[:], oh2[:], ALU.add).then_inc(*S("gates").one)
            dve.wait_ge(*S("gr_ps").next("dve"))
            nc.vector.tensor_copy(gr[0:NE, :], ps[0:NE, 6, 0:SEG]).then_inc(*S("gr_sb").one)
            dve.wait_ge(*S("gate_bc").next("dve"))
            for e2 in range(4):
                last = nc.vector.tensor_copy(fl(gate[:, 2 * e2:2 * e2 + 2, :]), ps[:, e2, :])
                if e2 < 3:
                    link(last)
            last.then_inc(*S("gate_sb").one)
            dve.wait_ge(*S("gate_sb").next("dve"))

        def act_router(act):
            act.wait_ge(*S("r_dif").next("act"))
            nc.scalar.activation(wv[:, 4:6], wv[:, 4:6], ACT.Exp).then_inc(*S("r_exp").one)

        conb = sb("conb", [P, NCONB], at=END - 64 - (NCONB * 4 + 63) // 64 * 64)
        z2, v2, vpad, o2, sg2, yc, _r = lay(arena + 8192, [
            ("z2", [P, 18, SEG]), ("v2", [P, 2, 768]), ("vpad", [P, 2, SEG + CONV2 - 1]), ("o2", [P, KT, SEG]),
            ("sg2", [P, 2, SEG]), ("yc", [P, 2, SEG])])
        zs, ex_, sp_, wv2, rt_, yr, sg3, _r = lay(_r, [
            ("zs", [P, 2, 384]), ("ex_", [P, 2, 384]), ("sp_", [P, 2, 384]), ("wv2", [P, 2, 384]),
            ("rt_", [P, 4, SEG]), ("yr", [P, 2, SEG]), ("sg3", [P, 2, SEG])])
        assert _r <= END - 64 - (NCONB * 4 + 63) // 64 * 64, _r

        def cb(name):
            return conb[:, BCOL[name][0]:BCOL[name][1]]

        def pool_conb(pool):
            pool.wait_ge(*S("arena_free2").next("pool"))
            pool.dma_start(conb[:], io["constsb"]).then_inc(*S("conb").dma)

        def pe_in2(pe, l):
            pe.wait_ge(*S("alo_ready").next("pe"))
            pe_gemm(pe, BASE[f"in_{l}"], 18, "act", None, lambda b: [(ps[:, b, 0:SEG], True, a_cols([LAT]))])
            pe_gemm(pe, BASE[f"in_{l}"] + 18, 6, "act", None, lambda b: tok_major(b, 2, 2))

        def act_in2(act, l):
            act_copies(act, BASE[f"in_{l}"], [
                (18, lambda t: flat1(z2[:, one(t), :]), lambda b: ps[:, b, 0:SEG]),
                (6, lambda t: v2[:, :, dyn(t, P)], lambda b: ps[:, b, 0:256].rearrange("p (a c) -> p a c", a=2))])

        def conv2_taps(link, l, first, n):
            for j in range(first, min(first + n, 2 * CONV2)):
                tap, i = j // 2, j % 2
                x, w = vpad[:, i, tap:tap + SEG], pc("c2w", l * 62 + i * 31 + tap, 1)
                if tap == 0:
                    link(nc.vector.tensor_scalar(yc[:, i, :], x, w, pc("c2b", 2 * l + i, 1), ALU.mult, ALU.add))
                else:
                    link(nc.vector.scalar_tensor_tensor(yc[:, i, :], x, w, yc[:, i, :], ALU.mult, ALU.add))

        def dve_conv2_in(dve, link, evac0):
            dve.wait_ge(act_evac.sem, evac0)
            link(nc.vector.memset(vpad[:, :, 0:CONV2 - 1], 0.0))
            dve.wait_ge(*S("c2_sig").next("dve"))
            link(nc.vector.tensor_tensor(vpad[:, :, CONV2 - 1:], z2[:, 0:2, :], sg2[:], ALU.mult))

        def dve_conv2(dve, link, l):
            dve.sem_inc(S("ln_in").sem, 1)
            dve.wait_ge(*S("ln_mu").next("dve"))
            for i in range(2):
                link(nc.vector.scalar_tensor_tensor(yc[:, i, :], ps[:, 4, 0:SEG], -1.0 / 256, yc[:, i, :],
                                                    ALU.mult, ALU.add))
            link(nc.vector.tensor_tensor(sg2[:], yc[:], yc[:], ALU.mult))
            dve.sem_inc(S("ln_sq").sem, 1)
            dve.wait_ge(*S("ln_var").next("dve"))
            link(nc.vector.tensor_scalar(rs[:, 0:SEG], ps[:, 4, 0:SEG], 1.0 / 256, EPS, ALU.mult, ALU.add))
            dve.sem_inc(S("ln_ve").sem, 1)
            dve.wait_ge(*S("ln_rt").next("dve"))
            link(nc.vector.reciprocal(rs[:, 0:SEG], rs[:, 0:SEG]))
            link(nc.vector.tensor_tensor(yc[:], yc[:], bc(rs[:, 0:SEG].unsqueeze(1), [P, 2, SEG]), ALU.mult))
            for i in range(2):
                link(nc.vector.tensor_scalar(yc[:, i, :], yc[:, i, :], pc("c2g", 2 * l + i, 1),
                                             pc("c2bb", 2 * l + i, 1), ALU.mult, ALU.add))
            dve.sem_inc(S("c2_ln").sem, 1)

        def act_conv2_in(act, evac0):
            act.wait_ge(act_evac.sem, evac0)
            nc.scalar.activation(sg2[:], z2[:, 2:4, :], ACT.Sigmoid).then_inc(*S("c2_sig").one)

        def act_conv2(act):
            act.wait_ge(*S("ln_ve").next("act"))
            nc.scalar.activation(rs[:, 0:SEG], rs[:, 0:SEG], ACT.Sqrt).then_inc(*S("ln_rt").one)
            act.wait_ge(*S("c2_ln").next("act"))
            nc.scalar.activation(o2[:, 0:2, :], yc[:], ACT.Silu).then_inc(*S("o2_conv").one)

        def pe_conv2(pe):
            for a, src, b in (("ln_in", yc, "ln_mu"), ("ln_sq", sg2, "ln_var")):
                pe.wait_ge(*S(a).next("pe"))
                for i in range(2):
                    last = nc.tensor.matmul(ps[:, 4, 0:SEG], ones[:], src[:, i, :], start=(i == 0), stop=(i == 1))
                last.then_inc(*S(b).one)

        def pe_stick(pe, evac0):
            pe.wait_ge(act_evac.sem, evac0)

            def scores(h):
                m, e, b_ = h // 2, h % 2, h % 2
                q, k = z2[hp(e), 4 + m, :], z2[hp(e), 8 + m, :]
                nc.tensor.matmul(ps[:, b_, 0:256], k[:, 0:P], q, start=True, stop=True)
                nc.tensor.matmul(ps[:, b_, 256:384], k[:, P:SEG], q[:, P:SEG], start=True, stop=True
                                 ).then_inc(*S("sk_ps").one)

            def sums(h):
                b_ = h % 2
                pe.wait_ge(*S("sk_sp").next("pe"))
                nc.tensor.matmul(ps[:, 2 + b_, 0:256], cb("tri"), sp_[:, b_, 0:256], start=True, stop=False,
                                 skip_group_check=True)
                nc.tensor.matmul(ps[:, 2 + b_, 128:256], ones[:], sp_[:, b_, 256:384], start=False, stop=True,
                                 skip_group_check=True)
                nc.tensor.matmul(ps[:, 2 + b_, 256:384], cb("tri"), sp_[:, b_, 256:384], start=True, stop=True,
                                 skip_group_check=True).then_inc(*S("sk_rc").one)

            def outputs(h):
                m, e, b_ = h // 2, h % 2, h % 2
                pe.wait_ge(*S("sk_w").next("pe"))
                if e == 0 and m >= 2:
                    pe.wait_ge(*S("sk_o").next("pe"))
                nc.tensor.matmul(ps[hp(e), 5 + m % 2, 0:256], v2[:, 0, h * 64:(h + 1) * 64], wv2[:, b_, 0:256],
                                 start=True, stop=False, skip_group_check=True)
                nc.tensor.matmul(ps[hp(e), 5 + m % 2, 128:256], v2[:, 1, h * 64:(h + 1) * 64], wv2[:, b_, 256:384],
                                 start=False, stop=True, skip_group_check=True).then_inc(*S("sk_y").one)
            scores(0)
            for h in range(8):
                if h < 7:
                    scores(h + 1)
                sums(h)
                if h >= 1:
                    outputs(h - 1)
            outputs(7)

        def act_stick(act):
            def softplus(h):
                b_ = h % 2
                act.wait_ge(*S("sk_ps").next("act"))
                if h >= 2:
                    act.wait_ge(*S("sk_t1").next("act"))
                nc.scalar.activation(zs[:, b_, :], ps[:, b_, 0:384], ACT.Copy, scale=0.125).then_inc(*S("sk_z").one)
                act.wait_ge(*S("sk_z").next("act"))
                nc.scalar.activation(ex_[:, b_, :], zs[:, b_, :], ACT.Abs).then_inc(*S("sk_c").one)
                act.wait_ge(*S("sk_c").next("act"))
                nc.scalar.activation(ex_[:, b_, :], ex_[:, b_, :], ACT.Exp, scale=-1.0).then_inc(*S("sk_c").one)
                act.wait_ge(*S("sk_c").next("act"))
                nc.scalar.activation(ex_[:, b_, :], ex_[:, b_, :], ACT.Ln, bias=1.0).then_inc(*S("sk_l").one)

            def weights(h):
                act.wait_ge(*S("sk_t").next("act"))
                if h >= 2:
                    act.wait_ge(*S("sk_y").next("act"))
                nc.scalar.activation(wv2[:, h % 2, :], ex_[:, h % 2, :], ACT.Exp).then_inc(*S("sk_e").one)
            softplus(0)
            for h in range(8):
                if h < 7:
                    softplus(h + 1)
                weights(h)
            act.wait_ge(*S("sk_t1").next("act", 2))
            act.wait_ge(*S("sk_y").next("act", 2))

        def dve_stick(dve, link, l):
            def masked(t, h):
                a, b = t[:, h % 2, 0:P], t[:, h % 2, 256:384]
                link(nc.vector.tensor_tensor(a, a, cb("smask"), ALU.mult))
                return nc.vector.tensor_tensor(b, b, cb("smask"), ALU.mult)

            def softplus(h):
                b_ = h % 2
                dve.wait_ge(*S("sk_z").next("dve"))
                link(nc.vector.tensor_scalar(sp_[:, b_, :], zs[:, b_, :], 0.0, None, ALU.max))
                dve.wait_ge(*S("sk_l").next("dve"))
                link(nc.vector.tensor_tensor(sp_[:, b_, :], sp_[:, b_, :], ex_[:, b_, :], ALU.add))
                masked(sp_, h).then_inc(*S("sk_sp").one)

            def logs(h):
                b_ = h % 2
                dve.wait_ge(*S("sk_rc").next("dve"))
                nc.vector.scalar_tensor_tensor(ex_[:, b_, :], ps[:, 2 + b_, 0:384], -1.0, zs[:, b_, :],
                                               ALU.mult, ALU.add).then_inc(*S("sk_t1").one)
                dve.wait_ge(*S("sk_t1").next("dve"))
                nc.vector.tensor_scalar(ex_[:, b_, :], ex_[:, b_, :], 0.0, None, ALU.min).then_inc(*S("sk_t").one)

            def out(m):
                dve.wait_ge(*S("sk_y").next("dve", 2))
                nc.vector.tensor_copy(o2[:, 2 + m, :], ps[:, 5 + m % 2, 0:SEG]).then_inc(*S("sk_o").one)
            softplus(0)
            for h in range(8):
                conv2_taps(link, l, 8 * h, 8)
                logs(h)
                if h < 7:
                    softplus(h + 1)
                dve.wait_ge(*S("sk_e").next("dve"))
                masked(wv2, h).then_inc(*S("sk_w").one)
                if h % 2 == 0 and h >= 2:
                    out(h // 2 - 1)
            out(3)
            dve.wait_ge(*S("sk_o").next("dve", 4))

        def pe_ret(pe):
            pe.wait_ge(*S("sk_o").next("pe", 2))
            for i in range(4):
                last = nc.tensor.matmul(ps[:, i // 2, (i % 2) * SEG:(i % 2 + 1) * SEG], cb("rot"), z2[:, 12 + i, :],
                                        start=True, stop=True)
            last.then_inc(*S("rt_ps").one)
            pe.wait_ge(*S("rt_sb").next("pe"))
            for h in range(4):
                m, e, b_ = h // 2, h % 2, 2 + h % 2
                q, k = rt_[hp(e), m, :], rt_[hp(e), 2 + m, :]
                nc.tensor.matmul(ps[:, b_, 0:256], k[:, 0:P], q, start=True, stop=True)
                nc.tensor.matmul(ps[:, b_, 256:384], k[:, P:SEG], q[:, P:SEG], start=True, stop=True
                                 ).then_inc(*S("re_ps").one)
                pe.wait_ge(*S("re_sc").next("pe"))
                out = ps[hp(e), 5 + m, 0:256]
                nc.tensor.matmul(out, v2[:, 0, 512 + h * 64:512 + (h + 1) * 64], sp_[:, h % 2, 0:256],
                                 start=True, stop=False, skip_group_check=True)
                nc.tensor.matmul(ps[hp(e), 5 + m, 128:256], v2[:, 1, 512 + h * 64:512 + (h + 1) * 64],
                                 sp_[:, h % 2, 256:384], start=False, stop=True, skip_group_check=True
                                 ).then_inc(*S("re_y").one)
            for a, src, b in (("ln_in", yr, "ln_mu"), ("ln_sq", sg2, "ln_var")):
                pe.wait_ge(*S(a).next("pe"))
                nc.tensor.matmul(ps[:, 0, :], bones[:], fl(src[:]), start=True, stop=True).then_inc(*S(b).one)

        def dve_ret(dve, link, l):
            dve.wait_ge(*S("rt_ps").next("dve"))
            sn = bc(cb("sin").unsqueeze(1), [P, 2, SEG])
            for b_ in range(2):
                link(nc.vector.tensor_tensor(rt_[:, 2 * b_:2 * b_ + 2, :], ps[:, b_, :].rearrange("p (a t) -> p a t", a=2),
                                             sn, ALU.mult))
            link(nc.vector.tensor_tensor(z2[:, 12:16, :], z2[:, 12:16, :], bc(cb("cos").unsqueeze(1), [P, 4, SEG]), ALU.mult))
            nc.vector.tensor_tensor(rt_[:], rt_[:], z2[:, 12:16, :], ALU.add).then_inc(*S("rt_sb").one)
            for h in range(4):
                dve.wait_ge(*S("re_ps").next("dve"))
                if h >= 2:
                    dve.wait_ge(*S("re_y").next("dve"))
                nc.vector.tensor_tensor(sp_[:, h % 2, :], ps[:, 2 + h % 2, 0:384],
                                        cb("dret")[:, h * 384:(h + 1) * 384], ALU.mult).then_inc(*S("re_sc").one)
            dve.wait_ge(*S("re_y").next("dve", 2))
            dve.wait_ge(*S("c2_lnd").next("dve"))
            for m in range(2):
                link(nc.vector.tensor_copy(yr[:, m, :], ps[:, 5 + m, 0:SEG]))
            dve.sem_inc(S("ln_in").sem, 1)
            dve.wait_ge(*S("ln_mu").next("dve"))
            link(nc.vector.scalar_tensor_tensor(fl(yr[:]), ps[:, 0, :], -1.0 / 64, fl(yr[:]), ALU.mult, ALU.add))
            link(nc.vector.tensor_tensor(sg2[:], yr[:], yr[:], ALU.mult))
            dve.sem_inc(S("ln_sq").sem, 1)
            dve.wait_ge(*S("ln_var").next("dve"))
            link(nc.vector.tensor_scalar(fl(sg2[:]), ps[:, 0, :], 1.0 / 64, EPS, ALU.mult, ALU.add))
            dve.sem_inc(S("ln_ve").sem, 1)
            dve.wait_ge(*S("ln_rt").next("dve"))
            link(nc.vector.reciprocal(sg2[:], sg2[:]))
            link(nc.vector.tensor_tensor(yr[:], yr[:], sg2[:], ALU.mult))
            for m in range(2):
                link(nc.vector.scalar_tensor_tensor(o2[:, 6 + m, :], yr[:, m, :], pc("rtg", 2 * l + m, 1),
                                                    sg3[:, m, :], ALU.mult, ALU.mult))
            dve.wait_ge(*S("o2_conv").next("dve"))

        def act_ret(act):
            nc.scalar.activation(sg3[:], z2[:, 16:18, :], ACT.Silu).then_inc(*S("c2_lnd").one)
            act.wait_ge(*S("ln_ve").next("act"))
            nc.scalar.activation(sg2[:], sg2[:], ACT.Sqrt).then_inc(*S("ln_rt").one)

        E_ADA = RING
        E_WIN = E_ADA + 27
        E_QKV = E_WIN + 24
        E_IN = [E_QKV + 24, E_QKV + 48]

        @block.sync
        def _(sp):
            load_list(sp)
            sp_stream(sp)
            sp.wait_ge(*S("out_ready").next("sp"))
            sp.dma_start(io["out"], hT[:, :, seg_cols(LAT)]).then_inc(*S("stored").dma)
            sp.wait_ge(*S("stored").next("sp", 16))

        @block.gpsimd
        def _(pool):
            pool_shift(pool)
            pool.wait_ge(*S("mb_done").next("pool"))
            pool.dma_start(lora[:], io["lora"]).then_inc(*S("lora").dma)
            pool.dma_start(gup[:], io["gup"]).then_inc(*S("lora").dma)
            pool_bias(pool)
            pool_conb(pool)

        @block.tensor
        def _(pe):
            pe.sem_inc(tile_used.sem, RING)
            pe.wait_ge(S("par").sem, NLOAD)
            pe_ada(pe)
            for s in (CTX, LAT):
                pe_norm(pe)
            pe.wait_ge(*S("alo_ready").next("pe", 2))
            pe_gemm(pe, BASE["w_in"], 27, "act", None, lambda b: [(ps[:, b, :], True, a_cols([CTX, LAT]))])
            pe_dt(pe)
            pe_states(pe)
            pe_ssd(pe)
            pe_mbout(pe)
            for s in (CTX, LAT):
                pe_rwprep(pe, s)
                for n in range(NRC):
                    pe_solve(pe, s, n)
                pe_rwout(pe, s)
            pe.wait_ge(*S("alo_ready").next("pe"))
            pe_gemm(pe, BASE["w_out"], 8, "dve", None, lambda b: [(ps[:, b, :], True, a_cols([CTX, LAT]))])
            for s, nm in ((CTX, "ffn_ctx"), (LAT, "ffn_lat")):
                pe_norm(pe)
                pe.wait_ge(*S("alo_ready").next("pe"))
                pe_ffn(pe, BASE[nm], s, FT)
            for s in (CTX, LAT):
                pe_norm(pe)
            pe_qkv(pe)
            pe_attn(pe, E_QKV)
            pe.wait_ge(*S("alo_ready").next("pe"))
            pe_gemm(pe, BASE["na_out"], 8, "dve", None, lambda b: [(ps[:, b, 0:SEG], True, a_cols([LAT]))])
            pe_norm(pe)
            pe.wait_ge(*S("alo_ready").next("pe"))
            pe_router(pe)
            pe_ffn(pe, BASE["moe"], LAT, FT * NE)
            pe_norm(pe)
            for l in range(2):
                pe_norm(pe)
                pe.wait_ge(*S("alo_ready").next("pe"))
                pe_ffn(pe, BASE[f"f1_{l}"], LAT, FT)
                pe_norm(pe)
                pe_in2(pe, l)
                pe_stick(pe, E_IN[l])
                pe_conv2(pe)
                pe_ret(pe)
                pe.wait_ge(*S("alo_ready").next("pe"))
                pe_gemm(pe, BASE[f"out_{l}"], 8, "dve", None, lambda b: [(ps[:, b, 0:SEG], True, a_cols([LAT]))])
                pe_norm(pe)
                pe.wait_ge(*S("alo_ready").next("pe"))
                pe_ffn(pe, BASE[f"f2_{l}"], LAT, FT)
            pe_norm(pe)

        @block.scalar
        def _(act):
            act.sem_inc(act_evac.sem, RING)
            for n in range(LEAD):
                act_split_ada(act, n, 0, n)
            act_ada(act)
            for s in (CTX, LAT):
                act_norm(act, s, normw, shift_of(0, 0, s))
            act_win(act)
            act_conv(act)
            act_dt(act)
            act_ssd(act)
            act_mbout(act)
            for s in (CTX, LAT):
                act_rwprep(act, s)
                for n in range(NRC):
                    act_solve(act, n)
                act_rwout(act, s)
            act_osplit(act, o0[:], slice(0, T2))
            run_tiles(act, "act", BASE["w_out"], 8)
            for s, nm in ((CTX, "ffn_ctx"), (LAT, "ffn_lat")):
                act_norm(act, s, normw, shift_of(0, 1, s))
                act_ffn(act, BASE[nm], FT)
            for s in (CTX, LAT):
                act_norm(act, s, normw, shift_of(1, 0, s))
            act_qkv(act)
            act_attn(act)
            act_osplit(act, oA[:], seg_cols(LAT))
            run_tiles(act, "act", BASE["na_out"], 8)
            act_norm(act, LAT, normw)
            act_router(act)
            act_ffn(act, BASE["moe"], FT * NE)
            act_norm(act, LAT, normw, to_a=False)
            for l in range(2):
                act_norm(act, LAT, normw)
                act_ffn(act, BASE[f"f1_{l}"], FT)
                act_norm(act, LAT, normw)
                act_in2(act, l)
                act_conv2_in(act, E_IN[l])
                act_stick(act)
                act_conv2(act)
                act_ret(act)
                act_osplit(act, o2[:], seg_cols(LAT))
                run_tiles(act, "act", BASE[f"out_{l}"], 8)
                act_norm(act, LAT, normw)
                act_ffn(act, BASE[f"f2_{l}"], FT)
            act_norm(act, LAT, normw, to_a=False)

        @block.vector
        def _(dve):
            link = Chain(dve, "dve_chain")
            dve.sem_inc(dve_evac.sem, RING)
            for n in range(LEAD):
                dve_split_ada(dve, n, n)
            dve_ada(dve, link)
            for s in (CTX, LAT):
                dve.sem_inc(S("h_ready").sem, KT)
                dve_norm(dve, link, s, normw, gain_of(0, 0, s), shift_of(0, 0, s))
            dve_win(dve, link)
            dve_dt(dve, link)
            dve_tm(dve, link)
            dve_states(dve, link)
            dve_ssd(dve, link)
            dve_mbout(dve, link)
            dve.sem_inc(S("mb_done").sem, 1)
            for s in (CTX, LAT):
                dve_rwprep(dve, link, s)
                for n in range(NRC):
                    dve_solve(dve, link, s, n)
                dve_rwout(dve, link, s)
            dve_osplit(dve, o0[:], slice(0, T2))
            dve_resid(dve, link, BASE["w_out"], 8, (CTX, LAT), lambda t, s: m_col(0, 2, t, s))
            for s, nm in ((CTX, "ffn_ctx"), (LAT, "ffn_lat")):
                dve.sem_inc(S("h_ready").sem, KT)
                dve_norm(dve, link, s, normw, gain_of(0, 1, s), shift_of(0, 1, s))
                dve_ffn(dve, BASE[nm], FT)
                dve_ffn_out(dve, link, BASE[nm], FT, s, lambda m, s=s: m_col(0, 5, m, s),
                            normed=False)
            dve.sem_inc(S("arena_free").sem, 1)
            for s in (CTX, LAT):
                dve.sem_inc(S("h_ready").sem, KT)
                dve_norm(dve, link, s, normw, gain_of(1, 0, s), shift_of(1, 0, s))
            run_tiles(dve, "dve", BASE["qkv"], 24)
            dve_attn(dve, link)
            dve_osplit(dve, oA[:], seg_cols(LAT))
            dve_resid(dve, link, BASE["na_out"], 8, (LAT,), lambda t, s: m_col(1, 2, t, s))
            dve.sem_inc(S("arena_free2").sem, 1)
            dve.sem_inc(S("h_ready").sem, KT)
            dve_norm(dve, link, LAT, normw, gain_of(1, 1, LAT), shift_of(1, 1, LAT), full=True)
            dve_router(dve, link)
            dve_ffn(dve, BASE["moe"], FT * NE, gate)
            dve_ffn_out(dve, link, BASE["moe"], FT * NE, LAT, lambda m: m_col(1, 5, m, LAT))
            dve_norm(dve, link, LAT, normw, lambda k: pc("n_fin", k, 1), None, final="x2")
            dve.wait_ge(*S("x2").next("dve"))
            for l in range(2):
                if l == 0:
                    dve.sem_inc(S("h_ready").sem, KT)
                dve_norm(dve, link, LAT, normw, lambda k, l=l: pc("n1", 8 * l + k, 1), None)
                dve_ffn(dve, BASE[f"f1_{l}"], FT)
                dve_ffn_out(dve, link, BASE[f"f1_{l}"], FT, LAT, lambda m: 0.5)
                dve_norm(dve, link, LAT, normw, lambda k, l=l: pc("nm", 8 * l + k, 1), None)
                run_tiles(dve, "dve", BASE[f"in_{l}"], 24)
                dve_conv2_in(dve, link, E_IN[l])
                dve_stick(dve, link, l)
                dve_conv2(dve, link, l)
                dve_ret(dve, link, l)
                dve_osplit(dve, o2[:], seg_cols(LAT))
                dve_resid(dve, link, BASE[f"out_{l}"], 8, (LAT,), lambda t, s: 1.0)
                dve.sem_inc(S("h_ready").sem, KT)
                dve_norm(dve, link, LAT, normw, lambda k, l=l: pc("n2", 8 * l + k, 1), None)
                dve_ffn(dve, BASE[f"f2_{l}"], FT)
                dve_ffn_out(dve, link, BASE[f"f2_{l}"], FT, LAT, lambda m: 0.5)
            dve_norm(dve, link, LAT, normw, lambda k: pc("nf2", k, 1), None, final="out_ready")


def vec(v):
    return v.reshape(-1, P).T


def pad_to(a, n, axis=-1):
    w = [(0, 0)] * a.ndim
    w[axis] = (0, n - a.shape[axis])
    return np.pad(a, w)


def tiles_of(w):
    n = w.shape[1] // P
    return w.reshape(KT, P, n, P).transpose(2, 1, 0, 3).reshape(n, P, KT * P)


def ffn_tiles(w1, w3, w2):
    h1, h3 = tiles_of(w1), tiles_of(w3)
    o = w2.reshape(-1, P, D)
    n = len(o)
    out = np.empty((3 * n, P, D), np.float32)
    out[0], out[1] = h1[0], h3[0]
    out[2:3 * n - 1:3], out[3:3 * n - 1:3], out[4:3 * n - 1:3] = h1[1:], h3[1:], o[:-1]
    out[3 * n - 1] = o[-1]
    return out


def rw_cols(a):
    return pad_to(a[..., :1760], 14 * P)


def consts_a():
    i = np.arange(RC)
    ident = np.eye(P, dtype=np.float32)
    bones = np.kron(np.eye(2), np.ones((64, 64)))
    i64 = np.tile(np.eye(RC), (2, 1))
    s, t = i[:, None], i[None, :]
    mx = np.concatenate([s < t, s <= t, s > t, s >= t], 1)
    lv = np.zeros((2, RLEV + 1, 2, RC, RC))
    for v in range(RLEV + 1):
        m = 1 << v
        low = (s // (2 * m) == t // (2 * m)) & ((s // m) % 2 == 1) & ((t // m) % 2 == 0)
        for d in range(2):
            nn = low if d == 0 else low.T
            lv[0, v, d], lv[1, v, d] = nn, nn.T
    lv = lv.transpose(3, 0, 1, 2, 4).reshape(RC, -1)
    scan64 = np.tile((np.arange(1024) % RC != 0).astype(np.float32), (P, 1))
    scan128 = np.tile((np.arange(T2) % MC != 0).astype(np.float32), (P, 1))
    j = np.arange(P)
    mssd = np.concatenate([j[:, None] <= j[None, :], j[:, None] >= j[None, :]], 1)
    two = lambda a: np.tile(a, (2, 1))
    return np.concatenate([ident, np.ones((P, P)), bones, i64, two(mx), two(lv), scan64, scan128, mssd],
                          1).astype(np.float32)


def consts_b():
    j = np.arange(P)
    iota = np.tile(np.arange(NE), (P, 2))
    tri = j[:, None] >= j[None, :]
    smask = j[:, None] < j[None, :]
    rot = np.zeros((P, P))
    for c in range(P):
        base, r = c // 64 * 64, c % 64
        if r < 32:
            rot[base + r + 32, c] = -1.0
        else:
            rot[base + r - 32, c] = 1.0
    half = 32
    inv = (1.0 / (np.float32(10000.0) ** (np.arange(half, dtype=np.float32) / half))).astype(np.float32)
    ang = np.arange(SEG, dtype=np.float32)[:, None] * inv[None, :]
    cos = np.tile(np.cos(ang).T, (4, 1))
    sin = np.tile(np.sin(ang).T, (4, 1))
    lg = np.log1p(-np.exp2(-5.0 - np.arange(4)))
    s, t = np.arange(SEG)[:, None], np.arange(SEG)[None, :]
    dret = []
    for h in range(4):
        same = s // 64 == t // 64
        w = np.where(same | (s // 64 < t // 64), np.exp(lg[h] * np.abs(t - s)), 0.0) * 0.125
        dret.append(np.concatenate([w[0:P, :], w[P:, P:]], 1))
    return np.concatenate([iota, tri, smask, rot, cos, sin] + dret, 1).astype(np.float32)


def lay_out(i):
    c = {}
    z = lambda a: np.asarray(a)
    cols = {}
    cols["b_ada"] = np.concatenate([vec(z(i["b_ada"])[l]) for l in range(2)], 1)
    for nm, src in (("n_mix", "norm_mix"), ("n_ffn", "norm_ffn"), ("n1", "ffn1_norm_2"), ("nm", "mix_norm_2"),
                    ("n2", "ffn2_norm_2")):
        cols[nm] = np.concatenate([vec(i[src][l]) for l in range(2)], 1)
    cols["n_fin"], cols["nf2"] = vec(i["norm_final"]), vec(i["final_norm_2"])
    mu = rw_cols(i["rw_mu"][0])
    cols["mu_p"], cols["mu_n"] = vec(mu[0]), vec(mu[1])
    for nm, src in (("w0", "rw_w0"), ("a0", "rw_a0")):
        cols[nm] = np.concatenate([vec(i[src][0, d]) for d in range(2)], 1)
    cols["rk"] = np.concatenate([vec(i["rw_r_k"][0, d].reshape(-1)) for d in range(2)], 1)
    for nm, src in (("kk", "rw_k_k"), ("ka", "rw_k_a"), ("gnw", "rw_gn_w"), ("gnb", "rw_gn_b"), ("cb", "mb_conv_b"),
                    ("mbn", "mb_norm_w")):
        cols[nm] = vec(i[src][0])
    cols["cw"] = i["mb_conv_w"][0].reshape(5, 8, P).transpose(2, 1, 0).reshape(P, 40)
    cols["mbd"] = vec(np.repeat(i["mb_d"][0], 64))
    for nm, src in (("dtb", "mb_dt_bias"), ("alog", "mb_a_log")):
        v = np.zeros((P, 1), np.float32)
        v[0:8, 0], v[32:40, 0] = i[src][0, 0], i[src][0, 1]
        cols[nm] = v
    cols["c2w"] = i["conv_w_2"].reshape(2, CONV2, 2, P).transpose(3, 0, 2, 1).reshape(P, 124)
    for nm, src in (("c2b", "conv_b_2"), ("c2g", "conv_ln_g_2"), ("c2bb", "conv_ln_b_2"), ("rtg", "ret_norm_g_2")):
        cols[nm] = np.concatenate([vec(i[src][l]) for l in range(2)], 1)
    cols["rb"] = np.tile(i["moe_router_b"], (P, 1))
    cols["rw"] = i["moe_router_w"][0].reshape(KT, P, NE).transpose(1, 0, 2).reshape(P, -1)
    cols["cvec"] = np.stack([vec(i["c_ctx"]), vec(i["c"][0])], 2).reshape(P, 16)
    c["params"] = np.concatenate([cols[n] for n, _ in PARAMS], 1)
    c["consts"], c["constsb"] = consts_a(), consts_b()
    for nm, src in (("ctxT", "ctx"), ("xT", "x")):
        c[nm] = i[src][0].T.reshape(KT, P, SEG).transpose(1, 0, 2)
    c["lora"] = np.concatenate([i["rw_w_up"][0].reshape(64, 512), i["rw_a_up"][0].reshape(64, 512)], 0)
    c["gup"] = pad_to(i["rw_g_up"][0], P, 0)
    qr, qc = np.arange(SEG) // 64, np.arange(SEG) % 64
    start = np.clip(qc - 8, 0, 48)
    inside = (qc[None, :] >= start[:, None]) & (qc[None, :] < start[:, None] + 16)
    rpb = np.concatenate([i["na_rpb"][0].reshape(16, -1), np.full((16, 1), -BIG, np.float32)], 1)
    idx = (qr[None, :] - qr[:, None] + 7) * 31 + np.clip(qc[None, :] - qc[:, None] + 15, 0, 30)
    idx = np.where(inside, idx, 15 * 31)
    bias = rpb[:, idx]
    c["bias"] = bias.reshape(16, 2, P, SEG).transpose(2, 0, 1, 3).reshape(P, 16, 512)
    w = i["mix_w_in"][0]
    mb = w[:, 1760:]
    dtc = np.zeros((D, P), np.float32)
    dtc[:, 0:8], dtc[:, 32:40] = mb[:, 1536:1544], mb[:, 1544:1552]
    w_in = np.concatenate([mb[:, 512:1536], mb[:, 0:512], dtc, rw_cols(w)], 1)
    q = i["na_w_qkv"][0]
    parts = {"ada": np.asarray(i["w_ada"]).reshape(2, KT, P, 6, D).transpose(0, 3, 1, 2, 4).reshape(96, P, D), "w_in": tiles_of(w_in),
             "w_out": tiles_of(i["mix_w_out"][0]), "qkv": tiles_of(q), "na_out": tiles_of(i["na_w_out"][0])}
    f0 = ffn_tiles(i["ffn_w1"][0], i["ffn_w3"][0], i["ffn_w2"][0])
    parts["ffn_ctx"] = parts["ffn_lat"] = f0
    st = lambda a: np.asarray(a[0]).transpose(1, 0, 2).reshape(D, NE * DFF)
    parts["moe"] = ffn_tiles(st(i["moe_w1"]), st(i["moe_w3"]), np.asarray(i["moe_w2"][0]).reshape(NE * DFF, D))
    for l in range(2):
        for f, nm in ((1, "f1"), (2, "f2")):
            wi = i[f"ffn{f}_w_in_2"][l]
            parts[f"{nm}_{l}"] = ffn_tiles(wi[:, :DFF], wi[:, DFF:], i[f"ffn{f}_w_out_2"][l])
        wi = i["mix_w_in_2"][l]
        order = [slice(0, 512), slice(512, 1536), slice(2048, 2560), slice(2816, 3072), slice(1536, 2048),
                 slice(2560, 2816)]
        parts[f"in_{l}"] = tiles_of(np.concatenate([wi[:, o] for o in order], 1))
        parts[f"out_{l}"] = tiles_of(i["mix_w_out_2"][l])
    stream = np.zeros((NTILES, P, D), np.float32)
    for nm, n in STREAM:
        stream[BASE[nm]:BASE[nm] + n] = parts[nm]
    c["wstream"] = stream
    return c


def kernel(**inputs):
    import concourse.bacc as _bacc
    from concourse.bass_utils import run_bass_kernel_spmd as _run

    arrays = {k: np.ascontiguousarray(v, dtype=np.float32) for k, v in
              lay_out({k: np.asarray(v) for k, v in inputs.items()}).items()}
    nc = _bacc.Bacc("TRN2", target_bir_lowering=False, num_devices=1)
    io = {k: nc.dram_tensor(k, v.shape, F32, kind="ExternalInput").ap() for k, v in arrays.items()}
    io["out"] = nc.dram_tensor("outT", (P, KT, SEG), F32, kind="ExternalOutput").ap()
    build(nc, io)
    r = _run(nc, [arrays], core_ids=[0]).results[0]
    return r["outT"].transpose(2, 1, 0).reshape(1, SEG, D)
```
